# Optimizing a Trainium2 kernel written in Bass

```python
import functools
import jax, jax.numpy as jnp
from jax import lax
import numpy as np

'''One inference step of a Hymba-style hybrid decoder layer stack (DEPTH layers), run for a
prompt group and a sample group that share the same weights.

Each layer:
  x -> RMSNorm -> ONE combined input projection, columns split into
       [q | k | v] for dilated sliding-window attention (N_HEADS x HEAD_DIM, QK-RMSNorm, NoPE)
       [a | gate] for the Conformer convolution module (GLU -> causal depthwise conv(31)
                  -> LayerNorm over channels -> swish)
  -> concat(attention heads, conv channels) -> ONE output projection -> residual
  -> RMSNorm -> SwiGLU FFN -> residual
Dilated attention: every head evaluates the (window, dilation) patterns (128,1), (512,4), (2048,16);
a query at position t reads t, t-d, t-2d, ..., t-window (positions >= 0), and the per-pattern
outputs are combined with weights proportional to their softmax denominators.

Inputs:
  x_prompt   (BATCH, SEQ, D_MODEL)       positions 0..SEQ-1
  x_sample   (DEC_BATCH, DEC_SEQ, D_MODEL) positions PAST_LEN..PAST_LEN+DEC_SEQ-1
  cache_k    (DEPTH, DEC_BATCH, L_BUF, N_HEADS, HEAD_DIM)  keys of the last L_BUF=min(2048,PAST_LEN) positions
  cache_v    (DEPTH, DEC_BATCH, L_BUF, N_HEADS, HEAD_DIM)  values of the same positions
  state_conv (DEPTH, DEC_BATCH, CONV_WIDTH-1, D_CONV)      last 30 GLU outputs (depthwise-conv inputs)
  weights stacked over DEPTH.
Output tuple:
  y_prompt               (BATCH, SEQ, D_MODEL)
  y_sample               (DEC_BATCH, DEC_SEQ, D_MODEL)
  new_cache_k_prompt     (DEPTH, BATCH, min(2048, SEQ), N_HEADS, HEAD_DIM)
  new_cache_v_prompt     (DEPTH, BATCH, min(2048, SEQ), N_HEADS, HEAD_DIM)
  new_state_conv_prompt  (DEPTH, BATCH, CONV_WIDTH-1, D_CONV)
  new_cache_k_sample     (DEPTH, DEC_BATCH, min(2048, L_BUF+DEC_SEQ), N_HEADS, HEAD_DIM)
  new_cache_v_sample     (DEPTH, DEC_BATCH, min(2048, L_BUF+DEC_SEQ), N_HEADS, HEAD_DIM)
  new_state_conv_sample  (DEPTH, DEC_BATCH, CONV_WIDTH-1, D_CONV)
'''

D_MODEL = 1024
BATCH = 1
SEQ = 1024
DEPTH = 1
DEC_BATCH = 8
DEC_SEQ = 8
PAST_LEN = 1024
PAGE_SIZE = 128

N_HEADS = 8
HEAD_DIM = 64
D_ATTN = N_HEADS * HEAD_DIM
D_CONV = D_MODEL - D_ATTN
D_MIX = D_ATTN + D_CONV
D_IN = 3 * D_ATTN + 2 * D_CONV
PATTERNS = ((128, 1), (512, 4), (2048, 16))
WIN_MAX = max(w for w, _ in PATTERNS)
CONV_WIDTH = 31
D_FF = ((-(-8 * D_MODEL // 3) + 255) // 256) * 256
BLK = 128
RMS_EPS = 1e-6
LN_EPS = 1e-5
ATTN_SCALE = HEAD_DIM ** -0.5

kernel_name = 'hymba_dilated_conformer_decode_step'

def _rms_norm(x, g):
    xf = x.astype(jnp.float32)
    y = xf * lax.rsqrt(jnp.mean(xf * xf, axis=-1, keepdims=True) + RMS_EPS)
    return (y * g.astype(jnp.float32)).astype(x.dtype)

def _layer_norm(x, g, b):
    xf = x.astype(jnp.float32)
    xc = xf - jnp.mean(xf, axis=-1, keepdims=True)
    y = xc * lax.rsqrt(jnp.mean(xc * xc, axis=-1, keepdims=True) + LN_EPS)
    return (y * g.astype(jnp.float32) + b.astype(jnp.float32)).astype(x.dtype)

def _dilated_band_prompt(q, k, v, window, dilation):
    B, S, H, Dh = q.shape
    n_sub = window // dilation
    span = dilation * BLK
    s_pad = -(-S // span) * span
    L = s_pad // dilation
    nb = L // BLK

    def to_blocks(t):
        t = jnp.pad(t, ((0, 0), (0, s_pad - S), (0, 0), (0, 0)))
        t = t.reshape(B, L, dilation, H, Dh).transpose(0, 2, 1, 3, 4)
        return t.reshape(B, dilation, nb, BLK, H, Dh)

    def with_prev(t):
        prev = jnp.pad(t, ((0, 0), (0, 0), (1, 0), (0, 0), (0, 0), (0, 0)))[:, :, :-1]
        return jnp.concatenate([prev, t], axis=3)

    qb = to_blocks(q)
    kk = with_prev(to_blocks(k))
    vv = with_prev(to_blocks(v))
    s = jnp.einsum('brnqhd,brnkhd->brnhqk', qb, kk).astype(jnp.float32) * ATTN_SCALE
    qi = jnp.arange(BLK)[:, None]
    ki = jnp.arange(2 * BLK)[None, :]
    dist = BLK + qi - ki
    band = (dist >= 0) & (dist <= n_sub)
    blk = jnp.arange(nb)[:, None, None]
    valid = band[None] & (blk * BLK + ki[None] - BLK >= 0)
    s = jnp.where(valid[None, None, :, None], s, -jnp.inf)
    m = jnp.max(s, axis=-1, keepdims=True)
    p = jnp.exp(s - m)
    l = jnp.sum(p, axis=-1, keepdims=True)
    o = jnp.einsum('brnhqk,brnkhd->brnqhd', p / l, vv.astype(jnp.float32))
    lse = jnp.swapaxes((m + jnp.log(l))[..., 0], 3, 4)
    o = o.reshape(B, dilation, L, H, Dh).transpose(0, 2, 1, 3, 4).reshape(B, s_pad, H, Dh)[:, :S]
    lse = lse.reshape(B, dilation, L, H).transpose(0, 2, 1, 3).reshape(B, s_pad, H)[:, :S]
    return o, lse

def _dilated_gather_sample(q, k_all, v_all, window, dilation):
    T = q.shape[1]
    lb = k_all.shape[1] - T
    n_sub = window // dilation
    idx = lb + jnp.arange(T)[:, None] - dilation * jnp.arange(n_sub + 1)[None, :]
    valid = idx >= 0
    idx = jnp.maximum(idx, 0)
    kg = k_all[:, idx]
    vg = v_all[:, idx]
    s = jnp.einsum('bthd,btjhd->bthj', q, kg).astype(jnp.float32) * ATTN_SCALE
    s = jnp.where(valid[None, :, None, :], s, -jnp.inf)
    m = jnp.max(s, axis=-1, keepdims=True)
    p = jnp.exp(s - m)
    l = jnp.sum(p, axis=-1, keepdims=True)
    o = jnp.einsum('bthj,btjhd->bthd', p / l, vg.astype(jnp.float32))
    lse = (m + jnp.log(l))[..., 0]
    return o, lse

def _combine(results):
    o = jnp.stack([r[0] for r in results])
    lse = jnp.stack([r[1] for r in results])
    w = jax.nn.softmax(lse, axis=0)
    return jnp.sum(w[..., None] * o, axis=0)

def _attend_prompt(q, k, v):
    S = q.shape[1]
    out = _combine([_dilated_band_prompt(q, k, v, w, r) for w, r in PATTERNS])
    keep = min(WIN_MAX, S)
    return out, k[:, S - keep:], v[:, S - keep:]

def _attend_sample(q, k, v, k_buf, v_buf):
    k_all = jnp.concatenate([k_buf.astype(k.dtype), k], axis=1)
    v_all = jnp.concatenate([v_buf.astype(v.dtype), v], axis=1)
    out = _combine([_dilated_gather_sample(q, k_all, v_all, w, r) for w, r in PATTERNS])
    keep = min(WIN_MAX, k_all.shape[1])
    return out, k_all[:, -keep:], v_all[:, -keep:]

def _causal_depthwise(u_ext, w, b):
    out = lax.conv_general_dilated(u_ext, w[:, None, :].astype(u_ext.dtype), window_strides=(1,),
                                   padding='VALID', dimension_numbers=('NWC', 'WIO', 'NWC'),
                                   feature_group_count=u_ext.shape[-1])
    return out + b.astype(out.dtype)

def _layer(x, conv_left, attend, attn_norm_g, w_in, q_norm_g, k_norm_g, conv_w, conv_b,
           conv_ln_g, conv_ln_b, w_out, ffn_norm_g, w_gate, w_up, w_down):
    N, T, _ = x.shape
    h = _rms_norm(x, attn_norm_g)
    z = h @ w_in
    q, k, v, a, g = jnp.split(z, [D_ATTN, 2 * D_ATTN, 3 * D_ATTN, 3 * D_ATTN + D_CONV], axis=-1)
    q = _rms_norm(q.reshape(N, T, N_HEADS, HEAD_DIM), q_norm_g)
    k = _rms_norm(k.reshape(N, T, N_HEADS, HEAD_DIM), k_norm_g)
    v = v.reshape(N, T, N_HEADS, HEAD_DIM)
    attn, k_state, v_state = attend(q, k, v)
    u = a * jax.nn.sigmoid(g)
    u_ext = jnp.concatenate([conv_left.astype(u.dtype), u], axis=1)
    c = _causal_depthwise(u_ext, conv_w, conv_b)
    c = jax.nn.silu(_layer_norm(c, conv_ln_g, conv_ln_b))
    mix = jnp.concatenate([attn.reshape(N, T, D_ATTN).astype(x.dtype), c.astype(x.dtype)], axis=-1)
    x = x + mix @ w_out
    h = _rms_norm(x, ffn_norm_g)
    x = x + (jax.nn.silu(h @ w_gate) * (h @ w_up)) @ w_down
    return x, k_state, v_state, u_ext[:, -(CONV_WIDTH - 1):]

def setup_inputs(seed: int = 0) -> dict:
    key = jax.random.key(seed)
    ks = jax.random.split(key, 18)
    f32 = jnp.float32
    l_buf = min(WIN_MAX, PAST_LEN)

    def nrm(k, shape, scale):
        return scale * jax.random.normal(k, shape, f32)

    return {
        'x_prompt': nrm(ks[0], (BATCH, SEQ, D_MODEL), 1.0),
        'x_sample': nrm(ks[1], (DEC_BATCH, DEC_SEQ, D_MODEL), 1.0),
        'cache_k': nrm(ks[2], (DEPTH, DEC_BATCH, l_buf, N_HEADS, HEAD_DIM), 1.0),
        'cache_v': nrm(ks[3], (DEPTH, DEC_BATCH, l_buf, N_HEADS, HEAD_DIM), 1.0),
        'state_conv': nrm(ks[4], (DEPTH, DEC_BATCH, CONV_WIDTH - 1, D_CONV), 0.5),
        'attn_norm_g': 1.0 + nrm(ks[5], (DEPTH, D_MODEL), 0.02),
        'w_in': nrm(ks[6], (DEPTH, D_MODEL, D_IN), D_MODEL ** -0.5),
        'q_norm_g': 1.0 + nrm(ks[7], (DEPTH, HEAD_DIM), 0.02),
        'k_norm_g': 1.0 + nrm(ks[8], (DEPTH, HEAD_DIM), 0.02),
        'conv_w': nrm(ks[9], (DEPTH, CONV_WIDTH, D_CONV), CONV_WIDTH ** -0.5),
        'conv_b': nrm(ks[10], (DEPTH, D_CONV), 0.02),
        'conv_ln_g': 1.0 + nrm(ks[11], (DEPTH, D_CONV), 0.02),
        'conv_ln_b': nrm(ks[12], (DEPTH, D_CONV), 0.02),
        'w_out': nrm(ks[13], (DEPTH, D_MIX, D_MODEL), D_MIX ** -0.5),
        'ffn_norm_g': 1.0 + nrm(ks[14], (DEPTH, D_MODEL), 0.02),
        'w_gate': nrm(ks[15], (DEPTH, D_MODEL, D_FF), D_MODEL ** -0.5),
        'w_up': nrm(ks[16], (DEPTH, D_MODEL, D_FF), D_MODEL ** -0.5),
        'w_down': nrm(ks[17], (DEPTH, D_FF, D_MODEL), D_FF ** -0.5),
    }

def reference(x_prompt, x_sample, cache_k, cache_v, state_conv, attn_norm_g, w_in, q_norm_g,
              k_norm_g, conv_w, conv_b, conv_ln_g, conv_ln_b, w_out, ffn_norm_g, w_gate, w_up, w_down):
    y_p, y_s = x_prompt, x_sample
    nk_p, nv_p, nc_p, nk_s, nv_s, nc_s = [], [], [], [], [], []
    for l in range(DEPTH):
        w = (attn_norm_g[l], w_in[l], q_norm_g[l], k_norm_g[l], conv_w[l], conv_b[l],
             conv_ln_g[l], conv_ln_b[l], w_out[l], ffn_norm_g[l], w_gate[l], w_up[l], w_down[l])
        zeros_left = jnp.zeros((y_p.shape[0], CONV_WIDTH - 1, D_CONV), y_p.dtype)
        y_p, kp, vp, cp = _layer(y_p, zeros_left, _attend_prompt, *w)
        attend_s = functools.partial(_attend_sample, k_buf=cache_k[l], v_buf=cache_v[l])
        y_s, ks_, vs_, cs_ = _layer(y_s, state_conv[l], attend_s, *w)
        nk_p.append(kp)
        nv_p.append(vp)
        nc_p.append(cp)
        nk_s.append(ks_)
        nv_s.append(vs_)
        nc_s.append(cs_)
    return (y_p, y_s, jnp.stack(nk_p), jnp.stack(nv_p), jnp.stack(nc_p),
            jnp.stack(nk_s), jnp.stack(nv_s), jnp.stack(nc_s))


_drawn_inputs = setup_inputs


def setup_inputs(seed=0):
    import zlib

    import numpy as np

    out = dict(_drawn_inputs(seed))
    spreads = {}
    factors = {'q_norm_g': 8.0,
     'k_norm_g': 2.968,
     'conv_b': 3.156,
     'conv_ln_g': 5.31,
     'conv_ln_b': 6.338,
     'ffn_norm_g': 4.161}
    for name, (base, spread) in spreads.items():
        noise = np.random.default_rng([zlib.crc32(name.encode()), seed]).standard_normal(out[name].shape)
        drawn = base * np.exp(spread * noise) if base else spread * noise
        out[name] = __import__('jax').numpy.asarray(drawn.astype(out[name].dtype))
    for name, factor in factors.items():
        out[name] = (out[name] * factor).astype(out[name].dtype)
    return out
```

```python
from contextlib import ExitStack

import concourse.bass as bass
from concourse import mybir

F32 = mybir.dt.float32
F32R = mybir.dt.float32r
ALU = mybir.AluOpType
ACT = mybir.ActivationFunctionType
AX = mybir.AxisListType
ds = bass.ds

P = 128
D = 1024
KT = D // P
SEQ, NB_S, TS = 1024, 8, 8
NS = NB_S * TS
TOK = SEQ + NS
H, DH = 8, 64
DA = H * DH
DC = D - DA
CT = DC // P
NPAIR = H // 2
TAPS = 31
PADC = TAPS - 1
DFF = 2816
NF = DFF // P
NCH = NF // 2
LB = 1024
CK = 768
CKT = CK // P
SK = CK + TS
PC = 1024
N_PIECES = 2 * CT + 12 + 8 + 6 * NCH
TILES = [t * P for t in range(SEQ // P)] + [TOK - P]
NT = len(TILES)
BLOCKS = [(0, 364), (364, 362), (726, 362)]
SMP = PADC + SEQ
SW = PADC + TS
UW = SMP + NB_S * SW
CVS = NB_S * SW - PADC
RMS_EPS, LN_EPS = 1e-6, 1e-5

LNB = [(0, 512), (512, 512), (SEQ, NS)]
E_ORDER = list(range(NT - 2)) + [NT - 1, NT - 2]

UNITS = [("p", 0, i) for i in range(8)] + [("s", 0, 0)] + [("p", 1, i) for i in range(8)] + [("s", 1, 0)]
NU = len(UNITS)


def quads_of_units():
    q, out = 6, []
    for kind, _, i in UNITS:
        tiles = i + 1 if kind == "p" else CKT + 1
        out.append((q, tiles))
        q += (tiles + 3) // 4
    return out, q


UQ, NQ = quads_of_units()
OGS = [("p", 0, 0, 4), ("p", 0, 4, 4), ("s", 0, 8, 1), ("p", 1, 9, 4), ("p", 1, 13, 4), ("s", 1, 17, 1)]
NOG = len(OGS)
assert NQ % 2 == 0


def hymba_layer(nc, w_stream, xT, x_all, kT_c, v_c, cache_k, cache_v, stT, g1, g2, qkg, cw, cb, lg, lb,
                ident_d, mask_p, mask_s, y_p, y_s, nk_p, nv_p, nc_p, nk_s, nv_s, nc_s):
    scr = nc.dram_tensor("qkv_scratch", (3, TOK, DA), F32, kind="Internal").ap()

    with ExitStack() as ctx:
        def const(name, shape, dt=F32):
            return ctx.enter_context(nc.sbuf_tensor(name, shape, dt))

        def sem(name):
            return ctx.enter_context(nc.semaphore(name))

        ident = const("ident", [P, P])
        ones_c = const("ones_c", [P, P])
        g1s = const("g1s", [P, KT])
        g2s = const("g2s", [P, KT])
        qkgs = const("qkgs", [P, 2, DH])
        cws = const("cws", [P, CT * TAPS])
        cbs = const("cbs", [P, CT])
        lgs = const("lgs", [P, CT])
        lbs = const("lbs", [P, CT])
        ssx = const("ssx", [P, NT])
        rsx = const("rsx", [P, NT])
        ssh = const("ssh", [P, 2, H])
        rsh = const("rsh", [P, 2, H])
        nmx = const("nmx", [P, 2])
        mxs = const("mxs", [P, 2])
        den = const("den", [P, 2])
        rden = const("rden", [P, 2])

        def place(at, name, shape, dt=F32):
            with ExitStack() as s:
                if at:
                    s.enter_context(nc.sbuf_tensor(f"below_{name}", [P, at // 4], F32))
                return s.enter_context(nc.sbuf_tensor(name, shape, dt))

        def row(name, ats, shape, dt=F32):
            t = place(ats[0], name, shape, dt)
            n = 4
            for d in shape[1:]:
                n *= d
            ats[0] += -(-n // 64) * 64
            return t

        RAW0 = 0
        WS0 = RAW0 + 2 * PC * 4
        WS4 = WS0 + 4 * 2 * PC * 4
        UC0 = WS0 + 8 * 2 * PC * 4
        GAP0 = -(-(UC0 + (CT + 1) * UW * 4) // 64) * 64
        M0 = 139968
        raw = place(RAW0, "raw", [P, 2, PC])
        ws = place(WS0, "ws", [P, 8, 2, PC], F32R)
        uc = place(UC0, "uc", [P, (CT + 1) * UW])
        at = [GAP0]
        xh = row("xh", at, [P, KT, TOK], F32R)
        xl = row("xl", at, [P, KT, TOK], F32R)
        tmp0 = at[0]
        xr = row("xr", at, [P, 4, TOK])
        xn = row("xn", at, [P, 2, D])
        rb = row("rb", at, [P, TOK])
        rbt = row("rbt", at, [P, 2, P])
        at = [tmp0]
        glu_g = row("glu_g", at, [P, 364])
        glu_s = row("glu_s", at, [P, 364])
        glu_a = row("glu_a", at, [P, 364])
        zt = row("zt", at, [P, 2, DA])
        zo = row("zo", at, [P, 2, DA])
        zsq = row("zsq", at, [P, DA])
        at = [WS4]
        tb = row("tb", at, [P, 2, D])
        pt = row("pt", at, [P, 2, D])
        skt = row("skt", at, [P, 4, CK])
        mks = row("mks", at, [P, SK])
        assert at[0] <= UC0
        at = [GAP0]
        sv = row("sv", at, [P, 4, CKT, P])
        qt = row("qt", at, [P, TOK])
        kt_ = row("kt", at, [P, TOK])
        vn = row("vn", at, [P, SEQ // P, P])
        vns = row("vns", at, [P, NB_S, P])
        qks = row("qks", at, [P, 2, P])
        mkp = row("mkp", at, [P, D])
        qb = row("qb", at, [P, NB_S, 32])
        assert at[0] <= M0
        qn, kn = raw[:, 0, :], raw[:, 1, :]
        at = [M0]
        mh = row("mh", at, [P, KT, TOK], F32R)
        ml = row("ml", at, [P, KT, TOK], F32R)
        at = [WS4]
        sq = row("sq", at, [P, CT, 512])
        nrm = row("nrm", at, [P, CT, 512])
        rstd_c = row("rstd_c", at, [P, TOK])
        csil = row("csil", at, [P, 2, 512])
        assert at[0] <= UC0
        ACT0 = WS4 + 2 * 2 * PC * 4
        Y0 = M0 - NT * D * 4
        y = place(Y0, "y", [P, NT, D])
        at = [UC0 + 16384]
        tn = row("tn", at, [P, D])
        hg = row("hg", at, [P, 2, 512])
        assert at[0] <= Y0 + 0
        at = [ACT0]
        ah = row("ah", at, [P, 4, TOK], F32R)
        al = row("al", at, [P, 4, TOK], F32R)
        sg = row("sg", at, [P, 2, 364])
        pr = row("pr", at, [P, 2, 364])
        assert at[0] <= Y0

        ps = ctx.enter_context(nc.psum_tensor("ps", [P, 8 * 512], F32))

        def bank(b, n=512, off=0):
            return ps[:, b * 512 + off:b * 512 + off + n]

        c_in = sem("consts_in")
        x_in = [sem(f"x_in{k}") for k in range(KT)]
        x_hi, x_lo = sem("x_hi"), sem("x_lo")
        xn_in = [sem("xn_in0"), sem("xn_in1")]
        xsq = sem("x_squares")
        ms_x, sd_x, rs_x = sem("x_meansq"), sem("x_rms"), sem("x_rstd")
        rbt_s, rbt_t, rb_s = sem("rstd_wide"), sem("rstd_turned"), sem("rstd_rows")
        raw_in = [sem("raw_in0"), sem("raw_in1")]
        w_hi, w_lo = sem("w_hi"), sem("w_lo")
        mem_s = sem("memsets")
        ag_mm, ag_ga, ag_sig, ag_aa, ag_u = (sem("ag_mm"), sem("ag_gate"), sem("ag_sigmoid"), sem("ag_a"),
                                             sem("ag_u"))
        st_in, st_out = sem("state_in"), sem("state_out")
        c_mm, c_z, c_sq, c_ss, c_rt, c_rs, c_n, c_o = (sem("qkv_mm"), sem("qkv_z"), sem("qkv_sq"), sem("qkv_ss"),
                                                 sem("qkv_rms"), sem("qkv_rstd"), sem("qkv_normed"), sem("qkv_out"))
        c_st = [sem("qkv_stored0"), sem("qkv_stored1")]
        d_msk = sem("masks_in")
        d_q, d_v = sem("pair_qk_in"), sem("pair_v_in")
        d_sk = [sem(f"sample_k_in{i}") for i in range(4)]
        d_sv = [sem(f"sample_v_in{i}") for i in range(4)]
        d_tr, d_ev, d_qb = sem("turned"), sem("turned_out"), sem("qb_ready")
        d_s, d_tt, d_mx, d_ex, d_rc, d_sc, d_pt, d_pv = (
            sem("scores"), sem("scores_masked"), sem("maximum"), sem("exped"), sem("den_recip"), sem("normed"),
            sem("probs_turned"), sem("values_summed"))
        d_oh, d_ol = sem("attn_hi"), sem("attn_lo")
        cv_a, cv_b = sem("conv_prompt"), sem("conv_samples")
        n_mm, n_xc, n_sq, n_vm, n_sd, n_rs, n_nm, n_si, n_hi, n_lo = (sem(f"ln_{x}") for x in (
            "mean", "centred", "squares", "var", "std", "rstd", "normed", "swish", "hi", "lo"))
        y_in = sem("residual_in")
        e_mm, e_y, e_ss, e_ms, e_sd, e_rs, e_tn, e_tr, e_g, e_hi, e_lo = (sem(f"out_{x}") for x in (
            "mm", "y", "ss", "ms", "sd", "rs", "tn", "turned", "g", "hi", "lo"))
        gu_mm, gu_si, gu_pr, gu_hi, gu_lo = (sem(f"glu_{x}") for x in ("mm", "silu", "prod", "hi", "lo"))
        dn_mm, dn_y = sem("down_mm"), sem("down_y")
        own_wait = sem("own_wait")
        s_out, s_cp = sem("outputs"), sem("cache_copies")

        def hi(slot):
            return ws[:, slot, 0, :]

        def lo(slot):
            return ws[:, slot, 1, :]

        def mm3(e, out, wh, wl, mh_, ml_, first, last):
            e.matmul(out, wh, mh_, start=first, stop=False)
            e.matmul(out, wh, ml_, start=False, stop=False)
            return e.matmul(out, wl, mh_, start=False, stop=last)

        def ustate(c, a, b):
            return uc[:, c * UW + SMP:(c + 1) * UW].rearrange("p (b n) -> p b n", b=NB_S)[:, :, a:b]

        N_B, N_QKV, N_OUT = 2 * CT, 12, 8
        E0 = N_B + N_QKV
        F0 = E0 + N_OUT
        L0 = F0 + 4
        CP_BEFORE = NB_S - 5

        def ln_cols(b, c):
            b0, w = LNB[b]
            return uc[:, c * UW + b0:c * UW + b0 + w] if b < 2 else ustate(c, 0, TS)

        def ln_mean(b):
            return bank(b, LNB[b][1])

        def ln_var(b):
            return bank(4 + b, LNB[b][1])

        def e_part(t_, t, q):
            r0, skip = (TILES[t], 0) if t < NT - 1 else (SEQ, P - NS)
            return t_[:, 4 * q:4 * q + 4, r0:r0 + P - skip], hg[:, q].rearrange("p (k r) -> p k r", k=4)[:, :, skip:P]

        block = ctx.enter_context(nc.Block())

        @block.sync
        def _(sp):
            def piece(n, k):
                if not isinstance(n, int) or n >= 2:
                    sp.wait_ge(w_lo, n - 1)
                src = w_stream[n] if isinstance(n, int) else w_stream[ds(n, 1)].rearrange("a p c -> (a p) c")
                sp.dma_start(raw[:, k % 2, :], src).then_inc(raw_in[k % 2], 16)

            sp.dma_start(g1s[:], g1).then_inc(c_in, 16)
            for k in range(4):
                sp.dma_start(xr[:, k, :], xT[k]).then_inc(x_in[k], 16)
            piece(0, 0)
            piece(1, 1)
            for k in range(4, KT):
                sp.wait_ge(x_lo, k - 3)
                sp.dma_start(xr[:, k % 4, :], xT[k]).then_inc(x_in[k], 16)
            for dst, src in ((ident[:], ident_d), (g2s[:], g2), (qkgs[:], qkg), (cws[:], cw), (cbs[:], cb),
                             (lgs[:], lg), (lbs[:], lb)):
                sp.dma_start(dst, src).then_inc(c_in, 16)
            for c in range(CT):
                sp.dma_start(ustate(c + 1, 0, PADC), stT[c]).then_inc(st_in, 16)
            for t, r0 in enumerate(TILES):
                if t >= 2:
                    sp.wait_ge(xsq, t - 1)
                sp.dma_start(xn[:, t % 2, :], x_all[r0:r0 + P, :]).then_inc(xn_in[t % 2], 16)
            for n in range(2, N_B + 8):
                piece(n, n)
            sp.wait_ge(ag_u, 3 * CT + CT)
            for c in range(CT):
                sp.dma_start(nc_p[c], uc[:, (c + 1) * UW + SEQ:(c + 1) * UW + SEQ + PADC]).then_inc(st_out, 16)
                sp.dma_start(nc_s[c], ustate(c + 1, TS, SW)).then_inc(st_out, 16)

            def store_block(j):
                for t, r0 in enumerate(TILES):
                    m = j * NT + t
                    sp.wait_ge(c_o if j < 2 else c_z, m + 1)
                    if t < NT - 1:
                        dst, src = scr[j, r0:r0 + P, :], zo[:, m % 2, :]
                    else:
                        dst, src = scr[j, SEQ:TOK, :], zo[P - NS:P, m % 2, :]
                    sp.dma_start(dst, src).then_inc(c_st[m % 2], 16)

            store_block(0)
            for n in range(N_B + 8, N_B + 12):
                piece(n, n)
            store_block(1)
            for n in range(E0, E0 + 4):
                piece(n, n)
            store_block(2)

            sp.wait_ge(c_mm, 3 * NT)
            sp.dma_start(mkp[:], mask_p).then_inc(d_msk, 16)
            sp.dma_start(mks[:], mask_s).then_inc(d_msk, 16)
            sp.wait_ge(c_st[0], 16 * 14)
            sp.wait_ge(c_st[1], 16 * 13)
            sp.wait_ge(w_lo, E0 + 4)
            with sp.Fori(0, NPAIR) as p:
                cols = ds(p * P, P)

                def tiles(j):
                    return scr[j, 0:SEQ, cols].rearrange("(t r) c -> r t c", r=P)

                sp.wait_ge(d_qb, 1 + p)
                sp.dma_start(qn.rearrange("p (t c) -> p t c", c=P), tiles(0)).then_inc(d_q, 16)
                sp.dma_start(kn.rearrange("p (t c) -> p t c", c=P), tiles(1)).then_inc(d_q, 16)
                sp.dma_start(qks[0:NS, 0, :], scr[0, SEQ:TOK, cols]).then_inc(d_q, 16)
                sp.dma_start(qks[0:NS, 1, :], scr[1, SEQ:TOK, cols]).then_inc(d_q, 16)
                for b in range(4):
                    sp.wait_ge(d_s, 1 + p * NU)
                    sp.dma_start(skt[:, b, :], kT_c[ds(p * NB_S + b, 1)].rearrange("a p c -> (a p) c")).then_inc(
                        d_sk[b], 16)
                sp.wait_ge(d_pv, 1 + p * NU)
                sp.dma_start(vn[:], tiles(2)).then_inc(d_v, 16)
                sp.dma_start(vns[0:TS, :, :], scr[2, SEQ:TOK, cols].rearrange("(b t) c -> t b c", t=TS)).then_inc(
                    d_v, 16)
                for b in range(4):
                    sp.dma_start(sv[:, b], v_c[ds(p * NB_S + b, 1)].rearrange("a p k c -> (a p) k c")).then_inc(
                        d_sv[b], 16)
                sp.wait_ge(d_s, 1 + p * NU + 9)
                for b in range(4):
                    sp.dma_start(skt[:, b, :], kT_c[ds(p * NB_S + 4 + b, 1)].rearrange("a p c -> (a p) c")).then_inc(
                        d_sk[b], 16)
                sp.wait_ge(d_pv, 1 + p * NU + 9)
                for b in range(4):
                    sp.dma_start(sv[:, b], v_c[ds(p * NB_S + 4 + b, 1)].rearrange("a p k c -> (a p) k c")).then_inc(
                        d_sv[b], 16)

            sp.wait_ge(d_ol, 1 + NOG * NPAIR)
            sp.wait_ge(d_pv, 1 + NU * NPAIR)
            sp.wait_ge(cv_a, 1 + TAPS * NPAIR)
            sp.wait_ge(cv_b, 1 + TAPS * NPAIR)
            sp.dma_start(y[:, 0:NT - 1, :], x_all[0:SEQ, :].rearrange("(t r) c -> r t c", r=P)).then_inc(y_in, 16)
            sp.dma_start(y[:, NT - 1, :], x_all[TOK - P:TOK, :]).then_inc(y_in, 16)
            for n in range(E0 + 4, F0 + 4):
                piece(n, n)
            for j, (dst_p, dst_s) in ((1, (nk_p, nk_s)), (2, (nv_p, nv_s))):
                sp.dma_start(dst_p, scr[j, 0:SEQ, :]).then_inc(s_cp, 16)
                sp.dma_start(dst_s[:, LB:LB + TS, :],
                             scr[j, SEQ:TOK, :].rearrange("(b t) c -> b t c", t=TS)).then_inc(s_cp, 16)
            with sp.Fori(0, (NCH - 1) // 2) as i:
                for k in range(12):
                    piece(i * 12 + (L0 + k), L0 + k)
            for n in range(N_PIECES - 2, N_PIECES):
                piece(n, n)
            for t, r0 in enumerate(TILES):
                sp.wait_ge(dn_y, 1 + 2 * NT * (NCH - 1) + 2 * (t + 1))
                if t < NT - 1:
                    sp.dma_start(y_p[r0:r0 + P, :], y[:, t, :]).then_inc(s_out, 16)
                else:
                    sp.dma_start(y_s, y[P - NS:P, t, :]).then_inc(s_out, 16)
            sp.wait_ge(s_out, 16 * NT)
            sp.wait_ge(s_cp, 16 * 4 + 16 * 2 * NB_S)
            sp.wait_ge(st_out, 16 * 2 * CT)

        @block.gpsimd
        def _(pool):
            pool.memset(ones_c[:], 1.0 / DC).then_inc(mem_s, 1)
            for c in range(CT):
                pool.memset(uc[:, (c + 1) * UW:(c + 1) * UW + PADC], 0.0).then_inc(mem_s, 1)

            def cut(n, k, slot):
                per = n // 2 if isinstance(n, int) else None
                pool.wait_ge(raw_in[k % 2], 16 * (per + 1))
                pool.tensor_copy(hi(slot), raw[:, k % 2, :]).then_inc(w_hi, 1)
                pool.wait_ge(w_hi, n + 1)
                pool.tensor_tensor(lo(slot), raw[:, k % 2, :], hi(slot).bitcast(F32), ALU.subtract).then_inc(w_lo, 1)

            for n in range(N_B):
                if n >= 4:
                    pool.wait_ge(ag_mm, 3 * (n // 2 - 1))
                cut(n, n, n % 4)
            for j in range(3):
                if j == 1:
                    pool.wait_ge(ag_mm, 3 * CT)
                if j == 2:
                    pool.wait_ge(c_mm, NT)
                for m in range(4):
                    n = N_B + 4 * j + m
                    cut(n, n, m + (0 if j == 1 else 4))
            pool.wait_ge(c_mm, 2 * NT)
            for m in range(4):
                cut(E0 + m, E0 + m, m)
            pool.wait_ge(n_lo, CT * 3)
            for m in range(4):
                cut(E0 + 4 + m, E0 + 4 + m, 4 + m)
            pool.wait_ge(e_mm, NT)
            for m in range(4):
                cut(F0 + m, F0 + m, m)
            with pool.Fori(0, (NCH - 1) // 2) as i:
                for half in range(2):
                    for m in range(6):
                        k = L0 + 6 * half + m
                        if m == 0:
                            pool.wait_ge(gu_mm, i * 12 + (6 * half + 3))
                        if m == 2:
                            pool.wait_ge(gu_mm, i * 12 + (6 * half + 6))
                        if m == 4:
                            if half == 0:
                                pool.wait_ge(e_mm, 2 * NT)
                            pool.wait_ge(dn_mm, 1 + i * (4 * NT) + 2 * NT * half)
                        pool.wait_ge(raw_in[k % 2], i * (16 * 6) + 16 * (k // 2 + 1))
                        pool.sem_inc(own_wait, 1)
                        slot = m
                        pool.tensor_copy(hi(slot), raw[:, k % 2, :]).then_inc(w_hi, 1)
                        pool.wait_ge(w_hi, i * 12 + (k + 1))
                        pool.tensor_tensor(lo(slot), raw[:, k % 2, :], hi(slot).bitcast(F32),
                                           ALU.subtract).then_inc(w_lo, 1)
            pool.wait_ge(dn_mm, 1 + 2 * NT * (NCH - 1))
            for m in range(2):
                n = N_PIECES - 2 + m
                cut(n, n, 4 + m)

        @block.tensor
        def _(pe):
            pe.sem_inc(d_s, 1)
            pe.sem_inc(d_pv, 1)
            pe.sem_inc(d_tr, 1)
            pe.sem_inc(dn_mm, 1)
            pe.wait_ge(x_lo, KT)
            g = 0
            for c in range(CT):
                pe.wait_ge(w_lo, 2 * (c + 1))
                for b0, bn in BLOCKS:
                    if g >= 2:
                        pe.wait_ge(ag_aa, g - 1)
                    for side in range(2):
                        out = bank(2 * (g % 2) + side, bn)
                        slot = (2 * c + side) % 4
                        for k in range(KT):
                            last = mm3(pe, out, hi(slot)[:, k * P:(k + 1) * P], lo(slot)[:, k * P:(k + 1) * P],
                                       xh[:, k, b0:b0 + bn], xl[:, k, b0:b0 + bn], k == 0, k == KT - 1)
                    last.then_inc(ag_mm, 1)
                    g += 1
                    if g == 2:
                        pe.wait_ge(c_in, 16 * 8)
                        for t, r0 in enumerate(TILES):
                            pe.wait_ge(rbt_s, t + 1)
                            pe.transpose(bank(4 + t // 4, P, (t % 4) * P), rbt[:, t % 2, :], ident[:]).then_inc(
                                rbt_t, 1)
            m = 0
            for j in range(3):
                pe.wait_ge(w_lo, N_B + 4 * (j + 1))
                s0 = 0 if j == 1 else 4
                for t, r0 in enumerate(TILES):
                    if m == 0:
                        pe.wait_ge(rb_s, 3)
                    if m >= 4:
                        pe.wait_ge(c_z, m - 3)
                    for k in range(KT):
                        wcol = slice((k % 2) * DA, (k % 2 + 1) * DA)
                        last = mm3(pe, bank(4 + m % 4), xh[:, k, r0:r0 + P], xl[:, k, r0:r0 + P],
                                   hi(s0 + k // 2)[:, wcol], lo(s0 + k // 2)[:, wcol], k == 0, k == KT - 1)
                    last.then_inc(c_mm, 1)
                    m += 1
            pe.wait_ge(c_z, 3 * NT)
            pe.wait_ge(ag_aa, 3 * CT)
            with pe.Fori(0, NPAIR) as p:
                pe.wait_ge(d_q, p * 64 + 64)

                def quad_wait(q):
                    pe.wait_ge(d_ev, 1 + p * NQ + max(q - 1, 0))

                for q, (src, t0) in enumerate(((qn, 0), (qn, 4), (kn, 0), (kn, 4))):
                    quad_wait(q)
                    for t in range(4):
                        last = pe.transpose(bank(4 + q % 2, P, t * P), src[:, (t0 + t) * P:(t0 + t + 1) * P], ident[:])
                    last.then_inc(d_tr, 1)
                for q in (4, 5):
                    quad_wait(q)
                    pe.sem_inc(own_wait, 1)
                    pe.transpose(bank(4 + q % 2, NS), qks[0:NS, q - 4, :], ident[0:NS, 0:NS]).then_inc(d_tr, 1)

                def scores(u):
                    kind, h, i = UNITS[u]
                    pe.wait_ge(d_tt, 1 + p * NU + max(u - 1, 0))
                    s = 2 * (u % 2)
                    if kind == "p":
                        if u == 0:
                            pe.wait_ge(d_ev, 1 + p * NQ + 4)
                        rows = slice(DH * h, DH * h + DH)
                        n = (i + 1) * P
                        for c0 in range(0, n, 512):
                            cn = min(512, n - c0)
                            last = pe.matmul(bank(s + c0 // 512, cn), qt[rows, i * P:(i + 1) * P],
                                             kt_[rows, c0:c0 + cn], start=True, stop=True)
                    else:
                        if h == 0:
                            pe.wait_ge(d_qb, 1 + p + 1)
                            pe.wait_ge(d_ev, 1 + p * NQ + 6)
                        for bb in range(4):
                            b = 4 * h + bb
                            pe.wait_ge(d_sk[bb], p * 32 + 16 * (h + 1))
                            out = slice(32 * bb, 32 * bb + 32)
                            for bk, k0, k1 in ((s, 0, 512), (s + 1, 512, CK)):
                                pe.matmul(ps[out, bk * 512:bk * 512 + k1 - k0], qb[:, b, :], skt[:, bb, k0:k1],
                                          start=True, stop=True)
                            last = pe.matmul(ps[out, s * 512 + CK:s * 512 + SK], qb[:, b, :],
                                             kt_[:, SEQ + TS * b:SEQ + TS * (b + 1)], start=True, stop=True)
                    last.then_inc(d_s, 1)

                def turn(u):
                    q, n = UQ[u]
                    pe.wait_ge(d_sc, p * NU + (u + 1))
                    for c in range(n):
                        if c % 4 == 0:
                            quad_wait(q + c // 4)
                        w = P if UNITS[u][0] == "p" or c < CKT else TS
                        last = pe.transpose(bank(4 + (q + c // 4) % 2, P, (c % 4) * P)[0:w, :],
                                            tb[:, u % 2, c * P:c * P + w], ident[:])
                        if c % 4 == 3 or c == n - 1:
                            last.then_inc(d_tr, 1)

                def values(u):
                    kind, h, i = UNITS[u]
                    q, n = UQ[u]
                    pe.wait_ge(d_ev, 1 + p * NQ + (q + (n + 3) // 4))
                    if u == 0:
                        pe.wait_ge(d_v, p * 32 + 32)
                    buf = u % 2
                    if kind == "p":
                        if i % 4 == 0:
                            group_wait(3 * h + i // 4)
                        o0 = (6 + (3 * h + i // 4) % 2) * 512 + (i % 4) * P
                        out = ps[DH * h:DH * h + DH, o0:o0 + P]
                        for c in range(n):
                            last = pe.matmul(out, vn[:, c, DH * h:DH * h + DH], pt[:, buf, c * P:(c + 1) * P],
                                             start=(c == 0), stop=(c == n - 1))
                    else:
                        og = 3 * h + 2
                        group_wait(og)
                        for bb in range(4):
                            b = 4 * h + bb
                            pe.wait_ge(d_sv[bb], p * 32 + 16 * (h + 1))
                            out = bank(6 + og % 2, 16, bb * 16)
                            for c in range(CKT):
                                pe.matmul(out, sv[:, bb, c, :], pt[:, buf, c * P + 32 * bb:c * P + 32 * bb + 16],
                                          start=(c == 0), stop=False)
                            last = pe.matmul(out, vns[0:TS, b, :],
                                             pt[0:TS, buf, CK + 32 * bb:CK + 32 * bb + 16], start=False, stop=True)
                    last.then_inc(d_pv, 1)

                def group_wait(og):
                    pe.wait_ge(d_ol, 1 + p * NOG + max(og - 1, 0))

                scores(0)
                for u in range(NU):
                    if u + 1 < NU:
                        scores(u + 1)
                    if u >= 1:
                        values(u - 1)
                    turn(u)
                values(NU - 1)
            pe.wait_ge(cv_a, 1 + TAPS * CT)
            pe.wait_ge(cv_b, 1 + TAPS * CT)
            pe.wait_ge(mem_s, 1)
            pe.wait_ge(d_tt, 1 + NU * NPAIR)
            for b in range(3):
                for c in range(CT):
                    last = pe.matmul(ln_mean(b), ones_c[:], ln_cols(b, c), start=(c == 0), stop=(c == CT - 1))
                last.then_inc(n_mm, 1)
            for b in range(3):
                pe.wait_ge(n_sq, CT * (b + 1))
                w = LNB[b][1]
                for c in range(CT):
                    last = pe.matmul(ln_var(b), ones_c[:], sq[:, c, 0:w],
                                     start=(c == 0), stop=(c == CT - 1))
                last.then_inc(n_vm, 1)
            pe.wait_ge(n_lo, 3 * CT)
            pe.wait_ge(d_ol, 1 + NOG * NPAIR)
            pe.wait_ge(d_ev, 1 + NQ * NPAIR)
            m = 0
            tq = 0

            def project(nh, t, m):
                if m >= 4:
                    pe.wait_ge(e_y, m - 3)
                r0 = TILES[t]
                for k in range(KT):
                    slot = 4 * nh + k // 2
                    wcol = slice((k % 2) * 512, (k % 2 + 1) * 512)
                    last = mm3(pe, bank(4 + m % 4), mh[:, k, r0:r0 + P], ml[:, k, r0:r0 + P],
                               hi(slot)[:, wcol], lo(slot)[:, wcol], k == 0, k == KT - 1)
                last.then_inc(e_mm, 1)

            def turn_back(n):
                pe.wait_ge(e_tn, n + 1)
                for q in range(2):
                    tq = 2 * n + q
                    if tq >= 4:
                        pe.wait_ge(e_g, tq - 3)
                    for c in range(4):
                        last = pe.transpose(bank(tq % 4, P, c * P), tn[:, (4 * q + c) * P:(4 * q + c + 1) * P], ident[:])
                    last.then_inc(e_tr, 1)

            pe.wait_ge(w_lo, E0 + 4)
            for n, t in enumerate(E_ORDER):
                project(0, t, n)
            pe.wait_ge(w_lo, E0 + 8)
            for n, t in enumerate(E_ORDER):
                project(1, t, NT + n)
                if n >= 1:
                    turn_back(n - 1)
            turn_back(NT - 1)

            def gate_up(c6, cslot, i=None):
                base = 0 if i is None else i * 12
                for f in range(2):
                    npc = (F0 + 4 if i is None else i * 12 + (L0 + cslot * 6 + 4))
                    pe.wait_ge(w_lo, npc - 2 * (1 - f))
                    for b, (b0, bn) in enumerate(BLOCKS):
                        k6 = c6 + 3 * f + b
                        if k6 >= 2:
                            pe.wait_ge(gu_pr, base + (k6 - 1))
                        for side in range(2):
                            out = bank(2 * (k6 % 2) + side, bn)
                            slot = 2 * f + side
                            for k in range(KT):
                                last = mm3(pe, out, hi(slot)[:, k * P:(k + 1) * P], lo(slot)[:, k * P:(k + 1) * P],
                                           mh[:, k, b0:b0 + bn], ml[:, k, b0:b0 + bn], k == 0, k == KT - 1)
                        last.then_inc(gu_mm, 1)

            def down(half, i=None):
                base_m = 0 if i is None else i * (4 * NT)
                const_m = 2 * NT * half if i is not None else 2 * NT * (NCH - 1)
                if i is None:
                    pe.wait_ge(w_lo, N_PIECES)
                    pe.wait_ge(gu_lo, 6 * NCH)
                else:
                    pe.wait_ge(w_lo, i * 12 + (L0 + 6 * half + 6))
                    pe.wait_ge(gu_lo, i * 12 + 6 * (half + 1))
                a0 = 2 * half
                for t, r0 in enumerate(TILES):
                    for nh in range(2):
                        m = 2 * t + nh
                        v = const_m + m - 3
                        if v > 0:
                            pe.wait_ge(dn_y, 1 + base_m + v)
                        elif i is not None:
                            pe.wait_ge(dn_y, 1 + base_m + 0)
                        for f in range(2):
                            last = mm3(pe, bank(4 + (const_m + m) % 4), ah[:, a0 + f, r0:r0 + P],
                                       al[:, a0 + f, r0:r0 + P], hi(4 + f)[:, nh * 512:(nh + 1) * 512],
                                       lo(4 + f)[:, nh * 512:(nh + 1) * 512], f == 0, f == 1)
                        last.then_inc(dn_mm, 1)

            pe.wait_ge(e_lo, 2 * NT)
            gate_up(0, 0)
            with pe.Fori(0, (NCH - 1) // 2) as i:
                gate_up(6, 0, i)
                down(0, i)
                gate_up(12, 1, i)
                down(1, i)
            down(0)

        @block.scalar
        def _(act):
            act.sem_inc(d_ev, 1)
            act.sem_inc(d_ex, 1)
            act.wait_ge(c_in, 16)
            for k in range(KT):
                act.wait_ge(x_in[k], 16)
                act.activation(xh[:, k, :], xr[:, k % 4, :], ACT.Copy, scale=g1s[:, k:k + 1]).then_inc(x_hi, 1)
            for t in range(NT):
                act.wait_ge(xn_in[t % 2], 16 * (t // 2 + 1))
                act.activation(xn[:, t % 2, :], xn[:, t % 2, :], ACT.Square, accum_out=ssx[:, t:t + 1]).then_inc(xsq, 1)
            act.wait_ge(ms_x, 1)
            act.activation(rsx[:], ssx[:], ACT.Sqrt).then_inc(sd_x, 1)
            for g in range(3 * CT):
                bn = BLOCKS[g % 3][1]
                act.wait_ge(ag_ga, g + 1)
                if g >= 1:
                    act.wait_ge(ag_u, 4 * (g // 3) + (g % 3))
                act.activation(glu_s[:, 0:bn], glu_g[:, 0:bn], ACT.Sigmoid).then_inc(ag_sig, 1)
            for m in range(2 * NT):
                act.wait_ge(c_z, m + 1)
                if m >= 1:
                    act.wait_ge(c_ss, m)
                act.activation(zsq[:], zt[:, m % 2, :], ACT.Square).then_inc(c_sq, 1)
                act.wait_ge(c_ss, m + 1)
                act.activation(rsh[:, m % 2, :], ssh[:, m % 2, :], ACT.Sqrt).then_inc(c_rt, 1)
            with act.Fori(0, NPAIR) as p:
                def evac_quad(q, dst, src):
                    act.wait_ge(d_tr, 1 + p * NQ + (q + 1))
                    act.activation(dst, src, ACT.Copy).then_inc(d_ev, 1)

                act.wait_ge(d_s, 1 + p * NU)
                for q in range(4):
                    dst = (qt, kt_)[q // 2]
                    evac_quad(q, dst[:, (q % 2) * 512:(q % 2 + 1) * 512], bank(4 + q % 2))
                for q in (4, 5):
                    dst = (qt, kt_)[q - 4]
                    evac_quad(q, dst[:, SEQ:TOK], bank(4 + q % 2, NS))

                def exps(u):
                    n = UQ[u][1] * P if UNITS[u][0] == "p" else SK
                    act.wait_ge(d_mx, p * NU + (u + 1))
                    act.wait_ge(d_rc, 1 + p * NU + max(u - 1, 0))
                    act.activation(tb[:, u % 2, 0:n], tb[:, u % 2, 0:n], ACT.Exp, bias=nmx[:, u % 2:u % 2 + 1],
                                   accum_out=den[:, u % 2:u % 2 + 1]).then_inc(d_ex, 1)

                def evac(u):
                    q, n = UQ[u]
                    act.wait_ge(d_pv, 1 + p * NU + max(u - 1, 0))
                    for c0 in range(0, n, 4):
                        cn = min(4, n - c0)
                        qq = q + c0 // 4
                        b = 4 + qq % 2
                        if UNITS[u][0] == "s" and c0 == 4:
                            act.wait_ge(d_tr, 1 + p * NQ + (qq + 1))
                            act.activation(pt[:, u % 2, 512:CK], bank(b, CK - 512), ACT.Copy)
                            act.activation(pt[0:TS, u % 2, CK:CK + P], bank(b, P, CK - 512)[0:TS, :],
                                           ACT.Copy).then_inc(d_ev, 1)
                        else:
                            evac_quad(qq, pt[:, u % 2, c0 * P:(c0 + cn) * P], bank(b, cn * P))

                exps(0)
                for u in range(NU):
                    if u + 1 < NU:
                        exps(u + 1)
                    evac(u)
            for b, (b0, w) in enumerate(LNB):
                for c in range(CT):
                    act.wait_ge(n_xc, CT * b + c + 1)
                    if b >= 1:
                        act.wait_ge(n_vm, b)
                    act.activation(sq[:, c, 0:w], ln_cols(b, c), ACT.Square).then_inc(n_sq, 1)
            for b, (b0, w) in enumerate(LNB):
                act.wait_ge(n_rs, b + 1)
                act.activation(rstd_c[:, b0:b0 + w], rstd_c[:, b0:b0 + w], ACT.Sqrt).then_inc(n_sd, 1)
            s = 0
            for b, (b0, w) in enumerate(LNB):
                for c in range(CT):
                    act.wait_ge(n_nm, s + 1)
                    if s >= 2:
                        act.wait_ge(n_lo, s - 1)
                    act.activation(csil[:, s % 2, 0:w], nrm[:, c, 0:w], ACT.Silu, scale=lgs[:, c:c + 1],
                                   bias=lbs[:, c:c + 1]).then_inc(n_si, 1)
                    act.wait_ge(n_si, s + 1)
                    act.activation(mh[:, CT + c, b0:b0 + w], csil[:, s % 2, 0:w], ACT.Copy).then_inc(n_hi, 1)
                    s += 1
            def hi_back(n):
                for q in range(2):
                    act.wait_ge(e_g, 2 * n + q + 1)
                    dst, src = e_part(mh, E_ORDER[n], q)
                    act.activation(dst, src, ACT.Copy).then_inc(e_hi, 1)

            for n, t in enumerate(E_ORDER):
                act.wait_ge(e_y, NT + n + 1)
                if n >= 1:
                    act.wait_ge(e_tr, 2 * n)
                act.activation(tn[:], y[:, t, :], ACT.Square, accum_out=ssx[:, n:n + 1]).then_inc(e_ss, 1)
                act.wait_ge(e_ms, n + 1)
                act.activation(rsx[:, n:n + 1], ssx[:, n:n + 1], ACT.Sqrt).then_inc(e_sd, 1)
                if n >= 1:
                    hi_back(n - 1)
            hi_back(NT - 1)
            for b in range(CP_BEFORE):
                act.dma_start(nk_s[5 + b, 0:LB, :], cache_k[5 + b]).then_inc(s_cp, 16)
                act.dma_start(nv_s[5 + b, 0:LB, :], cache_v[5 + b]).then_inc(s_cp, 16)

            def silus(c6, cslot, i=None):
                base = 0 if i is None else i * 12
                for f in range(2):
                    for b, (b0, bn) in enumerate(BLOCKS):
                        k6 = c6 + 3 * f + b
                        act.wait_ge(gu_mm, base + (k6 + 1))
                        if k6 >= 2:
                            act.wait_ge(gu_pr, base + (k6 - 1))
                        act.activation(sg[:, k6 % 2, 0:bn], bank(2 * (k6 % 2), bn), ACT.Silu).then_inc(gu_si, 1)
                        act.wait_ge(gu_pr, base + (k6 + 1))
                        if f == 0 and b == 0 and i is not None:
                            act.wait_ge(dn_mm, 1 + i * (4 * NT) + (0 if c6 == 6 else 2 * NT))
                        act.activation(ah[:, 2 * cslot + f, b0:b0 + bn], pr[:, k6 % 2, 0:bn], ACT.Copy).then_inc(
                            gu_hi, 1)

            silus(0, 0)
            with act.Fori(0, (NCH - 1) // 2) as i:
                act.dma_start(nk_s[ds(i, 1), 0:LB, :], cache_k[ds(i, 1)]).then_inc(s_cp, 16)
                act.dma_start(nv_s[ds(i, 1), 0:LB, :], cache_v[ds(i, 1)]).then_inc(s_cp, 16)
                silus(6, 1, i)
                silus(12, 0, i)

        @block.vector
        def _(dve):
            dve.sem_inc(d_qb, 1)
            dve.sem_inc(d_tt, 1)
            dve.sem_inc(d_rc, 1)
            dve.sem_inc(d_ol, 1)
            dve.sem_inc(cv_a, 1)
            dve.sem_inc(cv_b, 1)
            dve.sem_inc(dn_y, 1)
            for k in range(KT):
                dve.wait_ge(x_hi, k + 1)
                dve.scalar_tensor_tensor(out=xl[:, k, :], in0=xr[:, k % 4, :], scalar=g1s[:, k:k + 1],
                                         in1=xh[:, k, :].bitcast(F32), op0=ALU.mult, op1=ALU.subtract).then_inc(x_lo, 1)
            dve.wait_ge(xsq, NT)
            dve.tensor_scalar(ssx[:], ssx[:], 1.0 / D, RMS_EPS, ALU.mult, ALU.add).then_inc(ms_x, 1)
            dve.wait_ge(sd_x, 1)
            dve.reciprocal(rsx[:], rsx[:]).then_inc(rs_x, 1)
            dve.wait_ge(rs_x, 1)
            dve.wait_ge(mem_s, 1)
            for t in range(NT):
                if t >= 2:
                    dve.wait_ge(rbt_t, t - 1)
                dve.tensor_scalar(rbt[:, t % 2, :], ones_c[:], float(DC), rsx[:, t:t + 1], ALU.mult,
                                  ALU.mult).then_inc(rbt_s, 1)
            dve.wait_ge(rbt_t, NT)
            for q in range(2):
                dve.tensor_copy(rb[:, q * 512:(q + 1) * 512], bank(4 + q)).then_inc(rb_s, 1)
            dve.tensor_copy(rb[:, SEQ:TOK], bank(6, NS, P - NS)).then_inc(rb_s, 1)
            dve.wait_ge(c_in, 16 * 8)
            dve.tensor_scalar(qkgs[:, 0, :], qkgs[:, 0, :], DH ** -0.5, None, ALU.mult).then_inc(rb_s, 1)
            dve.wait_ge(rb_s, 4)
            nu = 0
            for g in range(3 * CT):
                c, (b0, bn) = g // 3, BLOCKS[g % 3]
                r = rb[:, b0:b0 + bn]
                dve.wait_ge(ag_mm, g + 1)
                if g >= 1:
                    dve.wait_ge(ag_sig, g)
                dve.tensor_tensor(glu_g[:, 0:bn], bank(2 * (g % 2) + 1, bn), r, ALU.mult).then_inc(ag_ga, 1)
                if g >= 1:
                    dve.wait_ge(ag_u, nu)
                dve.tensor_tensor(glu_a[:, 0:bn], bank(2 * (g % 2), bn), r, ALU.mult).then_inc(ag_aa, 1)
                dve.wait_ge(ag_sig, g + 1)
                dve.wait_ge(ag_aa, g + 1)
                if g == 0:
                    dve.wait_ge(mem_s, 1 + CT)
                n = min(bn, SEQ - b0)
                u0 = (c + 1) * UW + PADC + b0
                dve.tensor_tensor(uc[:, u0:u0 + n], glu_a[:, 0:n], glu_s[:, 0:n], ALU.mult).then_inc(ag_u, 1)
                nu += 1
                if n < bn:
                    def by_sample(a):
                        return a[:, n:bn].rearrange("p (b t) -> p b t", t=TS)
                    dve.tensor_tensor(ustate(c + 1, PADC, SW), by_sample(glu_a), by_sample(glu_s),
                                      ALU.mult).then_inc(ag_u, 1)
                    nu += 1
            for m in range(3 * NT):
                j, t = divmod(m, NT)
                dve.wait_ge(c_mm, m + 1)
                if m >= 2:
                    dve.wait_ge(c_st[m % 2], 16 * (m // 2))
                if j == 2:
                    dve.tensor_scalar(zo[:, m % 2, :], bank(4 + m % 4), rsx[:, t:t + 1], None, ALU.mult).then_inc(
                        c_z, 1)
                    continue
                if m >= 2:
                    dve.wait_ge(c_o, m - 1)
                dve.tensor_scalar(zt[:, m % 2, :], bank(4 + m % 4), rsx[:, t:t + 1], None, ALU.mult).then_inc(c_z, 1)
                dve.wait_ge(c_sq, m + 1)
                dve.tensor_reduce(ssh[:, m % 2, :], zsq[:].rearrange("p (h d) -> p h d", d=DH), AX.X,
                                  ALU.add).then_inc(c_n, 1)
                dve.wait_ge(c_n, 2 * m + 1)
                dve.tensor_scalar(ssh[:, m % 2, :], ssh[:, m % 2, :], 1.0 / DH, RMS_EPS, ALU.mult, ALU.add).then_inc(
                    c_ss, 1)
                dve.wait_ge(c_rt, m + 1)
                dve.reciprocal(rsh[:, m % 2, :], rsh[:, m % 2, :]).then_inc(c_rs, 1)
                dve.wait_ge(c_rs, m + 1)
                z3 = zt[:, m % 2, :].rearrange("p (h d) -> p h d", d=DH)
                dve.tensor_tensor(z3, z3, rsh[:, m % 2, :].unsqueeze(2).broadcast_to([P, H, DH]), ALU.mult).then_inc(
                    c_n, 1)
                dve.wait_ge(c_n, 2 * m + 2)
                dve.tensor_tensor(zo[:, m % 2, :].rearrange("p (h d) -> p h d", d=DH), z3,
                                  qkgs[:, j, :].unsqueeze(1).broadcast_to([P, H, DH]), ALU.mult).then_inc(c_o, 1)
            dve.wait_ge(st_in, 16 * CT)
            dve.wait_ge(st_out, 16 * 2 * CT)
            dve.wait_ge(d_msk, 32)
            dve.memset(qb[:], 0.0).then_inc(mem_s, 1)
            dve.wait_ge(mem_s, 2 + CT)
            with dve.Fori(0, NPAIR) as p:
                def conv_tap(j):
                    for s, off, w in ((cv_a, 0, SEQ), (cv_b, SMP, CVS)):
                        dst = uc[:, ds(p * UW + off, w)]
                        src = uc[:, ds(p * UW + (UW + off + j), w)]
                        tap = cws[:, ds(p * TAPS + j, 1)]
                        dve.wait_ge(s, 1 + p * TAPS + j)
                        if j == 0:
                            dve.tensor_scalar(dst, src, tap, cbs[:, ds(p, 1)], ALU.mult, ALU.add).then_inc(s, 1)
                        else:
                            dve.scalar_tensor_tensor(out=dst, in0=src, scalar=tap, in1=dst, op0=ALU.mult,
                                                     op1=ALU.add).then_inc(s, 1)

                def mask_max(u):
                    kind, h, i = UNITS[u]
                    n = UQ[u][1] * P if kind == "p" else SK
                    mask = mkp[:, D - n:D] if kind == "p" else mks[:]
                    dve.wait_ge(d_s, 1 + p * NU + (u + 1))
                    dve.wait_ge(d_tr, 1 + p * NQ + (UQ[u - 1][0] if u >= 2 else 0))
                    dve.sem_inc(own_wait, 1)
                    s = 2 * (u % 2) * 512
                    dve.tensor_tensor_reduce(out=tb[:, u % 2, 0:n], in0=ps[:, s:s + n], in1=mask, scale=1.0,
                                             scalar=-3.0e38, op0=ALU.add, op1=ALU.max,
                                             accum_out=mxs[:, u % 2:u % 2 + 1]).then_inc(d_tt, 1)
                    dve.wait_ge(d_tt, 1 + p * NU + (u + 1))
                    dve.wait_ge(d_ex, 1 + p * NU + max(u - 1, 0))
                    dve.tensor_scalar(nmx[:, u % 2:u % 2 + 1], mxs[:, u % 2:u % 2 + 1], -1.0, None,
                                      ALU.mult).then_inc(d_mx, 1)

                def norm(u):
                    n = UQ[u][1] * P if UNITS[u][0] == "p" else SK
                    dve.wait_ge(d_ex, 1 + p * NU + (u + 1))
                    dve.reciprocal(rden[:, u % 2:u % 2 + 1], den[:, u % 2:u % 2 + 1]).then_inc(d_rc, 1)
                    dve.wait_ge(d_rc, 1 + p * NU + (u + 1))
                    dve.tensor_scalar(tb[:, u % 2, 0:n], tb[:, u % 2, 0:n], rden[:, u % 2:u % 2 + 1], None,
                                      ALU.mult).then_inc(d_sc, 1)

                def outputs(og):
                    kind, h, u0, nu_ = OGS[og]
                    dve.wait_ge(d_pv, 1 + p * NU + (u0 + nu_))
                    if kind == "p":
                        rows = slice(DH * h, DH * h + DH)
                        parts = [(rows, (u0 - 9 * h) * P, 512, bank(6 + og % 2)[rows, :])]
                    else:
                        o = bank(6 + og % 2, 64).rearrange("p (b c) -> p b c", c=16)
                        parts = [(slice(DH * hh, DH * hh + DH), SEQ + 4 * TS * h, 4 * TS,
                                  o[DH * hh:DH * hh + DH, :, TS * hh:TS * hh + TS]) for hh in range(2)]

                    def part(t_, r, c0, w):
                        v = t_[r, ds(p, 1), c0:c0 + w].rearrange("p a c -> p (a c)")
                        return v if kind == "p" else v.rearrange("p (b c) -> p b c", c=TS)

                    for r, c0, w, o in parts:
                        last = dve.tensor_copy(part(mh, r, c0, w), o)
                    last.then_inc(d_oh, 1)
                    dve.wait_ge(d_oh, p * NOG + (og + 1))
                    for r, c0, w, o in parts:
                        last = dve.tensor_tensor(part(ml, r, c0, w), o, part(mh, r, c0, w).bitcast(F32), ALU.subtract)
                    last.then_inc(d_ol, 1)

                mask_max(0)
                dve.wait_ge(d_ev, 1 + p * NQ + 6)
                for h in range(2):
                    rows = slice(DH * h, DH * h + DH)
                    last = dve.tensor_copy(qb[rows, :, TS * h:TS * (h + 1)],
                                           qt[rows, SEQ:TOK].rearrange("p (b t) -> p b t", t=TS))
                last.then_inc(d_qb, 1)
                j = 0
                for u in range(NU):
                    if u + 1 < NU:
                        mask_max(u + 1)
                    norm(u)
                    for _ in range(2):
                        if j < TAPS:
                            conv_tap(j)
                            j += 1
                    for og in range(NOG):
                        if OGS[og][2] + OGS[og][3] == u:
                            outputs(og)
                outputs(NOG - 1)
            def cut_swish(s):
                b, c = divmod(s, CT)
                b0, w = LNB[b]
                dve.wait_ge(n_hi, s + 1)
                dve.tensor_tensor(ml[:, CT + c, b0:b0 + w], csil[:, s % 2, 0:w],
                                  mh[:, CT + c, b0:b0 + w].bitcast(F32), ALU.subtract).then_inc(n_lo, 1)

            dve.wait_ge(cv_a, 1 + TAPS * CT)
            dve.wait_ge(cv_b, 1 + TAPS * CT)
            for b, (b0, w) in enumerate(LNB):
                dve.wait_ge(n_mm, b + 1)
                for c in range(CT):
                    mean = ln_mean(b)
                    if b == 2:
                        mean = mean.rearrange("p (b t) -> p b t", t=TS)
                    dve.tensor_tensor(ln_cols(b, c), ln_cols(b, c), mean, ALU.subtract).then_inc(n_xc, 1)
            for b, (b0, w) in enumerate(LNB):
                dve.wait_ge(n_vm, b + 1)
                dve.tensor_scalar(rstd_c[:, b0:b0 + w], ln_var(b), LN_EPS, None,
                                  ALU.add).then_inc(n_rs, 1)
            s = 0
            for b, (b0, w) in enumerate(LNB):
                dve.wait_ge(n_sd, b + 1)
                dve.reciprocal(rstd_c[:, b0:b0 + w], rstd_c[:, b0:b0 + w]).then_inc(n_rs, 1)
                dve.wait_ge(n_rs, 3 + b + 1)
                for c in range(CT):
                    r = rstd_c[:, b0:b0 + w]
                    o = nrm[:, c, 0:w]
                    if b == 2:
                        r, o = (x.rearrange("p (b t) -> p b t", t=TS) for x in (r, o))
                    if b >= 1:
                        dve.wait_ge(n_si, CT * (b - 1) + c + 1)
                    dve.tensor_tensor(o, ln_cols(b, c), r, ALU.mult).then_inc(n_nm, 1)
                    if s >= 1:
                        cut_swish(s - 1)
                    s += 1
            cut_swish(s - 1)
            def normalise(n, t):
                dve.wait_ge(e_ss, n + 1)
                dve.tensor_scalar(ssx[:, n:n + 1], ssx[:, n:n + 1], 1.0 / D, RMS_EPS, ALU.mult, ALU.add).then_inc(
                    e_ms, 1)
                dve.wait_ge(e_sd, n + 1)
                dve.reciprocal(rsx[:, n:n + 1], rsx[:, n:n + 1]).then_inc(e_rs, 1)
                dve.wait_ge(e_rs, n + 1)
                dve.tensor_scalar(tn[:], y[:, t, :], rsx[:, n:n + 1], None, ALU.mult).then_inc(e_tn, 1)

            def cut_back(n):
                for q in range(2):
                    dve.wait_ge(e_tr, 2 * n + q + 1)
                    if n >= 1:
                        dve.wait_ge(e_lo, 2 * n + q - 1)
                    dve.tensor_tensor(hg[:, q].rearrange("p (k r) -> p k r", k=4),
                                      bank((2 * n + q) % 4).rearrange("p (k r) -> p k r", k=4),
                                      g2s[:, 4 * q:4 * q + 4].unsqueeze(2).broadcast_to([P, 4, P]),
                                      ALU.mult).then_inc(e_g, 1)
                for q in range(2):
                    dve.wait_ge(e_hi, 2 * n + q + 1)
                    h_, src = e_part(mh, E_ORDER[n], q)
                    l_, _ = e_part(ml, E_ORDER[n], q)
                    dve.tensor_tensor(l_, src, h_.bitcast(F32), ALU.subtract).then_inc(e_lo, 1)

            dve.wait_ge(y_in, 32)
            for nh in range(2):
                for n, t in enumerate(E_ORDER):
                    m = NT * nh + n
                    dve.wait_ge(e_mm, m + 1)
                    cols = slice(nh * 512, (nh + 1) * 512)
                    dve.tensor_tensor(y[:, t, cols], bank(4 + m % 4), y[:, t, cols], ALU.add).then_inc(e_y, 1)
                    if nh == 1:
                        normalise(n, t)
                        if n >= 1:
                            cut_back(n - 1)
            cut_back(NT - 1)

            def glus(c6, cslot, i=None):
                base = 0 if i is None else i * 12
                for f in range(2):
                    for b, (b0, bn) in enumerate(BLOCKS):
                        k6 = c6 + 3 * f + b
                        dve.wait_ge(gu_si, base + (k6 + 1))
                        if k6 >= 2:
                            dve.wait_ge(gu_lo, base + (k6 - 1))
                        dve.tensor_tensor(pr[:, k6 % 2, 0:bn], bank(2 * (k6 % 2) + 1, bn), sg[:, k6 % 2, 0:bn],
                                          ALU.mult).then_inc(gu_pr, 1)
                        dve.wait_ge(gu_hi, base + (k6 + 1))
                        dve.tensor_tensor(al[:, 2 * cslot + f, b0:b0 + bn], pr[:, k6 % 2, 0:bn],
                                          ah[:, 2 * cslot + f, b0:b0 + bn].bitcast(F32), ALU.subtract).then_inc(gu_lo, 1)

            def adds(half, i=None):
                base_m = 0 if i is None else i * (4 * NT)
                const_m = 2 * NT * half if i is not None else 2 * NT * (NCH - 1)
                for t in range(NT):
                    for nh in range(2):
                        m = const_m + 2 * t + nh
                        dve.wait_ge(dn_mm, 1 + base_m + (m + 1))
                        if t == 0 and nh == 0:
                            dve.wait_ge(dn_y, 1 + base_m + const_m)
                        cols = slice(nh * 512, (nh + 1) * 512)
                        dve.tensor_tensor(y[:, t, cols], bank(4 + m % 4), y[:, t, cols], ALU.add).then_inc(dn_y, 1)

            glus(0, 0)
            with dve.Fori(0, (NCH - 1) // 2) as i:
                glus(6, 1, i)
                adds(0, i)
                glus(12, 0, i)
                adds(1, i)
            adds(0)


def laid_out(v):
    import numpy as np

    f = {k: np.asarray(a) for k, a in v.items()}
    w_in, w_out, w_gate, w_up, w_down = (f[k][0] for k in ("w_in", "w_out", "w_gate", "w_up", "w_down"))

    def cols(w, c0):
        return w[:, c0:c0 + P].reshape(KT, P, P).transpose(1, 0, 2).reshape(P, PC)

    def two(w, j, c0):
        return w[2 * j * P:(2 * j + 2) * P, c0:c0 + 512].reshape(2, P, 512).transpose(1, 0, 2).reshape(P, PC)

    def gate_up(c):
        return [cols(w, (2 * c + t) * P) for t in range(2) for w in (w_gate, w_up)]

    def down(c):
        return [w_down[(2 * c + t) * P:(2 * c + t + 1) * P] for t in range(2)]

    stream = [cols(w_in, 3 * DA + s * DC + c * P) for c in range(CT) for s in range(2)]
    stream += [two(w_in, j, b * DA) for b in range(3) for j in range(4)]
    stream += [two(w_out, j, b * 512) for b in range(2) for j in range(4)]
    stream += gate_up(0)
    for c in range(NCH - 1):
        stream += gate_up(c + 1) + down(c)
    stream += down(NCH - 1)

    x_all = np.concatenate([f["x_prompt"].reshape(SEQ, D), f["x_sample"].reshape(NS, D)])
    rows = np.concatenate([np.arange(512, LB), np.array([r for r in range(512) if r % 16 < TS])])
    assert rows.size == CK

    def cache(a):
        return a[0].reshape(NB_S, LB, NPAIR, P)[:, rows]

    def count(d):
        return sum(((d >= 0) & (d <= w) & (d % r == 0)).astype(np.int64) for w, r in ((128, 1), (512, 4), (2048, 16)))

    def log_count(d):
        c = count(d)
        return np.where(c > 0, np.log(np.maximum(c, 1)), -1.0e30).astype(np.float32)

    part = np.arange(P)[:, None]
    new_rows = np.concatenate([rows, np.arange(LB, LB + TS)])[None, :]
    state = f["state_conv"][0].transpose(2, 0, 1).reshape(CT, P, NB_S, PADC)

    def column(a):
        return a[0].reshape(-1, P).T

    return {
        "w_stream": np.stack(stream),
        "xT": x_all.T.reshape(KT, P, TOK),
        "x_all": x_all,
        "kT_c": cache(f["cache_k"]).transpose(2, 0, 3, 1).reshape(NPAIR * NB_S, P, CK),
        "v_c": cache(f["cache_v"]).reshape(NB_S, CKT, P, NPAIR, P).transpose(3, 0, 2, 1, 4).reshape(
            NPAIR * NB_S, P, CKT, P),
        "cache_k": f["cache_k"].reshape(NB_S, LB, DA),
        "cache_v": f["cache_v"].reshape(NB_S, LB, DA),
        "stT": state,
        "g1": column(f["attn_norm_g"]),
        "g2": column(f["ffn_norm_g"]),
        "qkg": np.stack([np.tile(f[k], (P, 1)) for k in ("q_norm_g", "k_norm_g")], axis=1),
        "cw": f["conv_w"][0].T.reshape(CT, P, TAPS).transpose(1, 0, 2).reshape(P, CT * TAPS),
        "cb": column(f["conv_b"]),
        "lg": column(f["conv_ln_g"]),
        "lb": column(f["conv_ln_b"]),
        "ident_d": np.eye(P, dtype=np.float32),
        "mask_p": log_count(part + SEQ - P - np.arange(D)[None, :]),
        "mask_s": log_count(LB + part % TS - new_rows),
    }


OUTPUTS = [("y_p", (SEQ, D)), ("y_s", (NS, D)), ("nk_p", (SEQ, DA)), ("nv_p", (SEQ, DA)),
           ("nc_p", (CT, P, PADC)), ("nk_s", (NB_S, LB + TS, DA)), ("nv_s", (NB_S, LB + TS, DA)),
           ("nc_s", (CT, P, NB_S, PADC))]


def kernel(**inputs):
    import numpy as np
    import concourse.bacc as bacc
    from concourse.bass_utils import run_bass_kernel_spmd as run

    nc = bacc.Bacc("TRN2", target_bir_lowering=False, num_devices=1)
    arrays, args = {}, []
    for name, a in laid_out(inputs).items():
        a = np.ascontiguousarray(a)
        arrays[f"in_{name}"] = a
        args.append(nc.dram_tensor(f"in_{name}", a.shape, mybir.dt.from_np(a.dtype), kind="ExternalInput").ap())
    for name, shape in OUTPUTS:
        args.append(nc.dram_tensor(f"out_{name}", shape, F32, kind="ExternalOutput").ap())
    hymba_layer(nc, *args)
    r = run(nc, [arrays], core_ids=[0]).results[0]
    y_p, y_s, nk_p, nv_p, nc_p, nk_s, nv_s, nc_s = (r[f"out_{name}"] for name, _ in OUTPUTS)
    return (y_p.reshape(1, SEQ, D), y_s.reshape(NB_S, TS, D),
            nk_p.reshape(1, 1, SEQ, H, DH), nv_p.reshape(1, 1, SEQ, H, DH),
            nc_p.reshape(DC, PADC).T.reshape(1, 1, PADC, DC),
            nk_s.reshape(1, NB_S, LB + TS, H, DH), nv_s.reshape(1, NB_S, LB + TS, H, DH),
            nc_s.reshape(DC, NB_S, PADC).transpose(1, 2, 0).reshape(1, NB_S, PADC, DC))
```

```python
from contextlib import ExitStack

import concourse.bass as bass
from concourse import mybir

F32 = mybir.dt.float32
F32R = mybir.dt.float32r
ALU = mybir.AluOpType
ACT = mybir.ActivationFunctionType
AX = mybir.AxisListType
ds = bass.ds

P = 128
D = 1024
KT = D // P
SEQ, NB_S, TS = 1024, 8, 8
NS = NB_S * TS
TOK = SEQ + NS
H, DH = 8, 64
DA = H * DH
DC = D - DA
CT = DC // P
NPAIR = H // 2
TAPS = 31
PADC = TAPS - 1
DFF = 2816
NF = DFF // P
NCH = NF // 2
LB = 1024
CK = 768
CKT = CK // P
SK = CK + TS
PC = 1024
N_PIECES = 2 * CT + 12 + 8 + 6 * NCH
TILES = [t * P for t in range(SEQ // P)] + [TOK - P]
NT = len(TILES)
BLOCKS = [(0, 364), (364, 362), (726, 362)]
SMP = PADC + SEQ
SW = PADC + TS
UW = SMP + NB_S * SW
CVS = NB_S * SW - PADC
RMS_EPS, LN_EPS = 1e-6, 1e-5

LNB = [(0, 512), (512, 512), (SEQ, NS)]
E1_ORDER = [3, 4, 5, 6, 7, 8, 0, 1, 2]
E2_ORDER = list(range(NT - 2)) + [NT - 1, NT - 2]

UNITS = [("s", 0, 0)] + [("p", h, i) for i in range(4) for h in range(2)]
UNITS += [("s", 1, 0)] + [("p", h, i) for i in range(4, 8) for h in range(2)]
NU = len(UNITS)
S_UNITS = [u for u, (kind, _, _) in enumerate(UNITS) if kind == "s"]
VSTEPS = [[0]] + [[u, u + 1] for u in (1, 3, 5, 7)] + [[9]] + [[u, u + 1] for u in (10, 12, 14, 16)]
NV = len(VSTEPS)
V_OF = {u: v for v, us in enumerate(VSTEPS) for u in us}
OGROUPS = [[0], [1, 2, 3, 4], [5], [6, 7, 8, 9]]
NOG = len(OGROUPS)
UT = [i + 1 if kind == "p" else CKT + 1 for kind, _, i in UNITS]
UQ = [sum((t + 3) // 4 for t in UT[:u]) for u in range(NU + 1)]
QK_AT = NU - 2
QK_Q = 6
NQ = UQ[NU] + QK_Q
assert NQ % 2 == 0 and UQ[QK_AT] % 2 == 0 and NU % 3 == 0 and NV % 2 == 0
START = 8
TAPS_STEP = 10
TAP_UNITS = [u for u in range(NU) if u % 9 >= 4]
assert len(TAP_UNITS) == TAPS_STEP
PAIR0_TAPS = 14
TAPS_PRE = TAPS - (NPAIR - 1) * TAPS_STEP
assert TAPS_PRE == 1


def count(per_pair, p, n):
    return p * per_pair + (START + n)


def quads(p, n):
    return p * NQ + (START + QK_Q + n)


def quad_of(u, last):
    return UQ[u] + (QK_Q if u >= QK_AT and not last else 0)


def hymba_layer(nc, w_stream, xT, x_all, kT_c, v_c, cache_k, cache_v, stT, g1, g2, qkg, cw, cb, lg, lb,
                ident_d, mask_p, mask_s, y_p, y_s, nk_p, nv_p, nc_p, nk_s, nv_s, nc_s):
    scr = nc.dram_tensor("qkv_scratch", (3, TOK, DA), F32, kind="Internal").ap()

    with ExitStack() as ctx:
        def const(name, shape, dt=F32):
            return ctx.enter_context(nc.sbuf_tensor(name, shape, dt))

        def sem(name):
            return ctx.enter_context(nc.semaphore(name))

        ident = const("ident", [P, P])
        ones_c = const("ones_c", [P, P])
        zero_c = const("zero_c", [P, 1])
        g1s = const("g1s", [P, KT])
        g2s = const("g2s", [P, KT])
        qkgs = const("qkgs", [P, 2, DH])
        cws = const("cws", [P, CT * TAPS])
        cbs = const("cbs", [P, CT])
        lgs = const("lgs", [P, CT])
        lbs = const("lbs", [P, CT])
        ssx = const("ssx", [P, NT])
        rsx = const("rsx", [P, NT])
        ssh = const("ssh", [P, 2, H])
        rsh = const("rsh", [P, 2, H])
        nmx = const("nmx", [P, 3])
        mxs = const("mxs", [P, 3])
        den = const("den", [P, 3])
        rden = const("rden", [P, 3])

        def place(at, name, shape, dt=F32):
            with ExitStack() as s:
                if at:
                    s.enter_context(nc.sbuf_tensor(f"below_{name}", [P, at // 4], F32))
                return s.enter_context(nc.sbuf_tensor(name, shape, dt))

        def row(name, ats, shape, dt=F32):
            t = place(ats[0], name, shape, dt)
            n = 4
            for d in shape[1:]:
                n *= d
            ats[0] += -(-n // 64) * 64
            return t

        RAW0 = 0
        WS0 = RAW0 + 2 * PC * 4
        WS4 = WS0 + 4 * 2 * PC * 4
        UC0 = WS0 + 8 * 2 * PC * 4
        GAP0 = -(-(UC0 + (CT + 1) * UW * 4) // 64) * 64
        M0 = 139968
        raw = place(RAW0, "raw", [P, 2, PC])
        ws = place(WS0, "ws", [P, 8, 2, PC], F32R)
        uc = place(UC0, "uc", [P, (CT + 1) * UW])
        at = [GAP0]
        xh = row("xh", at, [P, KT, TOK], F32R)
        xl = row("xl", at, [P, KT, TOK], F32R)
        tmp0 = at[0]
        xr = row("xr", at, [P, 4, TOK])
        xn = row("xn", at, [P, 2, D])
        rb = row("rb", at, [P, TOK])
        rbt = row("rbt", at, [P, 2, P])
        at = [tmp0]
        glu_g = row("glu_g", at, [P, 364])
        glu_s = row("glu_s", at, [P, 364])
        glu_a = row("glu_a", at, [P, 364])
        zt = row("zt", at, [P, 2, DA])
        zo = row("zo", at, [P, 2, DA])
        zsq = row("zsq", at, [P, DA])
        at = [WS4]
        tb = row("tb", at, [P, 3, D])
        pt = row("pt", at, [P, 4, D])
        mks = row("mks", at, [P, SK])
        so = row("so", at, [P, P])
        assert at[0] <= UC0
        Y0 = M0 - NT * D * 4
        at = [GAP0]
        qt = row("qt", at, [P, TOK])
        kt_ = row("kt", at, [P, TOK])
        mkp = row("mkp", at, [P, D])
        assert at[0] <= Y0 + 3 * D * 4
        HALF = KT // 2 * TOK * 4
        at = [M0 + HALF]
        skt = row("skt", at, [P, 4, CK])
        vn = row("vn", at, [P, SEQ // P, P])
        qks = row("qks", at, [P, 2, P])
        assert at[0] <= M0 + 2 * HALF
        at = [M0 + 3 * HALF]
        sv = row("sv", at, [P, 4, CKT, P])
        vns = row("vns", at, [P, NB_S, P])
        qb = row("qb", at, [P, NB_S, 32])
        assert at[0] <= M0 + 4 * HALF
        qn, kn = raw[:, 0, :], raw[:, 1, :]
        at = [M0]
        mh = row("mh", at, [P, KT, TOK], F32R)
        ml = row("ml", at, [P, KT, TOK], F32R)
        sq = place(M0 + 3 * HALF, "sq", [P, CT, 512])
        rstd_c = place(-(-(UC0 + CT * UW * 4) // 64) * 64, "rstd_c", [P, TOK])
        ACT0 = WS4 + 2 * 2 * PC * 4
        y = place(Y0, "y", [P, NT, D])
        at = [UC0 + 16384]
        tn = row("tn", at, [P, D])
        hg = row("hg", at, [P, 2, 512])
        assert at[0] <= Y0 + 0
        at = [ACT0]
        ah = row("ah", at, [P, 4, TOK], F32R)
        al = row("al", at, [P, 4, TOK], F32R)
        sg = row("sg", at, [P, 2, 364])
        pr = row("pr", at, [P, 2, 364])
        assert at[0] <= Y0

        ps = ctx.enter_context(nc.psum_tensor("ps", [P, 8 * 512], F32))

        def bank(b, n=512, off=0):
            return ps[:, b * 512 + off:b * 512 + off + n]

        c_in = sem("consts_in")
        x_in = [sem(f"x_in{k}") for k in range(KT)]
        x_hi, x_lo = sem("x_hi"), sem("x_lo")
        xn_in = [sem("xn_in0"), sem("xn_in1")]
        xsq = sem("x_squares")
        ms_x, sd_x, rs_x = sem("x_meansq"), sem("x_rms"), sem("x_rstd")
        rbt_s, rbt_t, rb_s = sem("rstd_wide"), sem("rstd_turned"), sem("rstd_rows")
        raw_in = [sem("raw_in0"), sem("raw_in1")]
        w_hi, w_lo = sem("w_hi"), sem("w_lo")
        mem_s, zero_s = sem("memsets"), sem("zeroed")
        ag_mm, ag_ga, ag_sig, ag_aa, ag_u = (sem("ag_mm"), sem("ag_gate"), sem("ag_sigmoid"), sem("ag_a"),
                                             sem("ag_u"))
        st_in, st_out = sem("state_in"), [sem(f"state_out{c}") for c in range(CT)]
        c_mm, c_z, c_sq, c_ss, c_rt, c_rs, c_n, c_o = (sem("qkv_mm"), sem("qkv_z"), sem("qkv_sq"), sem("qkv_ss"),
                                                 sem("qkv_rms"), sem("qkv_rstd"), sem("qkv_normed"), sem("qkv_out"))
        c_st = [sem("qkv_stored0"), sem("qkv_stored1")]
        d_msk = sem("masks_in")
        d_q, d_v = sem("pair_qk_in"), sem("pair_v_in")
        d_sk = [sem(f"sample_k_in{i}") for i in range(4)]
        d_sv = [sem(f"sample_v_in{i}") for i in range(4)]
        d_tr, d_ev, d_qb = sem("turned"), sem("turned_out"), sem("qb_ready")
        d_s, d_tt, d_mx, d_ex, d_rc, d_sc, d_pv = (
            sem("scores"), sem("scores_masked"), sem("maximum"), sem("exped"), sem("den_recip"), sem("normed"),
            sem("values_summed"))
        d_oh, d_ol, d_oc, d_ot = sem("attn_hi"), sem("attn_lo"), sem("sample_out_copied"), sem("sample_out_turned")
        cv_a, cv_b = sem("conv_prompt"), sem("conv_samples")
        n_mm, n_xc, n_sq, n_vm, n_sd, n_rs, n_nm, n_si, n_hi, n_lo = (sem(f"ln_{x}") for x in (
            "mean", "centred", "squares", "var", "std", "rstd", "normed", "swish", "hi", "lo"))
        y_in = [sem("residual_in0"), sem("residual_in1")]
        e_mm, e_y, e_ss, e_ms, e_sd, e_rs, e_tn, e_tr, e_g, e_hi, e_lo = (sem(f"out_{x}") for x in (
            "mm", "y", "ss", "ms", "sd", "rs", "tn", "turned", "g", "hi", "lo"))
        gu_mm, gu_si, gu_pr, gu_hi, gu_lo = (sem(f"glu_{x}") for x in ("mm", "silu", "prod", "hi", "lo"))
        dn_mm, dn_y = sem("down_mm"), sem("down_y")
        own_wait = sem("own_wait")
        s_out, s_cp = sem("outputs"), sem("cache_copies")

        def hi(slot):
            return ws[:, slot, 0, :]

        def lo(slot):
            return ws[:, slot, 1, :]

        def mm3(e, out, wh, wl, mh_, ml_, first, last):
            e.matmul(out, wh, mh_, start=first, stop=False)
            e.matmul(out, wh, ml_, start=False, stop=False)
            return e.matmul(out, wl, mh_, start=False, stop=last)

        def ustate(c, a, b):
            return uc[:, c * UW + SMP:(c + 1) * UW].rearrange("p (b n) -> p b n", b=NB_S)[:, :, a:b]

        N_B, N_QKV, N_OUT = 2 * CT, 12, 8
        E0 = N_B + N_QKV
        F0 = E0 + N_OUT
        L0 = F0 + 4
        CP_BEFORE = NB_S - 5

        def ln_cols(b, c):
            b0, w = LNB[b]
            return uc[:, c * UW + b0:c * UW + b0 + w] if b < 2 else ustate(c, 0, TS)

        def ln_mean(b):
            return bank(b, LNB[b][1])

        def e_part(t_, t, q):
            r0, skip = (TILES[t], 0) if t < NT - 1 else (SEQ, P - NS)
            return t_[:, 4 * q:4 * q + 4, r0:r0 + P - skip], hg[:, q].rearrange("p (k r) -> p k r", k=4)[:, :, skip:P]

        block = ctx.enter_context(nc.Block())

        @block.sync
        def _(sp):
            def piece(n, k):
                if not isinstance(n, int) or n >= 2:
                    sp.wait_ge(w_lo, n - 1)
                src = w_stream[n] if isinstance(n, int) else w_stream[ds(n, 1)].rearrange("a p c -> (a p) c")
                sp.dma_start(raw[:, k % 2, :], src).then_inc(raw_in[k % 2], 16)

            sp.dma_start(g1s[:], g1).then_inc(c_in, 16)
            for k in range(4):
                sp.dma_start(xr[:, k, :], xT[k]).then_inc(x_in[k], 16)
            piece(0, 0)
            piece(1, 1)
            for k in range(4, KT):
                sp.wait_ge(x_lo, k - 3)
                sp.dma_start(xr[:, k % 4, :], xT[k]).then_inc(x_in[k], 16)
            for dst, src in ((ident[:], ident_d), (g2s[:], g2), (qkgs[:], qkg), (cws[:], cw), (cbs[:], cb),
                             (lgs[:], lg), (lbs[:], lb)):
                sp.dma_start(dst, src).then_inc(c_in, 16)
            for c in range(CT):
                sp.dma_start(ustate(c + 1, 0, PADC), stT[c]).then_inc(st_in, 16)
            for t, r0 in enumerate(TILES):
                if t >= 2:
                    sp.wait_ge(xsq, t - 1)
                sp.dma_start(xn[:, t % 2, :], x_all[r0:r0 + P, :]).then_inc(xn_in[t % 2], 16)
            for n in range(2, N_B + 8):
                piece(n, n)
            def store_block(j):
                for t, r0 in enumerate(TILES):
                    m = j * NT + t
                    sp.wait_ge(c_o if j < 2 else c_z, m + 1)
                    if t < NT - 1:
                        dst, src = scr[j, r0:r0 + P, :], zo[:, m % 2, :]
                    else:
                        dst, src = scr[j, SEQ:TOK, :], zo[P - NS:P, m % 2, :]
                    sp.dma_start(dst, src).then_inc(c_st[m % 2], 16)

            store_block(0)
            for n in range(N_B + 8, N_B + 12):
                piece(n, n)
            store_block(1)
            for n in range(E0, E0 + 4):
                piece(n, n)
            store_block(2)

            sp.wait_ge(c_mm, 3 * NT)
            sp.wait_ge(c_st[0], 16 * 14)
            sp.wait_ge(c_st[1], 16 * 13)
            sp.wait_ge(w_lo, E0 + 4)

            def rows_of(j, cols):
                return scr[j, 0:SEQ, cols].rearrange("(t r) c -> r t c", r=P)

            def load_qk(cols):
                sp.dma_start(qn.rearrange("p (t c) -> p t c", c=P), rows_of(0, cols)).then_inc(d_q, 16)
                sp.dma_start(kn.rearrange("p (t c) -> p t c", c=P), rows_of(1, cols)).then_inc(d_q, 16)
                sp.dma_start(qks[0:NS, 0, :], scr[0, SEQ:TOK, cols]).then_inc(d_q, 16)
                sp.dma_start(qks[0:NS, 1, :], scr[1, SEQ:TOK, cols]).then_inc(d_q, 16)

            def load_v(cols):
                sp.dma_start(vn[:], rows_of(2, cols)).then_inc(d_v, 16)
                sp.dma_start(vns[0:TS, :, :], scr[2, SEQ:TOK, cols].rearrange("(b t) c -> t b c", t=TS)).then_inc(
                    d_v, 16)

            def load_sk(first):
                for b in range(4):
                    sp.dma_start(skt[:, b, :], kT_c[ds(first + b, 1)].rearrange("a p c -> (a p) c")).then_inc(
                        d_sk[b], 16)

            def load_sv(first):
                for b in range(4):
                    sp.dma_start(sv[:, b], v_c[ds(first + b, 1)].rearrange("a p k c -> (a p) k c")).then_inc(
                        d_sv[b], 16)

            def second_samples(p):
                sp.wait_ge(d_s, count(NU, p, 1))
                load_sk(p * NB_S + 4)
                sp.wait_ge(d_pv, count(NV, p, 1))
                load_sv(p * NB_S + 4)

            load_qk(slice(0, P))
            load_sk(0)
            sp.dma_start(mks[:], mask_s).then_inc(d_msk, 16)
            sp.dma_start(mkp[:], mask_p).then_inc(d_msk, 16)
            load_v(slice(0, P))
            load_sv(0)
            sp.dma_start(y[:, 3:NT - 1, :], x_all[3 * P:SEQ, :].rearrange("(t r) c -> r t c", r=P)).then_inc(
                y_in[0], 16)
            sp.dma_start(y[:, NT - 1, :], x_all[TOK - P:TOK, :]).then_inc(y_in[0], 16)
            with sp.Fori(0, NPAIR - 1) as p:
                nxt = ds(p * P + P, P)
                sp.wait_ge(d_tr, quads(p, 0))
                load_qk(nxt)
                second_samples(p)
                sp.wait_ge(d_s, count(NU, p, 10))
                load_sk(p * NB_S + NB_S)
                sp.wait_ge(d_pv, count(NV, p, 6))
                load_sv(p * NB_S + NB_S)
                sp.wait_ge(d_pv, count(NV, p, NV))
                load_v(nxt)
            second_samples(NPAIR - 1)
            for n in range(E0 + 4, E0 + 6):
                piece(n, n)
            sp.wait_ge(d_s, count(NU, NPAIR - 1, NU))
            sp.wait_ge(d_tt, count(NU, NPAIR - 1, NU))
            sp.dma_start(y[:, 0:3, :], x_all[0:3 * P, :].rearrange("(t r) c -> r t c", r=P)).then_inc(y_in[1], 16)
            for n in range(E0 + 6, F0 + 4):
                piece(n, n)
            for j, (dst_p, dst_s) in ((1, (nk_p, nk_s)), (2, (nv_p, nv_s))):
                sp.dma_start(dst_p, scr[j, 0:SEQ, :]).then_inc(s_cp, 16)
                sp.dma_start(dst_s[:, LB:LB + TS, :],
                             scr[j, SEQ:TOK, :].rearrange("(b t) c -> b t c", t=TS)).then_inc(s_cp, 16)
            with sp.Fori(0, (NCH - 1) // 2) as i:
                for k in range(12):
                    piece(i * 12 + (L0 + k), L0 + k)
            for n in range(N_PIECES - 2, N_PIECES):
                piece(n, n)
            for t, r0 in enumerate(TILES):
                sp.wait_ge(dn_y, START + 2 * NT * (NCH - 1) + 2 * (t + 1))
                if t < NT - 1:
                    sp.dma_start(y_p[r0:r0 + P, :], y[:, t, :]).then_inc(s_out, 16)
                else:
                    sp.dma_start(y_s, y[P - NS:P, t, :]).then_inc(s_out, 16)
            sp.wait_ge(s_out, 16 * NT)
            sp.wait_ge(s_cp, 16 * 4 + 16 * 2 * NB_S)
            for c in range(CT):
                sp.wait_ge(st_out[c], 32)

        @block.gpsimd
        def _(pool):
            zeros = zero_c[:, 0:1].broadcast_to([P, PC])
            pool.memset(zero_c[:], 0.0).then_inc(zero_s, 1)
            pool.wait_ge(zero_s, 1)
            pool.memset(ones_c[:], 1.0 / DC).then_inc(mem_s, 1)
            for c in range(CT):
                pool.memset(uc[:, (c + 1) * UW:(c + 1) * UW + PADC], 0.0).then_inc(mem_s, 1)

            def cut(n, k, slot):
                per = n // 2 if isinstance(n, int) else None
                pool.wait_ge(raw_in[k % 2], 16 * (per + 1))
                pool.tensor_tensor(hi(slot), raw[:, k % 2, :], zeros, ALU.add).then_inc(w_hi, 1)
                pool.wait_ge(w_hi, n + 1)
                pool.tensor_tensor(lo(slot), raw[:, k % 2, :], hi(slot).bitcast(F32), ALU.subtract).then_inc(w_lo, 1)

            for n in range(N_B):
                if n >= 4:
                    pool.wait_ge(ag_mm, 3 * (n // 2 - 1))
                cut(n, n, n % 4)
            def gain(m):
                pool.wait_ge(c_n, 2 * m + 2)
                z3 = zo[:, m % 2, :].rearrange("p (h d) -> p h d", d=DH)
                pool.tensor_tensor(z3, z3, qkgs[:, m // NT, :].unsqueeze(1).broadcast_to([P, H, DH]),
                                   ALU.mult).then_inc(c_o, 1)

            pool.wait_ge(rb_s, 4)
            for j in range(3):
                if j == 1:
                    pool.wait_ge(ag_mm, 3 * CT)
                if j == 2:
                    pool.wait_ge(c_mm, NT)
                for m in range(4):
                    n = N_B + 4 * j + m
                    cut(n, n, m + (0 if j == 1 else 4))
                    if j:
                        gain(NT * (j - 1) + m)
                if j:
                    for t in range(4, NT):
                        gain(NT * (j - 1) + t)
            pool.wait_ge(c_mm, 2 * NT)
            for m in range(4):
                cut(E0 + m, E0 + m, m)
            pool.wait_ge(d_pv, count(NV, NPAIR - 1, NV))
            for m in range(4):
                cut(E0 + 4 + m, E0 + 4 + m, 4 + m)
            pool.wait_ge(e_mm, 2 * NT)
            for m in range(4):
                cut(F0 + m, F0 + m, m)
            with pool.Fori(0, (NCH - 1) // 2) as i:
                for half in range(2):
                    for m in range(6):
                        k = L0 + 6 * half + m
                        if m == 0:
                            pool.wait_ge(gu_mm, i * 12 + (6 * half + 3))
                        if m == 2:
                            pool.wait_ge(gu_mm, i * 12 + (6 * half + 6))
                        if m == 4:
                            if half == 0:
                                pool.wait_ge(e_mm, 4 * NT)
                            pool.wait_ge(dn_mm, i * (4 * NT) + (START + 2 * NT * half))
                        pool.wait_ge(raw_in[k % 2], i * (16 * 6) + 16 * (k // 2 + 1))
                        slot = m
                        pool.tensor_tensor(hi(slot), raw[:, k % 2, :], zeros, ALU.add).then_inc(w_hi, 1)
                        pool.wait_ge(w_hi, i * 12 + (k + 1))
                        pool.tensor_tensor(lo(slot), raw[:, k % 2, :], hi(slot).bitcast(F32),
                                           ALU.subtract).then_inc(w_lo, 1)
            pool.wait_ge(gu_mm, 6 * NCH)
            for m in range(2):
                n = N_PIECES - 2 + m
                cut(n, n, m)

        @block.tensor
        def _(pe):
            for s in (d_s, d_pv, d_tr, dn_mm):
                pe.sem_inc(s, START)
            def ag(c, g, side, k):
                b0, bn = BLOCKS[g % 3]
                slot = (2 * c + side) % 4
                return mm3(pe, bank(2 * (g % 3) + side, bn), hi(slot)[:, k * P:(k + 1) * P],
                           lo(slot)[:, k * P:(k + 1) * P], xh[:, k, b0:b0 + bn], xl[:, k, b0:b0 + bn],
                           k == 0, k == KT - 1)

            pe.wait_ge(w_lo, 2)
            for k in range(KT):
                pe.wait_ge(x_lo, k + 1)
                for g in range(3):
                    for side in range(2):
                        last = ag(0, g, side, k)
                    if k == KT - 1:
                        last.then_inc(ag_mm, 1)
            pe.wait_ge(c_in, 16 * 8)
            for t in range(NT):
                pe.wait_ge(rbt_s, t + 1)
                if t == 8:
                    pe.wait_ge(rb_s, 1)
                pe.transpose(bank(6 + t // 4 % 2, P, (t % 4) * P), rbt[:, t % 2, :], ident[:]).then_inc(rbt_t, 1)
            for c in range(1, CT):
                pe.wait_ge(w_lo, 2 * (c + 1))
                for g in range(3 * c, 3 * c + 3):
                    pe.wait_ge(ag_aa, g - 2)
                    for side in range(2):
                        for k in range(KT):
                            last = ag(c, g, side, k)
                    last.then_inc(ag_mm, 1)
            m = 0
            for j in range(3):
                pe.wait_ge(w_lo, N_B + 4 * (j + 1))
                s0 = 0 if j == 1 else 4
                for t, r0 in enumerate(TILES):
                    if m == 0:
                        pe.wait_ge(rb_s, 3)
                        pe.wait_ge(ag_aa, 3 * CT)
                    if m >= 4:
                        pe.wait_ge(c_z, m - 3)
                    for k in range(KT):
                        wcol = slice((k % 2) * DA, (k % 2 + 1) * DA)
                        last = mm3(pe, bank(4 + m % 4), xh[:, k, r0:r0 + P], xl[:, k, r0:r0 + P],
                                   hi(s0 + k // 2)[:, wcol], lo(s0 + k // 2)[:, wcol], k == 0, k == KT - 1)
                    last.then_inc(c_mm, 1)
                    m += 1
            pe.wait_ge(c_z, 3 * NT)

            def quad_wait(p, q):
                pe.wait_ge(d_ev, quads(p, q - 1))

            def turn_qk(p, q0):
                for q, (src, t0) in enumerate(((qn, 0), (qn, 4), (kn, 0), (kn, 4))):
                    quad_wait(p, q0 + q)
                    for t in range(4):
                        last = pe.transpose(bank(4 + q % 2, P, t * P), src[:, (t0 + t) * P:(t0 + t + 1) * P], ident[:])
                    last.then_inc(d_tr, 1)
                for q in (4, 5):
                    quad_wait(p, q0 + q)
                    pe.sem_inc(own_wait, 1)
                    pe.transpose(bank(4 + q % 2, NS), qks[0:NS, q - 4, :], ident[0:NS, 0:NS]).then_inc(d_tr, 1)

            def scores(p, u, first_pair=False):
                kind, h, i = UNITS[u]
                pe.wait_ge(d_tt, count(NU, p, u - 1))
                s = 2 * (u % 2)
                if kind == "p":
                    rows = slice(DH * h, DH * h + DH)
                    n = (i + 1) * P
                    for c0 in range(0, n, 512):
                        cn = min(512, n - c0)
                        last = pe.matmul(bank(s + c0 // 512, cn), qt[rows, i * P:(i + 1) * P],
                                         kt_[rows, c0:c0 + cn], start=True, stop=True)
                else:
                    if h == 0:
                        pe.wait_ge(d_ev, quads(p, 0 if first_pair else UQ[QK_AT] + QK_Q - NQ))
                        pe.wait_ge(d_qb, p + 1)
                    for k0, k1 in ((0, 512), (512, CK), (CK, SK)):
                        for bb in range(4):
                            b = 4 * h + bb
                            if k0 == 0:
                                pe.wait_ge(d_sk[bb], p * 32 + 16 * (h + 1))
                            keys = kt_[:, SEQ + TS * b:SEQ + TS * (b + 1)] if k0 == CK else skt[:, bb, k0:k1]
                            last = pe.matmul(ps[32 * bb:32 * bb + 32, s * 512 + k0:s * 512 + k1], qb[:, b, :], keys,
                                             start=True, stop=True)
                last.then_inc(d_s, 1)

            def turn(p, u, last_pair):
                pe.wait_ge(d_sc, p * NU + (u + 1))
                q = quad_of(u, last_pair)
                for c in range(UT[u]):
                    if c % 4 == 0:
                        quad_wait(p, q + c // 4)
                    w = P if UNITS[u][0] == "p" or c < CKT else TS
                    last = pe.transpose(bank(4 + (q + c // 4) % 2, P, (c % 4) * P)[0:w, :],
                                        tb[:, u % 3, c * P:c * P + w], ident[:])
                    if c % 4 == 3 or c == UT[u] - 1:
                        last.then_inc(d_tr, 1)

            def values(p, v, last_pair):
                us = VSTEPS[v]
                kind, h, i = UNITS[us[0]]
                end = us[-1]
                pe.wait_ge(d_ev, quads(p, quad_of(end, last_pair) + (UT[end] + 3) // 4))
                og = next(g for g, vs in enumerate(OGROUPS) if v in vs)
                if v == OGROUPS[og][0]:
                    pe.wait_ge(d_ol, count(NOG, p, og - 1))
                if v == 0:
                    pe.wait_ge(d_v, p * 32 + 32)
                ob = 6 + og % 2
                if kind == "p":
                    for c in range(i + 1):
                        for h in range(2):
                            last = pe.matmul(bank(ob, P, (i % 4) * P)[DH * h:DH * h + DH, :],
                                             vn[:, c, DH * h:DH * h + DH],
                                             pt[:, 2 * (v % 2) + h, c * P:(c + 1) * P],
                                             start=(c == 0), stop=(c == i))
                else:
                    for c in range(CKT + 1):
                        for bb in range(4):
                            b = 4 * h + bb
                            if c == 0:
                                pe.wait_ge(d_sv[bb], p * 32 + 16 * (h + 1))
                            r = slice(0, P) if c < CKT else slice(0, TS)
                            vals = sv[:, bb, c, :] if c < CKT else vns[0:TS, b, :]
                            last = pe.matmul(bank(ob, P)[32 * bb:32 * bb + 32, :],
                                             pt[r, 2 * (v % 2), c * P + 32 * bb:c * P + 32 * bb + 32], vals,
                                             start=(c == 0), stop=(c == CKT))
                last.then_inc(d_pv, 1)

            def turn_outputs(p, h):
                pe.wait_ge(d_oc, p * 2 + (h + 1))
                pe.transpose(bank(6, P, P), so[:], ident[:]).then_inc(d_ot, 1)

            def pair(p, last_pair):
                for u in range(NU):
                    if u + 2 < NU:
                        scores(p, u + 2)
                    elif u == NU - 1 and not last_pair:
                        scores(p + 1, 1)
                    if u == QK_AT and not last_pair:
                        pe.wait_ge(d_q, p * 64 + 128)
                        turn_qk(p, UQ[QK_AT])
                    turn(p, u, last_pair)
                    for v in range(NV):
                        if VSTEPS[v][-1] == u - 1:
                            values(p, v, last_pair)
                    for h in range(2):
                        if u == S_UNITS[h] + 3:
                            turn_outputs(p, h)
                    if u == QK_AT and not last_pair:
                        scores(p + 1, 0)
                values(p, NV - 1, last_pair)

            pe.wait_ge(d_q, 64)
            turn_qk(0, -QK_Q)
            scores(0, 0, True)
            scores(0, 1, True)
            with pe.Fori(0, NPAIR - 1) as p:
                pair(p, False)
            pair(NPAIR - 1, True)

            def project(rh, n, t):
                for nh in range(2):
                    m = 2 * NT * rh + 2 * n + nh
                    if m >= 4:
                        pe.wait_ge(e_y, m - 3)
                    r0 = TILES[t]
                    for k in range(4):
                        wcol = slice(nh * 512, (nh + 1) * 512)
                        kk = 4 * rh + k
                        last = mm3(pe, bank(4 + m % 4), mh[:, kk, r0:r0 + P], ml[:, kk, r0:r0 + P],
                                   hi(kk)[:, wcol], lo(kk)[:, wcol], k == 0, k == 3)
                    last.then_inc(e_mm, 1)

            pe.wait_ge(cv_a, START + TAPS * CT)
            pe.wait_ge(cv_b, START + TAPS * CT)
            pe.wait_ge(mem_s, 1)
            pe.wait_ge(d_tt, count(NU, NPAIR - 1, NU))
            for b in range(3):
                for c in range(CT):
                    last = pe.matmul(ln_mean(b), ones_c[:], ln_cols(b, c), start=(c == 0), stop=(c == CT - 1))
                last.then_inc(n_mm, 1)
            pe.wait_ge(d_ol, count(NOG, NPAIR - 1, NOG))
            pe.wait_ge(d_ev, START + QK_Q + NQ * NPAIR - QK_Q)
            pe.wait_ge(w_lo, E0 + 4)
            for n, t in enumerate(E1_ORDER):
                project(0, n, t)
                if 1 <= n <= 3:
                    b = n - 1
                    pe.wait_ge(n_sq, CT * (b + 1))
                    for c in range(CT):
                        last = pe.matmul(ln_mean(b), ones_c[:], sq[:, c, 0:LNB[b][1]], start=(c == 0),
                                         stop=(c == CT - 1))
                    last.then_inc(n_vm, 1)

            def turn_back(n):
                pe.wait_ge(e_tn, n + 1)
                for q in range(2):
                    tq = 2 * n + q
                    if tq >= 4:
                        pe.wait_ge(e_g, tq - 3)
                    for c in range(4):
                        last = pe.transpose(bank(tq % 4, P, c * P), tn[:, (4 * q + c) * P:(4 * q + c + 1) * P], ident[:])
                    last.then_inc(e_tr, 1)

            pe.wait_ge(n_lo, 3 * CT)
            pe.wait_ge(w_lo, E0 + 8)
            for n, t in enumerate(E2_ORDER):
                project(1, n, t)
                if n >= 1:
                    turn_back(n - 1)
            turn_back(NT - 1)

            def gate_up(c6, cslot, i=None):
                base = 0 if i is None else i * 12
                for f in range(2):
                    npc = (F0 + 4 if i is None else i * 12 + (L0 + cslot * 6 + 4))
                    pe.wait_ge(w_lo, npc - 2 * (1 - f))
                    for b, (b0, bn) in enumerate(BLOCKS):
                        k6 = c6 + 3 * f + b
                        if k6 >= 2:
                            pe.wait_ge(gu_pr, base + (k6 - 1))
                        for side in range(2):
                            out = bank(2 * (k6 % 2) + side, bn)
                            slot = 2 * f + side
                            for k in range(KT):
                                last = mm3(pe, out, hi(slot)[:, k * P:(k + 1) * P], lo(slot)[:, k * P:(k + 1) * P],
                                           mh[:, k, b0:b0 + bn], ml[:, k, b0:b0 + bn], k == 0, k == KT - 1)
                        last.then_inc(gu_mm, 1)

            def down(half, i=None):
                base_m = START if i is None else i * (4 * NT) + START
                const_m = 2 * NT * half if i is not None else 2 * NT * (NCH - 1)
                wd = 4 if i is not None else 0
                if i is None:
                    pe.wait_ge(w_lo, N_PIECES)
                    pe.wait_ge(gu_lo, 6 * NCH)
                else:
                    pe.wait_ge(w_lo, i * 12 + (L0 + 6 * half + 6))
                    pe.wait_ge(gu_lo, i * 12 + 6 * (half + 1))
                a0 = 2 * half
                for t, r0 in enumerate(TILES):
                    for nh in range(2):
                        m = 2 * t + nh
                        pe.wait_ge(dn_y, base_m + (const_m + m - 3))
                        for f in range(2):
                            last = mm3(pe, bank(4 + (const_m + m) % 4), ah[:, a0 + f, r0:r0 + P],
                                       al[:, a0 + f, r0:r0 + P], hi(wd + f)[:, nh * 512:(nh + 1) * 512],
                                       lo(wd + f)[:, nh * 512:(nh + 1) * 512], f == 0, f == 1)
                        last.then_inc(dn_mm, 1)

            pe.wait_ge(e_lo, 2 * NT)
            gate_up(0, 0)
            with pe.Fori(0, (NCH - 1) // 2) as i:
                gate_up(6, 0, i)
                down(0, i)
                gate_up(12, 1, i)
                down(1, i)
            down(0)

        @block.scalar
        def _(act):
            for s in (d_ev, d_ex):
                act.sem_inc(s, START)
            act.wait_ge(c_in, 16)
            for k in range(KT):
                act.wait_ge(x_in[k], 16)
                act.activation(xh[:, k, :], xr[:, k % 4, :], ACT.Copy, scale=g1s[:, k:k + 1]).then_inc(x_hi, 1)
            for t in range(NT):
                act.wait_ge(xn_in[t % 2], 16 * (t // 2 + 1))
                act.activation(xn[:, t % 2, :], xn[:, t % 2, :], ACT.Square, accum_out=ssx[:, t:t + 1]).then_inc(xsq, 1)
            act.wait_ge(ms_x, 1)
            act.activation(rsx[:], ssx[:], ACT.Sqrt).then_inc(sd_x, 1)
            def store_state(c):
                act.wait_ge(ag_u, 4 * (c + 1))
                act.wait_ge(st_in, 16 * CT)
                act.dma_start(nc_p[c], uc[:, (c + 1) * UW + SEQ:(c + 1) * UW + SEQ + PADC]).then_inc(st_out[c], 16)
                act.dma_start(nc_s[c], ustate(c + 1, TS, SW)).then_inc(st_out[c], 16)

            for g in range(3 * CT):
                bn = BLOCKS[g % 3][1]
                act.wait_ge(ag_ga, g + 1)
                if g >= 1:
                    act.wait_ge(ag_u, 4 * (g // 3) + (g % 3))
                act.activation(glu_s[:, 0:bn], glu_g[:, 0:bn], ACT.Sigmoid).then_inc(ag_sig, 1)
                if g % 3 == 0 and g >= 3:
                    store_state(g // 3 - 1)
            store_state(CT - 1)
            act.wait_ge(rs_x, 1)
            for m in range(3 * NT):
                j, t = divmod(m, NT)
                act.wait_ge(c_mm, m + 1)
                if j == 2:
                    act.wait_ge(c_st[m % 2], 16 * (m // 2))
                    act.activation(zo[:, m % 2, :], bank(4 + m % 4), ACT.Copy, scale=rsx[:, t:t + 1]).then_inc(c_z, 1)
                    continue
                if m >= 2:
                    act.wait_ge(c_n, 2 * (m - 1))
                act.activation(zt[:, m % 2, :], bank(4 + m % 4), ACT.Copy, scale=rsx[:, t:t + 1]).then_inc(c_z, 1)
                act.wait_ge(c_z, m + 1)
                if m >= 1:
                    act.wait_ge(c_ss, m)
                act.activation(zsq[:], zt[:, m % 2, :], ACT.Square).then_inc(c_sq, 1)
                act.wait_ge(c_ss, m + 1)
                act.activation(rsh[:, m % 2, :], ssh[:, m % 2, :], ACT.Sqrt).then_inc(c_rt, 1)
            def copy_quad(p, q, dst, src):
                act.wait_ge(d_tr, quads(p, q + 1))
                act.activation(dst, src, ACT.Copy).then_inc(d_ev, 1)

            def copy_qk(p, q0):
                for q in range(4):
                    dst = (qt, kt_)[q // 2]
                    copy_quad(p, q0 + q, dst[:, (q % 2) * 512:(q % 2 + 1) * 512], bank(4 + q % 2))
                for q in (4, 5):
                    dst = (qt, kt_)[q - 4]
                    copy_quad(p, q0 + q, dst[:, SEQ:TOK], bank(4 + q % 2, NS))

            def exps(p, u):
                n = UT[u] * P if UNITS[u][0] == "p" else SK
                r = slice(u % 3, u % 3 + 1)
                act.wait_ge(d_mx, p * NU + (u + 1))
                act.activation(tb[:, u % 3, 0:n], tb[:, u % 3, 0:n], ACT.Exp, bias=nmx[:, r],
                               accum_out=den[:, r]).then_inc(d_ex, 1)

            def copy_probs(p, u, last_pair):
                v, q = V_OF[u], quad_of(u, last_pair)
                kind, h, _ = UNITS[u]
                buf = 2 * (v % 2) + (h if kind == "p" else 0)
                act.wait_ge(d_pv, count(NV, p, v - 1))
                for c0 in range(0, UT[u], 4):
                    cn = min(4, UT[u] - c0)
                    qq = q + c0 // 4
                    b = 4 + qq % 2
                    if kind == "s" and c0 == 4:
                        act.wait_ge(d_tr, quads(p, qq + 1))
                        act.activation(pt[:, buf, 512:CK], bank(b, CK - 512), ACT.Copy)
                        act.activation(pt[0:TS, buf, CK:CK + P], bank(b, P, CK - 512)[0:TS, :],
                                       ACT.Copy).then_inc(d_ev, 1)
                    else:
                        copy_quad(p, qq, pt[:, buf, c0 * P:(c0 + cn) * P], bank(b, cn * P))

            def pair(p, last_pair):
                for u in range(NU):
                    if u == QK_AT and not last_pair:
                        act.wait_ge(d_s, count(NU, p, NU))
                        copy_qk(p, UQ[QK_AT])
                    copy_probs(p, u, last_pair)
                    if u + 2 < NU:
                        exps(p, u + 2)
                    elif not last_pair:
                        exps(p + 1, u + 2 - NU)

            copy_qk(0, -QK_Q)
            exps(0, 0)
            exps(0, 1)
            with act.Fori(0, NPAIR - 1) as p:
                pair(p, False)
            pair(NPAIR - 1, True)
            for b, (b0, w) in enumerate(LNB):
                for c in range(CT):
                    act.wait_ge(n_xc, CT * b + c + 1)
                    if b >= 1:
                        act.wait_ge(n_vm, b)
                    o = sq[:, c, 0:w]
                    if b == 2:
                        o = o.rearrange("p (b t) -> p b t", t=TS)
                    act.activation(o, ln_cols(b, c), ACT.Square).then_inc(n_sq, 1)
            for b, (b0, w) in enumerate(LNB):
                act.wait_ge(n_rs, b + 1)
                act.activation(rstd_c[:, b0:b0 + w], rstd_c[:, b0:b0 + w], ACT.Sqrt).then_inc(n_sd, 1)
            for s in range(3 * CT):
                b, c = divmod(s, CT)
                b0, w = LNB[b]
                v = ln_cols(b, c)
                act.wait_ge(n_nm, s + 1)
                act.activation(v, v, ACT.Silu, scale=lgs[:, c:c + 1], bias=lbs[:, c:c + 1]).then_inc(n_si, 1)
                act.wait_ge(n_si, s + 1)
                m_ = mh[:, CT + c, b0:b0 + w]
                if b == 2:
                    m_ = m_.rearrange("p (b t) -> p b t", t=TS)
                act.activation(m_, v, ACT.Copy).then_inc(n_hi, 1)
            def hi_back(n):
                for q in range(2):
                    act.wait_ge(e_g, 2 * n + q + 1)
                    dst, src = e_part(mh, E2_ORDER[n], q)
                    act.activation(dst, src, ACT.Copy).then_inc(e_hi, 1)

            for n, t in enumerate(E2_ORDER):
                act.wait_ge(e_y, 2 * NT + 2 * (n + 1))
                if n >= 1:
                    act.wait_ge(e_tr, 2 * n)
                act.activation(tn[:], y[:, t, :], ACT.Square, accum_out=ssx[:, n:n + 1]).then_inc(e_ss, 1)
                act.wait_ge(e_ms, n + 1)
                act.activation(rsx[:, n:n + 1], ssx[:, n:n + 1], ACT.Sqrt).then_inc(e_sd, 1)
                if n >= 1:
                    hi_back(n - 1)
            hi_back(NT - 1)
            for b in range(CP_BEFORE):
                act.dma_start(nk_s[5 + b, 0:LB, :], cache_k[5 + b]).then_inc(s_cp, 16)
                act.dma_start(nv_s[5 + b, 0:LB, :], cache_v[5 + b]).then_inc(s_cp, 16)

            def silus(c6, cslot, i=None):
                base = 0 if i is None else i * 12
                for f in range(2):
                    for b, (b0, bn) in enumerate(BLOCKS):
                        k6 = c6 + 3 * f + b
                        act.wait_ge(gu_mm, base + (k6 + 1))
                        if k6 >= 2:
                            act.wait_ge(gu_pr, base + (k6 - 1))
                        act.activation(sg[:, k6 % 2, 0:bn], bank(2 * (k6 % 2), bn), ACT.Silu).then_inc(gu_si, 1)
                        act.wait_ge(gu_pr, base + (k6 + 1))
                        if f == 0 and b == 0 and i is not None:
                            act.wait_ge(dn_mm, i * (4 * NT) + (START + (0 if c6 == 6 else 2 * NT)))
                        act.activation(ah[:, 2 * cslot + f, b0:b0 + bn], pr[:, k6 % 2, 0:bn], ACT.Copy).then_inc(
                            gu_hi, 1)

            silus(0, 0)
            with act.Fori(0, (NCH - 1) // 2) as i:
                act.dma_start(nk_s[ds(i, 1), 0:LB, :], cache_k[ds(i, 1)]).then_inc(s_cp, 16)
                act.dma_start(nv_s[ds(i, 1), 0:LB, :], cache_v[ds(i, 1)]).then_inc(s_cp, 16)
                silus(6, 1, i)
                silus(12, 0, i)

        @block.vector
        def _(dve):
            for s in (d_tt, d_rc, d_ol, cv_a, cv_b, dn_y):
                dve.sem_inc(s, START)

            def taps(c, j, n, tap, skip):
                for s, off, w in ((cv_a, 0, SEQ), (cv_b, SMP, CVS)):
                    dst = uc[:, c * UW + off:c * UW + off + w]
                    src = uc[:, ds((c + 1) * UW + off + skip, w)]
                    dve.wait_ge(s, START + n)
                    if not isinstance(j, int) or j > 0:
                        dve.scalar_tensor_tensor(out=dst, in0=src, scalar=cws[:, ds(tap, 1)], in1=dst, op0=ALU.mult,
                                                 op1=ALU.add).then_inc(s, 1)
                    else:
                        dve.tensor_scalar(dst, src, cws[:, ds(tap, 1)], cbs[:, c:c + 1], ALU.mult,
                                          ALU.add).then_inc(s, 1)

            todo = [(c, j) for c in range(CT) for j in range(TAPS)][:TAPS * (CT - 1) + TAPS_PRE]

            def conv(k):
                for _ in range(k):
                    if todo:
                        c, j = todo.pop(0)
                        if j == 0 and c == 0:
                            dve.wait_ge(c_in, 16 * 8)
                            dve.wait_ge(st_in, 16 * CT)
                        if j == 0 and c >= 1:
                            dve.wait_ge(st_out[c - 1], 32)
                        taps(c, j, TAPS * c + j, TAPS * c + j, j)

            for k in range(KT):
                dve.wait_ge(x_hi, k + 1)
                dve.scalar_tensor_tensor(out=xl[:, k, :], in0=xr[:, k % 4, :], scalar=g1s[:, k:k + 1],
                                         in1=xh[:, k, :].bitcast(F32), op0=ALU.mult, op1=ALU.subtract).then_inc(x_lo, 1)
            dve.wait_ge(xsq, NT)
            dve.tensor_scalar(ssx[:], ssx[:], 1.0 / D, RMS_EPS, ALU.mult, ALU.add).then_inc(ms_x, 1)
            dve.wait_ge(sd_x, 1)
            dve.reciprocal(rsx[:], rsx[:]).then_inc(rs_x, 1)
            dve.wait_ge(rs_x, 1)
            dve.wait_ge(mem_s, 1)
            for t in range(NT):
                if t >= 2:
                    dve.wait_ge(rbt_t, t - 1)
                dve.tensor_scalar(rbt[:, t % 2, :], ones_c[:], float(DC), rsx[:, t:t + 1], ALU.mult,
                                  ALU.mult).then_inc(rbt_s, 1)
            dve.wait_ge(rbt_t, NT - 1)
            for q in range(2):
                dve.tensor_copy(rb[:, q * 512:(q + 1) * 512], bank(6 + q)).then_inc(rb_s, 1)
            dve.wait_ge(rbt_t, NT)
            dve.tensor_copy(rb[:, SEQ:TOK], bank(6, NS, P - NS)).then_inc(rb_s, 1)
            dve.wait_ge(c_in, 16 * 8)
            dve.tensor_scalar(qkgs[:, 0, :], qkgs[:, 0, :], DH ** -0.5, None, ALU.mult).then_inc(rb_s, 1)
            dve.wait_ge(rb_s, 4)
            nu = 0
            for g in range(3 * CT):
                c, (b0, bn) = g // 3, BLOCKS[g % 3]
                r = rb[:, b0:b0 + bn]
                dve.wait_ge(ag_mm, g + 1)
                if g >= 1:
                    dve.wait_ge(ag_sig, g)
                dve.tensor_tensor(glu_g[:, 0:bn], bank(2 * (g % 3) + 1, bn), r, ALU.mult).then_inc(ag_ga, 1)
                if g >= 1:
                    dve.wait_ge(ag_u, nu)
                dve.tensor_tensor(glu_a[:, 0:bn], bank(2 * (g % 3), bn), r, ALU.mult).then_inc(ag_aa, 1)
                dve.wait_ge(ag_sig, g + 1)
                dve.wait_ge(ag_aa, g + 1)
                if g == 0:
                    dve.wait_ge(mem_s, 1 + CT)
                n = min(bn, SEQ - b0)
                u0 = (c + 1) * UW + PADC + b0
                dve.tensor_tensor(uc[:, u0:u0 + n], glu_a[:, 0:n], glu_s[:, 0:n], ALU.mult).then_inc(ag_u, 1)
                nu += 1
                if n < bn:
                    def by_sample(a):
                        return a[:, n:bn].rearrange("p (b t) -> p b t", t=TS)
                    dve.tensor_tensor(ustate(c + 1, PADC, SW), by_sample(glu_a), by_sample(glu_s),
                                      ALU.mult).then_inc(ag_u, 1)
                    nu += 1
                if g >= 3:
                    conv(3)
            for m in range(3 * NT):
                j = m // NT
                if j == 2:
                    dve.wait_ge(c_z, m + 1)
                    conv(2)
                    continue
                dve.wait_ge(c_sq, m + 1)
                dve.tensor_reduce(ssh[:, m % 2, :], zsq[:].rearrange("p (h d) -> p h d", d=DH), AX.X,
                                  ALU.add).then_inc(c_n, 1)
                dve.wait_ge(c_n, 2 * m + 1)
                dve.tensor_scalar(ssh[:, m % 2, :], ssh[:, m % 2, :], 1.0 / DH, RMS_EPS, ALU.mult, ALU.add).then_inc(
                    c_ss, 1)
                dve.wait_ge(c_rt, m + 1)
                dve.reciprocal(rsh[:, m % 2, :], rsh[:, m % 2, :]).then_inc(c_rs, 1)
                dve.wait_ge(c_rs, m + 1)
                z3 = zt[:, m % 2, :].rearrange("p (h d) -> p h d", d=DH)
                if m >= 2:
                    dve.wait_ge(c_st[m % 2], 16 * (m // 2))
                dve.tensor_tensor(zo[:, m % 2, :].rearrange("p (h d) -> p h d", d=DH), z3,
                                  rsh[:, m % 2, :].unsqueeze(2).broadcast_to([P, H, DH]), ALU.mult).then_inc(c_n, 1)
                conv(2)
            conv(len(todo) - PAIR0_TAPS)
            dve.wait_ge(c_mm, 3 * NT)
            dve.memset(qb[:], 0.0).then_inc(mem_s, 1)
            dve.wait_ge(mem_s, 2 + CT)
            dve.wait_ge(d_msk, 32)

            def mask_max(p, u):
                kind, h, i = UNITS[u]
                n = UT[u] * P if kind == "p" else SK
                mask = mkp[:, D - n:D] if kind == "p" else mks[:]
                r = slice(u % 3, u % 3 + 1)
                dve.wait_ge(d_s, count(NU, p, u + 1))
                end = UQ[u - 2] if u >= 3 else quad_of(u + NU - 3, False) + (UT[u + NU - 3] + 3) // 4 - NQ
                dve.wait_ge(d_tr, quads(p, end))
                dve.sem_inc(own_wait, 1)
                s = 2 * (u % 2) * 512
                dve.tensor_tensor_reduce(out=tb[:, u % 3, 0:n], in0=ps[:, s:s + n], in1=mask, scale=1.0,
                                         scalar=-3.0e38, op0=ALU.add, op1=ALU.max,
                                         accum_out=mxs[:, r]).then_inc(d_tt, 1)
                dve.wait_ge(d_tt, count(NU, p, u + 1))
                dve.tensor_scalar(nmx[:, r], mxs[:, r], -1.0, None, ALU.mult).then_inc(d_mx, 1)

            def norm(p, u):
                n = UT[u] * P if UNITS[u][0] == "p" else SK
                r = slice(u % 3, u % 3 + 1)
                dve.wait_ge(d_ex, count(NU, p, u + 1))
                dve.reciprocal(rden[:, r], den[:, r]).then_inc(d_rc, 1)
                dve.wait_ge(d_rc, count(NU, p, u + 1))
                dve.tensor_scalar(tb[:, u % 3, 0:n], tb[:, u % 3, 0:n], rden[:, r], None, ALU.mult).then_inc(d_sc, 1)

            def outputs(p, og):
                vs = OGROUPS[og]
                kind, h, i = UNITS[VSTEPS[vs[0]][0]]
                dve.wait_ge(d_pv, count(NV, p, vs[-1] + 1))
                if kind == "p":
                    parts = [(slice(0, P), i * P, 512, bank(6 + og % 2))]
                else:
                    dve.wait_ge(d_ot, p * 2 + (h + 1))
                    o = bank(6, P, P).rearrange("p (b c) -> p b c", c=32)
                    parts = [(slice(DH * hh, DH * hh + DH), SEQ + 4 * TS * h, 4 * TS,
                              o[DH * hh:DH * hh + DH, :, TS * hh:TS * hh + TS]) for hh in range(2)]

                def part(t_, r, c0, w):
                    v = t_[r, ds(p, 1), c0:c0 + w].rearrange("p a c -> p (a c)")
                    return v if kind == "p" else v.rearrange("p (b c) -> p b c", c=TS)

                for r, c0, w, o in parts:
                    last = dve.tensor_copy(part(mh, r, c0, w), o)
                last.then_inc(d_oh, 1)
                dve.wait_ge(d_oh, p * NOG + (og + 1))
                for r, c0, w, o in parts:
                    last = dve.tensor_tensor(part(ml, r, c0, w), o, part(mh, r, c0, w).bitcast(F32), ALU.subtract)
                last.then_inc(d_ol, 1)

            def copy_samples(p, h):
                dve.wait_ge(d_pv, count(NV, p, V_OF[S_UNITS[h]] + 1))
                dve.tensor_copy(so[:], bank(6, P)).then_inc(d_oc, 1)

            def fill_qb(p, q0):
                dve.wait_ge(d_ev, quads(p, q0 + QK_Q))
                for h in range(2):
                    rows = slice(DH * h, DH * h + DH)
                    last = dve.tensor_copy(qb[rows, :, TS * h:TS * (h + 1)],
                                           qt[rows, SEQ:TOK].rearrange("p (b t) -> p b t", t=TS))
                last.then_inc(d_qb, 1)

            def pair(p, first_pair, last_pair):
                for u in range(NU):
                    if u + 1 < NU:
                        norm(p, u + 1)
                    elif not last_pair:
                        norm(p + 1, 0)
                    if u == QK_AT and not last_pair:
                        fill_qb(p, UQ[QK_AT])
                    if u + 2 < NU:
                        mask_max(p, u + 2)
                    elif not last_pair:
                        mask_max(p + 1, u + 2 - NU)
                    if u == 0 and not first_pair:
                        outputs(p - 1, NOG - 1)
                    for h in range(2):
                        if u == S_UNITS[h] + 2:
                            copy_samples(p, h)
                    for og in range(NOG - 1):
                        if VSTEPS[OGROUPS[og][-1]][-1] + (4 if UNITS[VSTEPS[OGROUPS[og][0]][0]][0] == "s" else 2) == u:
                            outputs(p, og)
                    if first_pair:
                        conv(1 if u >= NU - PAIR0_TAPS else 0)
                    elif u in TAP_UNITS:
                        j0 = TAPS_PRE - TAPS_STEP + TAP_UNITS.index(u)
                        n = p * TAPS_STEP + (TAPS * (CT - 1) + j0)
                        taps(CT - 1, p, n, n, p * TAPS_STEP + j0)
                if last_pair:
                    outputs(p, NOG - 1)

            fill_qb(0, -QK_Q)
            mask_max(0, 0)
            mask_max(0, 1)
            norm(0, 0)
            pair(0, True, False)
            with dve.Fori(1, NPAIR - 1) as p:
                pair(p, False, False)
            pair(NPAIR - 1, False, True)
            def variance(b):
                b0, w = LNB[b]
                if b == 0:
                    dve.wait_ge(st_out[CT - 1], 32)
                dve.wait_ge(n_vm, b + 1)
                dve.tensor_scalar(rstd_c[:, b0:b0 + w], ln_mean(b), LN_EPS, None, ALU.add).then_inc(n_rs, 1)

            def rstd(b):
                b0, w = LNB[b]
                dve.wait_ge(n_sd, b + 1)
                dve.reciprocal(rstd_c[:, b0:b0 + w], rstd_c[:, b0:b0 + w]).then_inc(n_rs, 1)
                dve.wait_ge(n_rs, 3 + b + 1)

            def by_block(b, a):
                return a.rearrange("p (b t) -> p b t", t=TS) if b == 2 else a

            def normed(s):
                b, c = divmod(s, CT)
                b0, w = LNB[b]
                v = ln_cols(b, c)
                dve.tensor_tensor(v, v, by_block(b, rstd_c[:, b0:b0 + w]), ALU.mult).then_inc(n_nm, 1)
                if s >= 1:
                    cut_swish(s - 1)

            def cut_swish(s):
                b, c = divmod(s, CT)
                b0, w = LNB[b]
                dve.wait_ge(n_hi, s + 1)
                dve.tensor_tensor(by_block(b, ml[:, CT + c, b0:b0 + w]), ln_cols(b, c),
                                  by_block(b, mh[:, CT + c, b0:b0 + w].bitcast(F32)), ALU.subtract).then_inc(n_lo, 1)

            def add_y(rh, n, t):
                for nh in range(2):
                    m = 2 * NT * rh + 2 * n + nh
                    dve.wait_ge(e_mm, m + 1)
                    cols = slice(nh * 512, (nh + 1) * 512)
                    dve.tensor_tensor(y[:, t, cols], bank(4 + m % 4), y[:, t, cols], ALU.add).then_inc(e_y, 1)

            for b in range(3):
                dve.wait_ge(n_mm, b + 1)
                for c in range(CT):
                    dve.tensor_tensor(ln_cols(b, c), ln_cols(b, c), by_block(b, ln_mean(b)),
                                      ALU.subtract).then_inc(n_xc, 1)
            steps = [(variance, b) for b in range(3)]
            for b in range(3):
                steps += [(rstd, b)] + [(normed, CT * b + c) for c in range(CT)]
            dve.wait_ge(y_in[0], 32)
            for n, t in enumerate(E1_ORDER):
                if t == 0:
                    dve.wait_ge(y_in[1], 16)
                add_y(0, n, t)
                for _ in range(0 if n == 0 else 1 if n <= 3 else 3):
                    f, a = steps.pop(0)
                    f(a)
            assert not steps
            cut_swish(3 * CT - 1)
            def normalise(n, t):
                dve.wait_ge(e_ss, n + 1)
                dve.tensor_scalar(ssx[:, n:n + 1], ssx[:, n:n + 1], 1.0 / D, RMS_EPS, ALU.mult, ALU.add).then_inc(
                    e_ms, 1)
                dve.wait_ge(e_sd, n + 1)
                dve.reciprocal(rsx[:, n:n + 1], rsx[:, n:n + 1]).then_inc(e_rs, 1)
                dve.wait_ge(e_rs, n + 1)
                dve.tensor_scalar(tn[:], y[:, t, :], rsx[:, n:n + 1], None, ALU.mult).then_inc(e_tn, 1)

            def cut_back(n):
                for q in range(2):
                    dve.wait_ge(e_tr, 2 * n + q + 1)
                    if n >= 1:
                        dve.wait_ge(e_lo, 2 * n + q - 1)
                    dve.tensor_tensor(hg[:, q].rearrange("p (k r) -> p k r", k=4),
                                      bank((2 * n + q) % 4).rearrange("p (k r) -> p k r", k=4),
                                      g2s[:, 4 * q:4 * q + 4].unsqueeze(2).broadcast_to([P, 4, P]),
                                      ALU.mult).then_inc(e_g, 1)
                for q in range(2):
                    dve.wait_ge(e_hi, 2 * n + q + 1)
                    h_, src = e_part(mh, E2_ORDER[n], q)
                    l_, _ = e_part(ml, E2_ORDER[n], q)
                    dve.tensor_tensor(l_, src, h_.bitcast(F32), ALU.subtract).then_inc(e_lo, 1)

            for n, t in enumerate(E2_ORDER):
                add_y(1, n, t)
                normalise(n, t)
                if n >= 1:
                    cut_back(n - 1)
            cut_back(NT - 1)

            def glus(c6, cslot, i=None):
                base = 0 if i is None else i * 12
                for f in range(2):
                    for b, (b0, bn) in enumerate(BLOCKS):
                        k6 = c6 + 3 * f + b
                        dve.wait_ge(gu_si, base + (k6 + 1))
                        if k6 >= 2:
                            dve.wait_ge(gu_lo, base + (k6 - 1))
                        dve.tensor_tensor(pr[:, k6 % 2, 0:bn], bank(2 * (k6 % 2) + 1, bn), sg[:, k6 % 2, 0:bn],
                                          ALU.mult).then_inc(gu_pr, 1)
                        dve.wait_ge(gu_hi, base + (k6 + 1))
                        dve.tensor_tensor(al[:, 2 * cslot + f, b0:b0 + bn], pr[:, k6 % 2, 0:bn],
                                          ah[:, 2 * cslot + f, b0:b0 + bn].bitcast(F32), ALU.subtract).then_inc(gu_lo, 1)

            def adds(half, i=None):
                base_m = START if i is None else i * (4 * NT) + START
                const_m = 2 * NT * half if i is not None else 2 * NT * (NCH - 1)
                for t in range(NT):
                    for nh in range(2):
                        m = const_m + 2 * t + nh
                        dve.wait_ge(dn_mm, base_m + (m + 1))
                        if t == 0 and nh == 0:
                            dve.wait_ge(dn_y, base_m + const_m)
                        cols = slice(nh * 512, (nh + 1) * 512)
                        dve.tensor_tensor(y[:, t, cols], bank(4 + m % 4), y[:, t, cols], ALU.add).then_inc(dn_y, 1)

            glus(0, 0)
            with dve.Fori(0, (NCH - 1) // 2) as i:
                glus(6, 1, i)
                adds(0, i)
                glus(12, 0, i)
                adds(1, i)
            adds(0)


def laid_out(v):
    import numpy as np

    f = {k: np.asarray(a) for k, a in v.items()}
    w_in, w_out, w_gate, w_up, w_down = (f[k][0] for k in ("w_in", "w_out", "w_gate", "w_up", "w_down"))

    def cols(w, c0):
        return w[:, c0:c0 + P].reshape(KT, P, P).transpose(1, 0, 2).reshape(P, PC)

    def two(w, j, c0):
        return w[2 * j * P:(2 * j + 2) * P, c0:c0 + 512].reshape(2, P, 512).transpose(1, 0, 2).reshape(P, PC)

    def gate_up(c):
        return [cols(w, (2 * c + t) * P) for t in range(2) for w in (w_gate, w_up)]

    def down(c):
        return [w_down[(2 * c + t) * P:(2 * c + t + 1) * P] for t in range(2)]

    stream = [cols(w_in, 3 * DA + s * DC + c * P) for c in range(CT) for s in range(2)]
    stream += [two(w_in, j, b * DA) for b in range(3) for j in range(4)]
    stream += [w_out[k * P:(k + 1) * P] for k in range(KT)]
    stream += gate_up(0)
    for c in range(NCH - 1):
        stream += gate_up(c + 1) + down(c)
    stream += down(NCH - 1)

    x_all = np.concatenate([f["x_prompt"].reshape(SEQ, D), f["x_sample"].reshape(NS, D)])
    rows = np.concatenate([np.arange(512, LB), np.array([r for r in range(512) if r % 16 < TS])])
    assert rows.size == CK

    def cache(a):
        return a[0].reshape(NB_S, LB, NPAIR, P)[:, rows]

    def count(d):
        return sum(((d >= 0) & (d <= w) & (d % r == 0)).astype(np.int64) for w, r in ((128, 1), (512, 4), (2048, 16)))

    def log_count(d):
        c = count(d)
        return np.where(c > 0, np.log(np.maximum(c, 1)), -1.0e30).astype(np.float32)

    part = np.arange(P)[:, None]
    new_rows = np.concatenate([rows, np.arange(LB, LB + TS)])[None, :]
    state = f["state_conv"][0].transpose(2, 0, 1).reshape(CT, P, NB_S, PADC)

    def column(a):
        return a[0].reshape(-1, P).T

    return {
        "w_stream": np.stack(stream),
        "xT": x_all.T.reshape(KT, P, TOK),
        "x_all": x_all,
        "kT_c": cache(f["cache_k"]).transpose(2, 0, 3, 1).reshape(NPAIR * NB_S, P, CK),
        "v_c": cache(f["cache_v"]).reshape(NB_S, CKT, P, NPAIR, P).transpose(3, 0, 2, 1, 4).reshape(
            NPAIR * NB_S, P, CKT, P),
        "cache_k": f["cache_k"].reshape(NB_S, LB, DA),
        "cache_v": f["cache_v"].reshape(NB_S, LB, DA),
        "stT": state,
        "g1": column(f["attn_norm_g"]),
        "g2": column(f["ffn_norm_g"]),
        "qkg": np.stack([np.tile(f[k], (P, 1)) for k in ("q_norm_g", "k_norm_g")], axis=1),
        "cw": f["conv_w"][0].T.reshape(CT, P, TAPS).transpose(1, 0, 2).reshape(P, CT * TAPS),
        "cb": column(f["conv_b"]),
        "lg": column(f["conv_ln_g"]),
        "lb": column(f["conv_ln_b"]),
        "ident_d": np.eye(P, dtype=np.float32),
        "mask_p": log_count(part + SEQ - P - np.arange(D)[None, :]),
        "mask_s": log_count(LB + part % TS - new_rows),
    }


OUTPUTS = [("y_p", (SEQ, D)), ("y_s", (NS, D)), ("nk_p", (SEQ, DA)), ("nv_p", (SEQ, DA)),
           ("nc_p", (CT, P, PADC)), ("nk_s", (NB_S, LB + TS, DA)), ("nv_s", (NB_S, LB + TS, DA)),
           ("nc_s", (CT, P, NB_S, PADC))]


def kernel(**inputs):
    import numpy as np
    import concourse.bacc as bacc
    from concourse.bass_utils import run_bass_kernel_spmd as run

    nc = bacc.Bacc("TRN2", target_bir_lowering=False, num_devices=1)
    arrays, args = {}, []
    for name, a in laid_out(inputs).items():
        a = np.ascontiguousarray(a)
        arrays[f"in_{name}"] = a
        args.append(nc.dram_tensor(f"in_{name}", a.shape, mybir.dt.from_np(a.dtype), kind="ExternalInput").ap())
    for name, shape in OUTPUTS:
        args.append(nc.dram_tensor(f"out_{name}", shape, F32, kind="ExternalOutput").ap())
    hymba_layer(nc, *args)
    r = run(nc, [arrays], core_ids=[0]).results[0]
    y_p, y_s, nk_p, nv_p, nc_p, nk_s, nv_s, nc_s = (r[f"out_{name}"] for name, _ in OUTPUTS)
    return (y_p.reshape(1, SEQ, D), y_s.reshape(NB_S, TS, D),
            nk_p.reshape(1, 1, SEQ, H, DH), nv_p.reshape(1, 1, SEQ, H, DH),
            nc_p.reshape(DC, PADC).T.reshape(1, 1, PADC, DC),
            nk_s.reshape(1, NB_S, LB + TS, H, DH), nv_s.reshape(1, NB_S, LB + TS, H, DH),
            nc_s.reshape(DC, NB_S, PADC).transpose(1, 2, 0).reshape(1, NB_S, PADC, DC))
```

```python
from contextlib import ExitStack

import concourse.bass as bass
from concourse import mybir

F32 = mybir.dt.float32
F32R = mybir.dt.float32r
ALU = mybir.AluOpType
ACT = mybir.ActivationFunctionType
AX = mybir.AxisListType
ds = bass.ds

P = 128
D = 1024
KT = D // P
SEQ, NB_S, TS = 1024, 8, 8
NS = NB_S * TS
TOK = SEQ + NS
H, DH = 8, 64
DA = H * DH
DC = D - DA
CT = DC // P
NPAIR = H // 2
TAPS = 31
PADC = TAPS - 1
DFF = 2816
NF = DFF // P
NCH = NF // 2
LB = 1024
CK = 768
CKT = CK // P
SK = CK + TS
PC = 1024
N_PIECES = 2 * CT + 12 + 8 + 6 * NCH
TILES = [t * P for t in range(SEQ // P)] + [TOK - P]
NT = len(TILES)
BLOCKS = [(0, 364), (364, 362), (726, 362)]
SMP = PADC + SEQ
SW = PADC + TS
UW = SMP + NB_S * SW
CVS = NB_S * SW - PADC
RMS_EPS, LN_EPS = 1e-6, 1e-5

LNB = [(0, 512), (512, 512), (SEQ, NS)]
NG = KT * len(BLOCKS)
Y_LATE = 3
E1_ORDER = list(range(Y_LATE, KT)) + list(range(Y_LATE))
VAR0 = 4
SUM_AT = 2

GLU_ORDER = [(f, b) for f in range(2) for b in range(3)]
FIRST_ORDER = [(0, 0), (0, 1), (1, 0), (0, 2), (1, 1), (1, 2)]

UNITS = [("s", 0, 0)] + [("p", h, i) for i in range(4) for h in range(2)]
UNITS += [("s", 1, 0)] + [("p", h, i) for i in range(4, 8) for h in range(2)]
NU = len(UNITS)
S_UNITS = [u for u, (kind, _, _) in enumerate(UNITS) if kind == "s"]
VSTEPS = [[0]] + [[u, u + 1] for u in (1, 3, 5, 7)] + [[9]] + [[u, u + 1] for u in (10, 12, 14, 16)]
NV = len(VSTEPS)
V_OF = {u: v for v, us in enumerate(VSTEPS) for u in us}
OGROUPS = [[0], [1, 2, 3, 4], [5], [6, 7, 8, 9]]
NOG = len(OGROUPS)
UT = [i + 1 if kind == "p" else CKT + 1 for kind, _, i in UNITS]
UQ = [sum((t + 3) // 4 for t in UT[:u]) for u in range(NU + 1)]
QK_AT = NU - 2
QK_Q = 6
NQ = UQ[NU] + QK_Q
assert NQ % 2 == 0 and UQ[QK_AT] % 2 == 0 and NU % 3 == 0 and NV % 2 == 0
START = 8
TAPS_STEP = 10
TAP_UNITS = [1, 3, 5, 7, 9, 11, 13, 15, 16, 17]
assert len(TAP_UNITS) == TAPS_STEP
PAIR0_TAPS = 14
TAPS_PRE = TAPS - (NPAIR - 1) * TAPS_STEP
assert TAPS_PRE == 1


def count(per_pair, p, n):
    return p * per_pair + (START + n)


def quads(p, n):
    return p * NQ + (START + QK_Q + n)


def quad_of(u, last):
    return UQ[u] + (QK_Q if u >= QK_AT and not last else 0)


def hymba_layer(nc, w_stream, xT, kT_c, v_c, cache_k, cache_v, stT, g1, g2, qkg, cw, cb, lg, lb,
                ident_d, mask_p, mask_s, yT_out, nk_p, nv_p, nc_p, nk_s, nv_s, nc_s):
    scr = nc.dram_tensor("qkv_scratch", (3, TOK, DA), F32, kind="Internal").ap()

    with ExitStack() as ctx:
        def const(name, shape, dt=F32):
            return ctx.enter_context(nc.sbuf_tensor(name, shape, dt))

        def sem(name):
            return ctx.enter_context(nc.semaphore(name))

        ident = const("ident", [P, P])
        ones_c = const("ones_c", [P, P])
        zero_c = const("zero_c", [P, 1])
        g1s = const("g1s", [P, KT])
        g2s = const("g2s", [P, KT])
        qkgs = const("qkgs", [P, 2, DH])
        cws = const("cws", [P, CT * TAPS])
        cbs = const("cbs", [P, CT])
        lgs = const("lgs", [P, CT])
        lbs = const("lbs", [P, CT])
        ssx = const("ssx", [P, NT])
        rsx = const("rsx", [P, NT])
        ssh = const("ssh", [P, 2, H])
        rsh = const("rsh", [P, 2, H])
        nmx = const("nmx", [P, 3])
        mxs = const("mxs", [P, 3])
        den = const("den", [P, 3])
        rden = const("rden", [P, 3])

        def place(at, name, shape, dt=F32):
            with ExitStack() as s:
                if at:
                    s.enter_context(nc.sbuf_tensor(f"below_{name}", [P, at // 4], F32))
                return s.enter_context(nc.sbuf_tensor(name, shape, dt))

        def row(name, ats, shape, dt=F32):
            t = place(ats[0], name, shape, dt)
            n = 4
            for d in shape[1:]:
                n *= d
            ats[0] += -(-n // 64) * 64
            return t

        RAW0 = 0
        WS0 = RAW0 + 2 * PC * 4
        WS4 = WS0 + 4 * 2 * PC * 4
        UC0 = WS0 + 8 * 2 * PC * 4
        GAP0 = -(-(UC0 + (CT + 1) * UW * 4) // 64) * 64
        M0 = 139968
        raw = place(RAW0, "raw", [P, 2, PC])
        ws = place(WS0, "ws", [P, 8, 2, PC], F32R)
        uc = place(UC0, "uc", [P, (CT + 1) * UW])
        at = [GAP0]
        xh = row("xh", at, [P, KT, TOK], F32R)
        xl = row("xl", at, [P, KT, TOK], F32R)
        tmp0 = at[0]
        xr = row("xr", at, [P, 4, TOK])
        xq = row("xq", at, [P, 2, TOK])
        rb = row("rb", at, [P, TOK])
        rbt = row("rbt", at, [P, 2, P])
        at = [tmp0]
        glu_g = row("glu_g", at, [P, 364])
        glu_s = row("glu_s", at, [P, 364])
        glu_a = row("glu_a", at, [P, 364])
        zt = row("zt", at, [P, 2, DA])
        zo = row("zo", at, [P, 2, DA])
        zsq = row("zsq", at, [P, DA])
        at = [WS4]
        tb = row("tb", at, [P, 3, D])
        pt = row("pt", at, [P, 4, D])
        mks = row("mks", at, [P, SK])
        so = row("so", at, [P, P])
        assert at[0] <= UC0
        Y0 = M0 - KT * TOK * 4
        at = [GAP0]
        qt = row("qt", at, [P, TOK])
        kt_ = row("kt", at, [P, TOK])
        mkp = row("mkp", at, [P, D])
        assert at[0] <= Y0 + Y_LATE * TOK * 4
        HALF = KT // 2 * TOK * 4
        at = [M0 + HALF]
        skt = row("skt", at, [P, 4, CK])
        vn = row("vn", at, [P, SEQ // P, P])
        qks = row("qks", at, [P, 2, P])
        assert at[0] <= M0 + 2 * HALF
        at = [M0 + 3 * HALF]
        sv = row("sv", at, [P, 4, CKT, P])
        vns = row("vns", at, [P, NB_S, P])
        qb = row("qb", at, [P, NB_S, 32])
        assert at[0] <= M0 + 4 * HALF
        qn, kn = raw[:, 0, :], raw[:, 1, :]
        at = [M0]
        mh = row("mh", at, [P, KT, TOK], F32R)
        ml = row("ml", at, [P, KT, TOK], F32R)
        sq = place(M0 + 3 * HALF, "sq", [P, 2, CT, 512])
        rstd_c = place(-(-(UC0 + CT * UW * 4) // 64) * 64, "rstd_c", [P, TOK])
        ACT0 = WS4 + 2 * 2 * PC * 4
        y = place(Y0, "y", [P, KT, TOK])
        at = [ACT0 + 4 * TOK * 4]
        ysq = row("ysq", at, [P, KT, 364])
        yn = row("yn", at, [P, 3, 364])
        assert at[0] <= ACT0 + 8 * TOK * 4
        at = [ACT0]
        ah = row("ah", at, [P, 4, TOK], F32R)
        al = row("al", at, [P, 4, TOK], F32R)
        sg = row("sg", at, [P, 2, 364])
        pr = row("pr", at, [P, 2, 364])
        assert at[0] <= Y0

        ps = ctx.enter_context(nc.psum_tensor("ps", [P, 8 * 512], F32))

        def bank(b, n=512, off=0):
            return ps[:, b * 512 + off:b * 512 + off + n]

        c_in = sem("consts_in")
        x_in = [sem(f"x_in{k}") for k in range(KT)]
        x_hi, x_lo = sem("x_hi"), sem("x_lo")
        xsq, x_ac, x_ss = sem("x_squares"), sem("x_squares_added"), sem("x_square_sums")
        ms_x, sd_x, rs_x = sem("x_meansq"), sem("x_rms"), sem("x_rstd")
        rbt_s, rbt_t, rb_s = sem("rstd_wide"), sem("rstd_turned"), sem("rstd_rows")
        raw_in = [sem("raw_in0"), sem("raw_in1")]
        w_hi, w_lo = sem("w_hi"), sem("w_lo")
        mem_s, zero_s = sem("memsets"), sem("zeroed")
        ag_mm, ag_ga, ag_sig, ag_aa, ag_u = (sem("ag_mm"), sem("ag_gate"), sem("ag_sigmoid"), sem("ag_a"),
                                             sem("ag_u"))
        st_in, st_out = sem("state_in"), [sem(f"state_out{c}") for c in range(CT)]
        c_mm, c_z, c_sq, c_ss, c_rt, c_rs, c_n, c_o = (sem("qkv_mm"), sem("qkv_z"), sem("qkv_sq"), sem("qkv_ss"),
                                                 sem("qkv_rms"), sem("qkv_rstd"), sem("qkv_normed"), sem("qkv_out"))
        c_st = [sem("qkv_stored0"), sem("qkv_stored1")]
        d_msk = sem("masks_in")
        d_q, d_qs, d_v = sem("pair_qk_in"), sem("pair_qk_samples_in"), sem("pair_v_in")
        d_sk = [sem(f"sample_k_in{i}") for i in range(4)]
        d_sv = [sem(f"sample_v_in{i}") for i in range(4)]
        d_tr, d_ev, d_qb = sem("turned"), sem("turned_out"), sem("qb_ready")
        d_s, d_tt, d_mx, d_ex, d_rc, d_sc, d_pv = (
            sem("scores"), sem("scores_masked"), sem("maximum"), sem("exped"), sem("den_recip"), sem("normed"),
            sem("values_summed"))
        d_oh, d_ol, d_oc, d_ot = sem("attn_hi"), sem("attn_lo"), sem("sample_out_copied"), sem("sample_out_turned")
        cv_a, cv_b = sem("conv_prompt"), sem("conv_samples")
        n_mm, n_xc, n_sq, n_ac, n_vm, n_sd, n_rs, n_nm, n_si, n_hi, n_lo = (sem(f"ln_{x}") for x in (
            "mean", "centred", "squares", "squares_added", "var", "std", "rstd", "normed", "swish", "hi", "lo"))
        y_in = [sem("residual_in0"), sem("residual_in1")]
        e_mm, e_y, e_sq, e_ac, e_ss, e_ms, e_sd, e_rs, e_n, e_hi, e_lo = (sem(f"out_{x}") for x in (
            "mm", "y", "squares", "squares_added", "sum_squares", "meansq", "rms", "rstd", "normed", "hi", "lo"))
        gu_mm, gu_si, gu_pr, gu_hi, gu_lo = (sem(f"glu_{x}") for x in ("mm", "silu", "prod", "hi", "lo"))
        dn_mm, dn_y = sem("down_mm"), sem("down_y")
        own_wait = sem("own_wait")
        s_out, s_cp = sem("outputs"), sem("cache_copies")

        def hi(slot):
            return ws[:, slot, 0, :]

        def lo(slot):
            return ws[:, slot, 1, :]

        def mm3(e, out, wh, wl, mh_, ml_, first, last):
            e.matmul(out, wh, mh_, start=first, stop=False)
            e.matmul(out, wh, ml_, start=False, stop=False)
            return e.matmul(out, wl, mh_, start=False, stop=last)

        def ustate(c, a, b):
            return uc[:, c * UW + SMP:(c + 1) * UW].rearrange("p (b n) -> p b n", b=NB_S)[:, :, a:b]

        N_B, N_QKV, N_OUT = 2 * CT, 12, 8
        E0 = N_B + N_QKV
        F0 = E0 + N_OUT
        L0 = F0 + 4
        CP_BEFORE = NB_S - 5

        def ln_cols(b, c):
            b0, w = LNB[b]
            return uc[:, c * UW + b0:c * UW + b0 + w] if b < 2 else ustate(c, 0, TS)

        def ln_mean(b):
            return bank(b, LNB[b][1])

        def y_meansq(b):
            return bank((0, 1, 4)[b], BLOCKS[b][1])

        block = ctx.enter_context(nc.Block())

        @block.sync
        def _(sp):
            def piece(n, k):
                if not isinstance(n, int) or n >= 2:
                    sp.wait_ge(w_lo, n - 1)
                src = w_stream[n] if isinstance(n, int) else w_stream[ds(n, 1)].rearrange("a p c -> (a p) c")
                sp.dma_start(raw[:, k % 2, :], src).then_inc(raw_in[k % 2], 16)

            sp.dma_start(g1s[:], g1).then_inc(c_in, 16)
            piece(0, 0)
            for k in range(4):
                sp.dma_start(xr[:, k, :], xT[k]).then_inc(x_in[k], 16)
                if k == 0:
                    piece(1, 1)
            for k in range(4, KT):
                sp.wait_ge(x_lo, k - 3)
                sp.wait_ge(xsq, k - 3)
                sp.dma_start(xr[:, k % 4, :], xT[k]).then_inc(x_in[k], 16)
            for dst, src in ((ident[:], ident_d), (g2s[:], g2), (qkgs[:], qkg), (cws[:], cw), (cbs[:], cb),
                             (lgs[:], lg), (lbs[:], lb)):
                sp.dma_start(dst, src).then_inc(c_in, 16)
            for c in range(CT):
                sp.dma_start(ustate(c + 1, 0, PADC), stT[c]).then_inc(st_in, 16)
            for n in range(2, N_B + 8):
                piece(n, n)

            def store_block(j, t0=0, t1=NT):
                for t, r0 in list(enumerate(TILES))[t0:t1]:
                    m = j * NT + t
                    sp.wait_ge(c_o if j < 2 else c_z, m + 1)
                    if t < NT - 1:
                        dst, src = scr[j, r0:r0 + P, :], zo[:, m % 2, :]
                    else:
                        dst, src = scr[j, SEQ:TOK, :], zo[P - NS:P, m % 2, :]
                    sp.dma_start(dst, src).then_inc(c_st[m % 2], 16)

            store_block(0)
            for n in range(N_B + 8, N_B + 12):
                piece(n, n)
            store_block(1)
            for n in range(E0, E0 + 4):
                piece(n, n)

            def rows_of(j, cols):
                return scr[j, 0:SEQ, cols].rearrange("(t r) c -> r t c", r=P)

            def load_qk(cols):
                sp.dma_start(qn.rearrange("p (t c) -> p t c", c=P), rows_of(0, cols)).then_inc(d_q, 16)
                sp.dma_start(kn.rearrange("p (t c) -> p t c", c=P), rows_of(1, cols)).then_inc(d_q, 16)

            def load_qks(cols):
                sp.dma_start(qks[0:NS, 0, :], scr[0, SEQ:TOK, cols]).then_inc(d_qs, 16)
                sp.dma_start(qks[0:NS, 1, :], scr[1, SEQ:TOK, cols]).then_inc(d_qs, 16)

            def load_v(cols):
                sp.dma_start(vn[:], rows_of(2, cols)).then_inc(d_v, 16)
                sp.dma_start(vns[0:TS, :, :], scr[2, SEQ:TOK, cols].rearrange("(b t) c -> t b c", t=TS)).then_inc(
                    d_v, 16)

            def load_sk(first):
                for b in range(4):
                    sp.dma_start(skt[:, b, :], kT_c[ds(first + b, 1)].rearrange("a p c -> (a p) c")).then_inc(
                        d_sk[b], 16)

            def load_sv(first):
                for b in range(4):
                    sp.dma_start(sv[:, b], v_c[ds(first + b, 1)].rearrange("a p k c -> (a p) k c")).then_inc(
                        d_sv[b], 16)

            def second_samples(p):
                sp.wait_ge(d_s, count(NU, p, 1))
                load_sk(p * NB_S + 4)
                sp.wait_ge(d_pv, count(NV, p, 1))
                load_sv(p * NB_S + 4)

            sp.wait_ge(c_st[0], 16 * NT)
            sp.wait_ge(c_st[1], 16 * NT)
            store_block(2, 0, NT - 3)
            sp.wait_ge(w_lo, E0 + 4)
            load_qk(slice(0, P))
            store_block(2, NT - 3)
            sp.wait_ge(c_mm, 3 * NT)
            load_qks(slice(0, P))
            load_sk(0)
            sp.dma_start(mks[:], mask_s).then_inc(d_msk, 16)
            sp.dma_start(mkp[:], mask_p).then_inc(d_msk, 16)
            sp.wait_ge(c_st[0], 16 * 14)
            sp.wait_ge(c_st[1], 16 * 13)
            load_v(slice(0, P))
            load_sv(0)
            with sp.Fori(0, NPAIR - 1) as p:
                nxt = ds(p * P + P, P)
                sp.wait_ge(d_tr, quads(p, 0))
                load_qk(nxt)
                load_qks(nxt)
                second_samples(p)
                sp.wait_ge(d_s, count(NU, p, 10))
                load_sk(p * NB_S + NB_S)
                sp.wait_ge(d_pv, count(NV, p, 6))
                load_sv(p * NB_S + NB_S)
                sp.wait_ge(d_pv, count(NV, p, NV))
                load_v(nxt)
            second_samples(NPAIR - 1)
            sp.dma_start(y[:, Y_LATE:KT, :], xT[Y_LATE:KT].rearrange("k p n -> p k n")).then_inc(y_in[0], 16)
            for n in range(E0 + 4, E0 + 6):
                piece(n, n)
            sp.wait_ge(d_s, count(NU, NPAIR - 1, NU))
            sp.wait_ge(d_tt, count(NU, NPAIR - 1, NU))
            sp.dma_start(y[:, 0:Y_LATE, :], xT[0:Y_LATE].rearrange("k p n -> p k n")).then_inc(y_in[1], 16)
            for n in range(E0 + 6, F0 + 4):
                piece(n, n)
            for j, (dst_p, dst_s) in ((1, (nk_p, nk_s)), (2, (nv_p, nv_s))):
                sp.dma_start(dst_p, scr[j, 0:SEQ, :]).then_inc(s_cp, 16)
                sp.dma_start(dst_s[:, LB:LB + TS, :],
                             scr[j, SEQ:TOK, :].rearrange("(b t) c -> b t c", t=TS)).then_inc(s_cp, 16)
            with sp.Fori(0, (NCH - 1) // 2) as i:
                for k in range(12):
                    piece(i * 12 + (L0 + k), L0 + k)
            for n in range(N_PIECES - 2, N_PIECES):
                piece(n, n)
            for oc in range(KT):
                sp.wait_ge(dn_y, START + NG * (NCH - 1) + 3 * (oc + 1))
                sp.dma_start(yT_out[oc], y[:, oc, :]).then_inc(s_out, 16)
            sp.wait_ge(s_out, 16 * KT)
            sp.wait_ge(s_cp, 16 * 4 + 16 * 2 * NB_S)
            for c in range(CT):
                sp.wait_ge(st_out[c], 32)

        @block.gpsimd
        def _(pool):
            zeros = zero_c[:, 0:1].broadcast_to([P, PC])
            pool.memset(zero_c[:], 0.0).then_inc(zero_s, 1)
            pool.wait_ge(zero_s, 1)
            pool.memset(ones_c[:], 1.0 / DC).then_inc(mem_s, 1)
            for c in range(CT):
                pool.memset(uc[:, (c + 1) * UW:(c + 1) * UW + PADC], 0.0).then_inc(mem_s, 1)

            def cut(n, k, slot):
                per = n // 2 if isinstance(n, int) else None
                pool.wait_ge(raw_in[k % 2], 16 * (per + 1))
                pool.tensor_tensor(hi(slot), raw[:, k % 2, :], zeros, ALU.add).then_inc(w_hi, 1)
                pool.wait_ge(w_hi, n + 1)
                pool.tensor_tensor(lo(slot), raw[:, k % 2, :], hi(slot).bitcast(F32), ALU.subtract).then_inc(w_lo, 1)

            pool.wait_ge(w_lo, 2)
            for n in range(2, N_B):
                if n >= 4:
                    pool.wait_ge(ag_mm, 3 * (n // 2 - 1))
                cut(n, n, n % 4)
            def gain(m):
                pool.wait_ge(c_n, 2 * m + 2)
                z3 = zo[:, m % 2, :].rearrange("p (h d) -> p h d", d=DH)
                pool.tensor_tensor(z3, z3, qkgs[:, m // NT, :].unsqueeze(1).broadcast_to([P, H, DH]),
                                   ALU.mult).then_inc(c_o, 1)

            pool.wait_ge(rb_s, 4)
            for j in range(3):
                if j == 1:
                    pool.wait_ge(ag_mm, 3 * CT)
                if j == 2:
                    pool.wait_ge(c_mm, NT)
                for m in range(4):
                    n = N_B + 4 * j + m
                    cut(n, n, m + (0 if j == 1 else 4))
                    if j:
                        gain(NT * (j - 1) + m)
                if j:
                    for t in range(4, NT):
                        gain(NT * (j - 1) + t)
            pool.wait_ge(c_mm, 2 * NT)
            for m in range(4):
                cut(E0 + m, E0 + m, m)
            pool.wait_ge(d_pv, count(NV, NPAIR - 1, NV))
            cut(E0 + 4, E0 + 4, 4)
            for b in range(3):
                o = sq[:, b % 2, 0, 0:LNB[b][1]]
                for c in range(1, CT):
                    pool.wait_ge(n_sq, CT * b + c + 1)
                    if c >= 2:
                        pool.wait_ge(n_ac, (CT - 1) * b + c - 1)
                    pool.tensor_tensor(o, o, sq[:, b % 2, c, 0:LNB[b][1]], ALU.add).then_inc(n_ac, 1)
            for m in range(1, 4):
                cut(E0 + 4 + m, E0 + 4 + m, 4 + m)
            pool.wait_ge(e_mm, NG)
            cut(F0, F0, 0)
            for b in range(3):
                cut(F0 + b + 1, F0 + b + 1, b + 1)
                for k in range(1, KT):
                    pool.wait_ge(e_sq, KT * b + k + 1)
                    if k >= 2:
                        pool.wait_ge(e_ac, (KT - 1) * b + k - 1)
                    o = ysq[:, 0, 0:BLOCKS[b][1]]
                    pool.tensor_tensor(o, o, ysq[:, k, 0:BLOCKS[b][1]], ALU.add).then_inc(e_ac, 1)
            pool.wait_ge(gu_mm, FIRST_ORDER.index((0, 2)) + 1)
            with pool.Fori(0, (NCH - 1) // 2) as i:
                for half in range(2):
                    for m in range(6):
                        k = L0 + 6 * half + m
                        if m == 0:
                            pool.wait_ge(gu_mm, i * 12 + (6 * half + 3))
                        if m == 2:
                            pool.wait_ge(gu_mm, i * 12 + (6 * half + 6))
                        if m == 4:
                            if half == 0:
                                pool.wait_ge(e_mm, 2 * NG)
                            pool.wait_ge(dn_mm, i * (2 * NG) + (START + NG * half))
                        pool.wait_ge(raw_in[k % 2], i * (16 * 6) + 16 * (k // 2 + 1))
                        slot = m
                        pool.tensor_tensor(hi(slot), raw[:, k % 2, :], zeros, ALU.add).then_inc(w_hi, 1)
                        pool.wait_ge(w_hi, i * 12 + (k + 1))
                        pool.tensor_tensor(lo(slot), raw[:, k % 2, :], hi(slot).bitcast(F32),
                                           ALU.subtract).then_inc(w_lo, 1)
            pool.wait_ge(gu_mm, 6 * NCH)
            for m in range(2):
                n = N_PIECES - 2 + m
                cut(n, n, m)

        @block.tensor
        def _(pe):
            for s in (d_s, d_pv, d_tr, dn_mm):
                pe.sem_inc(s, START)
            def ag(c, g, side, k):
                b0, bn = BLOCKS[g % 3]
                slot = (2 * c + side) % 4
                return mm3(pe, bank(2 * (g % 3) + side, bn), hi(slot)[:, k * P:(k + 1) * P],
                           lo(slot)[:, k * P:(k + 1) * P], xh[:, k, b0:b0 + bn], xl[:, k, b0:b0 + bn],
                           k == 0, k == KT - 1)

            pe.wait_ge(w_lo, 2)
            for k in range(KT):
                pe.wait_ge(x_lo, k + 1)
                for g in range(3):
                    for side in range(2):
                        last = ag(0, g, side, k)
                    if k == KT - 1:
                        last.then_inc(ag_mm, 1)
            pe.wait_ge(mem_s, 1)
            pe.wait_ge(x_ac, KT - 1)
            for t, r0 in enumerate(TILES):
                last = pe.matmul(bank(6, 1, t), rb[:, r0:r0 + P], ones_c[:, 0:1], start=True, stop=True)
            last.then_inc(x_ss, 1)
            pe.wait_ge(c_in, 16 * 8)
            pe.wait_ge(ms_x, 1)
            for t in range(NT):
                pe.wait_ge(rbt_s, t + 1)
                if t == 8:
                    pe.wait_ge(rb_s, 1)
                pe.transpose(bank(6 + t // 4 % 2, P, (t % 4) * P), rbt[:, t % 2, :], ident[:]).then_inc(rbt_t, 1)
            for c in range(1, CT):
                pe.wait_ge(w_lo, 2 * (c + 1))
                for g in range(3 * c, 3 * c + 3):
                    pe.wait_ge(ag_aa, g - 2)
                    for side in range(2):
                        for k in range(KT):
                            last = ag(c, g, side, k)
                    last.then_inc(ag_mm, 1)
            m = 0
            for j in range(3):
                pe.wait_ge(w_lo, N_B + 4 * (j + 1))
                s0 = 0 if j == 1 else 4
                for t, r0 in enumerate(TILES):
                    if m == 0:
                        pe.wait_ge(rb_s, 3)
                        pe.wait_ge(ag_aa, 3 * CT)
                    if m >= 4:
                        pe.wait_ge(c_z, m - 3)
                    for k in range(KT):
                        wcol = slice((k % 2) * DA, (k % 2 + 1) * DA)
                        last = mm3(pe, bank(4 + m % 4), xh[:, k, r0:r0 + P], xl[:, k, r0:r0 + P],
                                   hi(s0 + k // 2)[:, wcol], lo(s0 + k // 2)[:, wcol], k == 0, k == KT - 1)
                    last.then_inc(c_mm, 1)
                    m += 1
            pe.wait_ge(c_z, 3 * NT)

            def quad_wait(p, q):
                pe.wait_ge(d_ev, quads(p, q - 1))

            def turn_qk(p, q0, first, end):
                for q, (src, t0) in list(enumerate(((qn, 0), (qn, 4), (kn, 0), (kn, 4))))[first:end]:
                    quad_wait(p, q0 + q)
                    for t in range(4):
                        last = pe.transpose(bank(4 + q % 2, P, t * P), src[:, (t0 + t) * P:(t0 + t + 1) * P], ident[:])
                    last.then_inc(d_tr, 1)
                for q in range(4, end):
                    quad_wait(p, q0 + q)
                    pe.sem_inc(own_wait, 1)
                    pe.transpose(bank(4 + q % 2, NS), qks[0:NS, q - 4, :], ident[0:NS, 0:NS]).then_inc(d_tr, 1)

            def scores(p, u, first_pair=False):
                kind, h, i = UNITS[u]
                pe.wait_ge(d_tt, count(NU, p, u - 1))
                s = 2 * (u % 2)
                if kind == "p":
                    rows = slice(DH * h, DH * h + DH)
                    n = (i + 1) * P
                    for c0 in range(0, n, 512):
                        cn = min(512, n - c0)
                        last = pe.matmul(bank(s + c0 // 512, cn), qt[rows, i * P:(i + 1) * P],
                                         kt_[rows, c0:c0 + cn], start=True, stop=True)
                else:
                    if h == 0:
                        pe.wait_ge(d_ev, quads(p, 0 if first_pair else UQ[QK_AT] + QK_Q - NQ))
                        pe.wait_ge(d_qb, p + 1)
                    for k0, k1 in ((0, 512), (512, CK), (CK, SK)):
                        for bb in range(4):
                            b = 4 * h + bb
                            if k0 == 0:
                                pe.wait_ge(d_sk[bb], p * 32 + 16 * (h + 1))
                            keys = kt_[:, SEQ + TS * b:SEQ + TS * (b + 1)] if k0 == CK else skt[:, bb, k0:k1]
                            last = pe.matmul(ps[32 * bb:32 * bb + 32, s * 512 + k0:s * 512 + k1], qb[:, b, :], keys,
                                             start=True, stop=True)
                last.then_inc(d_s, 1)

            def turn(p, u, last_pair):
                pe.wait_ge(d_sc, p * NU + (u + 1))
                q = quad_of(u, last_pair)
                for c in range(UT[u]):
                    if c % 4 == 0:
                        quad_wait(p, q + c // 4)
                    w = P if UNITS[u][0] == "p" or c < CKT else TS
                    last = pe.transpose(bank(4 + (q + c // 4) % 2, P, (c % 4) * P)[0:w, :],
                                        tb[:, u % 3, c * P:c * P + w], ident[:])
                    if c % 4 == 3 or c == UT[u] - 1:
                        last.then_inc(d_tr, 1)

            def values(p, v, last_pair):
                us = VSTEPS[v]
                kind, h, i = UNITS[us[0]]
                end = us[-1]
                pe.wait_ge(d_ev, quads(p, quad_of(end, last_pair) + (UT[end] + 3) // 4))
                og = next(g for g, vs in enumerate(OGROUPS) if v in vs)
                if v == OGROUPS[og][0]:
                    pe.wait_ge(d_ol, count(NOG, p, og - 1))
                if v == 0:
                    pe.wait_ge(d_v, p * 32 + 32)
                ob = 6 + og % 2
                if kind == "p":
                    for c in range(i + 1):
                        for h in range(2):
                            last = pe.matmul(bank(ob, P, (i % 4) * P)[DH * h:DH * h + DH, :],
                                             vn[:, c, DH * h:DH * h + DH],
                                             pt[:, 2 * (v % 2) + h, c * P:(c + 1) * P],
                                             start=(c == 0), stop=(c == i))
                else:
                    for c in range(CKT + 1):
                        for bb in range(4):
                            b = 4 * h + bb
                            if c == 0:
                                pe.wait_ge(d_sv[bb], p * 32 + 16 * (h + 1))
                            r = slice(0, P) if c < CKT else slice(0, TS)
                            vals = sv[:, bb, c, :] if c < CKT else vns[0:TS, b, :]
                            last = pe.matmul(bank(ob, P)[32 * bb:32 * bb + 32, :],
                                             pt[r, 2 * (v % 2), c * P + 32 * bb:c * P + 32 * bb + 32], vals,
                                             start=(c == 0), stop=(c == CKT))
                last.then_inc(d_pv, 1)

            def turn_outputs(p, h):
                pe.wait_ge(d_oc, p * 2 + (h + 1))
                pe.transpose(bank(6, P, P), so[:], ident[:]).then_inc(d_ot, 1)

            def pair(p, last_pair):
                for u in range(NU):
                    if u + 2 < NU:
                        scores(p, u + 2)
                    elif u == NU - 1 and not last_pair:
                        scores(p + 1, 1)
                    if u == QK_AT and not last_pair:
                        pe.wait_ge(d_q, p * 32 + 64)
                        pe.wait_ge(d_qs, p * 32 + 64)
                        turn_qk(p, UQ[QK_AT], 0, 2)
                        values(p, V_OF[u - 1], last_pair)
                        turn_qk(p, UQ[QK_AT], 2, QK_Q)
                    turn(p, u, last_pair)
                    for v in range(NV):
                        if VSTEPS[v][-1] == u - 1 and (u != QK_AT or last_pair):
                            values(p, v, last_pair)
                    for h in range(2):
                        if u == S_UNITS[h] + 3:
                            turn_outputs(p, h)
                    if u == QK_AT and not last_pair:
                        scores(p + 1, 0)
                values(p, NV - 1, last_pair)

            pe.wait_ge(d_q, 32)
            turn_qk(0, -QK_Q, 0, 4)
            pe.wait_ge(d_qs, 32)
            turn_qk(0, -QK_Q, 4, QK_Q)
            scores(0, 0, True)
            scores(0, 1, True)
            with pe.Fori(0, NPAIR - 1) as p:
                pair(p, False)
            pair(NPAIR - 1, True)

            def project(rh, m, oc, g):
                b0, bn = BLOCKS[g]
                if m >= 4:
                    pe.wait_ge(e_y, m - 3)
                for k in range(4 * rh, 4 * rh + 4):
                    col = slice(oc * P, (oc + 1) * P)
                    last = mm3(pe, bank(4 + m % 4, bn), hi(k)[:, col], lo(k)[:, col], mh[:, k, b0:b0 + bn],
                               ml[:, k, b0:b0 + bn], k == 4 * rh, k == 4 * rh + 3)
                last.then_inc(e_mm, 1)

            pe.wait_ge(cv_a, START + TAPS * CT)
            pe.wait_ge(cv_b, START + TAPS * CT)
            pe.wait_ge(mem_s, 1)
            pe.wait_ge(d_tt, count(NU, NPAIR - 1, NU))
            for b in range(3):
                for c in range(CT):
                    last = pe.matmul(ln_mean(b), ones_c[:], ln_cols(b, c), start=(c == 0), stop=(c == CT - 1))
                last.then_inc(n_mm, 1)
            pe.wait_ge(d_ol, count(NOG, NPAIR - 1, NOG))
            pe.wait_ge(d_ev, START + QK_Q + NQ * NPAIR - QK_Q)
            pe.wait_ge(w_lo, E0 + 4)
            for n, oc in enumerate(E1_ORDER):
                for g in range(3):
                    m = 3 * n + g
                    project(0, m, oc, g)
                    if VAR0 <= m < VAR0 + 3:
                        b = m - VAR0
                        pe.wait_ge(n_ac, (CT - 1) * (b + 1))
                        pe.matmul(ln_mean(b), ones_c[:], sq[:, b % 2, 0, 0:LNB[b][1]], start=True,
                                  stop=True).then_inc(n_vm, 1)

            def sum_squares(b):
                pe.wait_ge(e_ac, (KT - 1) * (b + 1))
                if b == 2:
                    pe.wait_ge(e_y, 2 * NG - 3)
                pe.matmul(y_meansq(b), ones_c[:], ysq[:, 0, 0:BLOCKS[b][1]], start=True, stop=True).then_inc(e_ss, 1)

            pe.wait_ge(w_lo, E0 + 8)
            for g in range(3):
                pe.wait_ge(n_lo, CT * (g + 1))
                for oc in range(KT):
                    project(1, NG + KT * g + oc, oc, g)
                    if g >= 1 and oc == SUM_AT:
                        sum_squares(g - 1)
            pe.wait_ge(e_ms, 2)

            def gate_up(c6, cslot, i=None):
                base = 0 if i is None else i * 12
                npc = F0 + 4 if i is None else i * 12 + (L0 + cslot * 6 + 4)
                for n, (f, b) in enumerate(FIRST_ORDER if i is None else GLU_ORDER):
                    b0, bn = BLOCKS[b]
                    k6 = c6 + n
                    if b == 0:
                        pe.wait_ge(w_lo, npc - 2 * (1 - f))
                    if i is None and f == 0:
                        pe.wait_ge(e_lo, KT * (b + 1))
                    if k6 >= 2:
                        pe.wait_ge(gu_pr, base + (k6 - 1))
                    for side in range(2):
                        out = bank(2 * (k6 % 2) + side, bn)
                        slot = 2 * f + side
                        for k in range(KT):
                            last = mm3(pe, out, hi(slot)[:, k * P:(k + 1) * P], lo(slot)[:, k * P:(k + 1) * P],
                                       mh[:, k, b0:b0 + bn], ml[:, k, b0:b0 + bn], k == 0, k == KT - 1)
                    last.then_inc(gu_mm, 1)
                    if i is None and n == 0:
                        sum_squares(2)

            def down(half, i=None):
                base_m = START if i is None else i * (2 * NG) + START
                const_m = NG * half if i is not None else NG * (NCH - 1)
                wd = 4 if i is not None else 0
                if i is None:
                    pe.wait_ge(w_lo, N_PIECES)
                    pe.wait_ge(gu_lo, 6 * NCH)
                else:
                    pe.wait_ge(w_lo, i * 12 + (L0 + 6 * half + 6))
                    pe.wait_ge(gu_lo, i * 12 + 6 * (half + 1))
                a0 = 2 * half
                for m in range(NG):
                    oc, (b0, bn) = m // 3, BLOCKS[m % 3]
                    pe.wait_ge(dn_y, base_m + (const_m + m - 3))
                    col = slice(oc * P, (oc + 1) * P)
                    for f in range(2):
                        last = mm3(pe, bank(4 + m % 4, bn), hi(wd + f)[:, col], lo(wd + f)[:, col],
                                   ah[:, a0 + f, b0:b0 + bn], al[:, a0 + f, b0:b0 + bn], f == 0, f == 1)
                    last.then_inc(dn_mm, 1)

            gate_up(0, 0)
            with pe.Fori(0, (NCH - 1) // 2) as i:
                gate_up(6, 0, i)
                down(0, i)
                gate_up(12, 1, i)
                down(1, i)
            down(0)

        @block.scalar
        def _(act):
            for s in (d_ev, d_ex):
                act.sem_inc(s, START)
            act.wait_ge(c_in, 16)
            for k in range(KT):
                if k < 2:
                    act.wait_ge(raw_in[k], 16)
                    act.activation(hi(k), raw[:, k, :], ACT.Copy).then_inc(w_hi, 1)
                act.wait_ge(x_in[k], 16)
                act.activation(xh[:, k, :], xr[:, k % 4, :], ACT.Copy, scale=g1s[:, k:k + 1]).then_inc(x_hi, 1)
                if k >= 3:
                    act.wait_ge(x_ac, k - 2)
                act.activation(xq[:, k % 2, :] if k else rb[:], xr[:, k % 4, :], ACT.Square).then_inc(xsq, 1)
            act.wait_ge(ms_x, 1)
            act.activation(rsx[:], ssx[:], ACT.Sqrt).then_inc(sd_x, 1)
            def store_state(c):
                act.wait_ge(ag_u, 4 * (c + 1))
                act.wait_ge(st_in, 16 * CT)
                act.dma_start(nc_p[c], uc[:, (c + 1) * UW + SEQ:(c + 1) * UW + SEQ + PADC]).then_inc(st_out[c], 16)
                act.dma_start(nc_s[c], ustate(c + 1, TS, SW)).then_inc(st_out[c], 16)

            for g in range(3 * CT):
                bn = BLOCKS[g % 3][1]
                act.wait_ge(ag_ga, g + 1)
                if g >= 1:
                    act.wait_ge(ag_u, 4 * (g // 3) + (g % 3))
                act.activation(glu_s[:, 0:bn], glu_g[:, 0:bn], ACT.Sigmoid).then_inc(ag_sig, 1)
                if g % 3 == 0 and g >= 3:
                    store_state(g // 3 - 1)
            store_state(CT - 1)
            act.wait_ge(rs_x, 1)
            for m in range(3 * NT):
                j, t = divmod(m, NT)
                act.wait_ge(c_mm, m + 1)
                if j == 2:
                    act.wait_ge(c_st[m % 2], 16 * (m // 2))
                    act.activation(zo[:, m % 2, :], bank(4 + m % 4), ACT.Copy, scale=rsx[:, t:t + 1]).then_inc(c_z, 1)
                    continue
                if m >= 2:
                    act.wait_ge(c_n, 2 * (m - 1))
                act.activation(zt[:, m % 2, :], bank(4 + m % 4), ACT.Copy, scale=rsx[:, t:t + 1]).then_inc(c_z, 1)
                act.wait_ge(c_z, m + 1)
                if m >= 1:
                    act.wait_ge(c_ss, m)
                act.activation(zsq[:], zt[:, m % 2, :], ACT.Square).then_inc(c_sq, 1)
                act.wait_ge(c_ss, m + 1)
                act.activation(rsh[:, m % 2, :], ssh[:, m % 2, :], ACT.Sqrt).then_inc(c_rt, 1)
            def copy_quad(p, q, dst, src):
                act.wait_ge(d_tr, quads(p, q + 1))
                act.activation(dst, src, ACT.Copy).then_inc(d_ev, 1)

            def copy_qk(p, q0):
                for q in range(4):
                    dst = (qt, kt_)[q // 2]
                    copy_quad(p, q0 + q, dst[:, (q % 2) * 512:(q % 2 + 1) * 512], bank(4 + q % 2))
                for q in (4, 5):
                    dst = (qt, kt_)[q - 4]
                    copy_quad(p, q0 + q, dst[:, SEQ:TOK], bank(4 + q % 2, NS))

            def exps(p, u):
                n = UT[u] * P if UNITS[u][0] == "p" else SK
                r = slice(u % 3, u % 3 + 1)
                act.wait_ge(d_mx, p * NU + (u + 1))
                act.activation(tb[:, u % 3, 0:n], tb[:, u % 3, 0:n], ACT.Exp, bias=nmx[:, r],
                               accum_out=den[:, r]).then_inc(d_ex, 1)

            def copy_probs(p, u, last_pair):
                v, q = V_OF[u], quad_of(u, last_pair)
                kind, h, _ = UNITS[u]
                buf = 2 * (v % 2) + (h if kind == "p" else 0)
                act.wait_ge(d_pv, count(NV, p, v - 1))
                for c0 in range(0, UT[u], 4):
                    cn = min(4, UT[u] - c0)
                    qq = q + c0 // 4
                    b = 4 + qq % 2
                    if kind == "s" and c0 == 4:
                        act.wait_ge(d_tr, quads(p, qq + 1))
                        act.activation(pt[:, buf, 512:CK], bank(b, CK - 512), ACT.Copy)
                        act.activation(pt[0:TS, buf, CK:CK + P], bank(b, P, CK - 512)[0:TS, :],
                                       ACT.Copy).then_inc(d_ev, 1)
                    else:
                        copy_quad(p, qq, pt[:, buf, c0 * P:(c0 + cn) * P], bank(b, cn * P))

            def pair(p, last_pair):
                for u in range(NU):
                    if u == QK_AT and not last_pair:
                        act.wait_ge(d_s, count(NU, p, NU))
                        copy_qk(p, UQ[QK_AT])
                    copy_probs(p, u, last_pair)
                    if u + 2 < NU:
                        exps(p, u + 2)
                    elif not last_pair:
                        exps(p + 1, u + 2 - NU)

            copy_qk(0, -QK_Q)
            exps(0, 0)
            exps(0, 1)
            with act.Fori(0, NPAIR - 1) as p:
                pair(p, False)
            pair(NPAIR - 1, True)
            for b, (b0, w) in enumerate(LNB):
                for c in range(CT):
                    act.wait_ge(n_xc, CT * b + c + 1)
                    if b >= 2:
                        act.wait_ge(n_vm, b - 1)
                    o = sq[:, b % 2, c, 0:w]
                    if b == 2:
                        o = o.rearrange("p (b t) -> p b t", t=TS)
                    act.activation(o, ln_cols(b, c), ACT.Square).then_inc(n_sq, 1)
            for b, (b0, w) in enumerate(LNB):
                act.wait_ge(n_rs, b + 1)
                act.activation(rstd_c[:, b0:b0 + w], rstd_c[:, b0:b0 + w], ACT.Sqrt).then_inc(n_sd, 1)
            for s in range(3 * CT):
                b, c = divmod(s, CT)
                b0, w = LNB[b]
                v = ln_cols(b, c)
                act.wait_ge(n_nm, s + 1)
                act.activation(v, v, ACT.Silu, scale=lgs[:, c:c + 1], bias=lbs[:, c:c + 1]).then_inc(n_si, 1)
                act.wait_ge(n_si, s + 1)
                m_ = mh[:, CT + c, b0:b0 + w]
                if b == 2:
                    m_ = m_.rearrange("p (b t) -> p b t", t=TS)
                act.activation(m_, v, ACT.Copy).then_inc(n_hi, 1)
            def root(b):
                b0, bn = BLOCKS[b]
                act.wait_ge(e_ms, b + 1)
                act.activation(rstd_c[:, b0:b0 + bn], rstd_c[:, b0:b0 + bn], ACT.Sqrt).then_inc(e_sd, 1)

            def hi_of(s):
                b, k = divmod(s, KT)
                b0, bn = BLOCKS[b]
                act.wait_ge(e_n, s + 1)
                act.activation(mh[:, k, b0:b0 + bn], yn[:, s % 3, 0:bn], ACT.Copy, scale=g2s[:, k:k + 1]).then_inc(
                    e_hi, 1)

            act.wait_ge(n_lo, 3 * CT)
            for g in range(3):
                b0, bn = BLOCKS[g]
                for oc in range(KT):
                    act.wait_ge(e_y, NG + KT * g + oc + 1)
                    if g >= 1:
                        act.wait_ge(e_ss, g)
                    act.activation(ysq[:, oc, 0:bn], y[:, oc, b0:b0 + bn], ACT.Square).then_inc(e_sq, 1)
                    if g >= 1 and oc == SUM_AT:
                        root(g - 1)
                    if g >= 1 and oc >= KT // 2:
                        hi_of(KT * (g - 1) + 2 * (oc - KT // 2))
                        hi_of(KT * (g - 1) + 2 * (oc - KT // 2) + 1)
            for b in range(CP_BEFORE):
                act.dma_start(nk_s[5 + b, 0:LB, :], cache_k[5 + b]).then_inc(s_cp, 16)
                act.dma_start(nv_s[5 + b, 0:LB, :], cache_v[5 + b]).then_inc(s_cp, 16)

            def silu(k6, cslot, f, b, i=None):
                base = 0 if i is None else i * 12
                b0, bn = BLOCKS[b]
                act.wait_ge(gu_mm, base + (k6 + 1))
                if k6 >= 2:
                    act.wait_ge(gu_pr, base + (k6 - 1))
                act.activation(sg[:, k6 % 2, 0:bn], bank(2 * (k6 % 2), bn), ACT.Silu).then_inc(gu_si, 1)
                act.wait_ge(gu_pr, base + (k6 + 1))
                if f == 0 and b == 0 and i is not None:
                    act.wait_ge(dn_mm, i * (2 * NG) + (START + (0 if k6 == 6 else NG)))
                act.activation(ah[:, 2 * cslot + f, b0:b0 + bn], pr[:, k6 % 2, 0:bn], ACT.Copy).then_inc(gu_hi, 1)

            def silus(c6, cslot, i):
                for n, (f, b) in enumerate(GLU_ORDER):
                    silu(c6 + n, cslot, f, b, i)

            root(2)
            for n, (f, b) in enumerate(FIRST_ORDER):
                silu(n, 0, f, b)
                if n == 0:
                    for k in range(KT):
                        hi_of(KT * 2 + k)
            with act.Fori(0, (NCH - 1) // 2) as i:
                act.dma_start(nk_s[ds(i, 1), 0:LB, :], cache_k[ds(i, 1)]).then_inc(s_cp, 16)
                act.dma_start(nv_s[ds(i, 1), 0:LB, :], cache_v[ds(i, 1)]).then_inc(s_cp, 16)
                silus(6, 1, i)
                silus(12, 0, i)

        @block.vector
        def _(dve):
            for s in (d_tt, d_rc, d_ol, cv_a, cv_b, dn_y):
                dve.sem_inc(s, START)

            def taps(c, j, n, tap, skip):
                for s, off, w in ((cv_a, 0, SEQ), (cv_b, SMP, CVS)):
                    dst = uc[:, c * UW + off:c * UW + off + w]
                    src = uc[:, ds((c + 1) * UW + off + skip, w)]
                    dve.wait_ge(s, START + n)
                    if not isinstance(j, int) or j > 0:
                        dve.scalar_tensor_tensor(out=dst, in0=src, scalar=cws[:, ds(tap, 1)], in1=dst, op0=ALU.mult,
                                                 op1=ALU.add).then_inc(s, 1)
                    else:
                        dve.tensor_scalar(dst, src, cws[:, ds(tap, 1)], cbs[:, c:c + 1], ALU.mult,
                                          ALU.add).then_inc(s, 1)

            todo = [(c, j) for c in range(CT) for j in range(TAPS)][:TAPS * (CT - 1) + TAPS_PRE]

            def conv(k):
                for _ in range(k):
                    if todo:
                        c, j = todo.pop(0)
                        if j == 0 and c == 0:
                            dve.wait_ge(c_in, 16 * 8)
                            dve.wait_ge(st_in, 16 * CT)
                        if j == 0 and c >= 1:
                            dve.wait_ge(st_out[c - 1], 32)
                        taps(c, j, TAPS * c + j, TAPS * c + j, j)

            for k in range(KT):
                if k < 2:
                    dve.wait_ge(w_hi, k + 1)
                    dve.tensor_tensor(lo(k), raw[:, k, :], hi(k).bitcast(F32), ALU.subtract).then_inc(w_lo, 1)
                dve.wait_ge(x_hi, k + 1)
                dve.scalar_tensor_tensor(out=xl[:, k, :], in0=xr[:, k % 4, :], scalar=g1s[:, k:k + 1],
                                         in1=xh[:, k, :].bitcast(F32), op0=ALU.mult, op1=ALU.subtract).then_inc(x_lo, 1)
                if k >= 1:
                    dve.wait_ge(xsq, k + 1)
                    if k >= 2:
                        dve.wait_ge(x_ac, k - 1)
                    dve.tensor_tensor(rb[:], rb[:], xq[:, k % 2, :], ALU.add).then_inc(x_ac, 1)
            dve.wait_ge(x_ss, 1)
            dve.tensor_scalar(ssx[:], bank(6, NT), DC / D, RMS_EPS, ALU.mult, ALU.add).then_inc(ms_x, 1)
            dve.wait_ge(sd_x, 1)
            dve.reciprocal(rsx[:], rsx[:]).then_inc(rs_x, 1)
            dve.wait_ge(rs_x, 1)
            dve.wait_ge(mem_s, 1)
            for t in range(NT):
                if t >= 2:
                    dve.wait_ge(rbt_t, t - 1)
                dve.tensor_scalar(rbt[:, t % 2, :], ones_c[:], float(DC), rsx[:, t:t + 1], ALU.mult,
                                  ALU.mult).then_inc(rbt_s, 1)
            dve.wait_ge(rbt_t, NT - 1)
            for q in range(2):
                dve.tensor_copy(rb[:, q * 512:(q + 1) * 512], bank(6 + q)).then_inc(rb_s, 1)
            dve.wait_ge(rbt_t, NT)
            dve.tensor_copy(rb[:, SEQ:TOK], bank(6, NS, P - NS)).then_inc(rb_s, 1)
            dve.wait_ge(c_in, 16 * 8)
            dve.tensor_scalar(qkgs[:, 0, :], qkgs[:, 0, :], DH ** -0.5, None, ALU.mult).then_inc(rb_s, 1)
            dve.wait_ge(rb_s, 4)
            nu = 0
            for g in range(3 * CT):
                c, (b0, bn) = g // 3, BLOCKS[g % 3]
                r = rb[:, b0:b0 + bn]
                dve.wait_ge(ag_mm, g + 1)
                if g >= 1:
                    dve.wait_ge(ag_sig, g)
                dve.tensor_tensor(glu_g[:, 0:bn], bank(2 * (g % 3) + 1, bn), r, ALU.mult).then_inc(ag_ga, 1)
                if g >= 1:
                    dve.wait_ge(ag_u, nu)
                dve.tensor_tensor(glu_a[:, 0:bn], bank(2 * (g % 3), bn), r, ALU.mult).then_inc(ag_aa, 1)
                dve.wait_ge(ag_sig, g + 1)
                dve.wait_ge(ag_aa, g + 1)
                if g == 0:
                    dve.wait_ge(mem_s, 1 + CT)
                n = min(bn, SEQ - b0)
                u0 = (c + 1) * UW + PADC + b0
                dve.tensor_tensor(uc[:, u0:u0 + n], glu_a[:, 0:n], glu_s[:, 0:n], ALU.mult).then_inc(ag_u, 1)
                nu += 1
                if n < bn:
                    def by_sample(a):
                        return a[:, n:bn].rearrange("p (b t) -> p b t", t=TS)
                    dve.tensor_tensor(ustate(c + 1, PADC, SW), by_sample(glu_a), by_sample(glu_s),
                                      ALU.mult).then_inc(ag_u, 1)
                    nu += 1
                if g >= 3:
                    conv(3)
            for m in range(3 * NT):
                j = m // NT
                if j == 2:
                    dve.wait_ge(c_z, m + 1)
                    conv(2)
                    continue
                dve.wait_ge(c_sq, m + 1)
                dve.tensor_reduce(ssh[:, m % 2, :], zsq[:].rearrange("p (h d) -> p h d", d=DH), AX.X,
                                  ALU.add).then_inc(c_n, 1)
                dve.wait_ge(c_n, 2 * m + 1)
                dve.tensor_scalar(ssh[:, m % 2, :], ssh[:, m % 2, :], 1.0 / DH, RMS_EPS, ALU.mult, ALU.add).then_inc(
                    c_ss, 1)
                dve.wait_ge(c_rt, m + 1)
                dve.reciprocal(rsh[:, m % 2, :], rsh[:, m % 2, :]).then_inc(c_rs, 1)
                dve.wait_ge(c_rs, m + 1)
                z3 = zt[:, m % 2, :].rearrange("p (h d) -> p h d", d=DH)
                if m >= 2:
                    dve.wait_ge(c_st[m % 2], 16 * (m // 2))
                dve.tensor_tensor(zo[:, m % 2, :].rearrange("p (h d) -> p h d", d=DH), z3,
                                  rsh[:, m % 2, :].unsqueeze(2).broadcast_to([P, H, DH]), ALU.mult).then_inc(c_n, 1)
                conv(2)
            conv(len(todo) - PAIR0_TAPS)
            dve.wait_ge(c_mm, 3 * NT)
            dve.memset(qb[:], 0.0).then_inc(mem_s, 1)
            dve.wait_ge(mem_s, 2 + CT)
            dve.wait_ge(d_msk, 32)

            def mask_max(p, u):
                kind, h, i = UNITS[u]
                n = UT[u] * P if kind == "p" else SK
                mask = mkp[:, D - n:D] if kind == "p" else mks[:]
                r = slice(u % 3, u % 3 + 1)
                dve.wait_ge(d_s, count(NU, p, u + 1))
                end = UQ[u - 2] if u >= 3 else quad_of(u + NU - 3, False) + (UT[u + NU - 3] + 3) // 4 - NQ
                dve.wait_ge(d_tr, quads(p, end))
                dve.sem_inc(own_wait, 1)
                s = 2 * (u % 2) * 512
                dve.tensor_tensor_reduce(out=tb[:, u % 3, 0:n], in0=ps[:, s:s + n], in1=mask, scale=1.0,
                                         scalar=-3.0e38, op0=ALU.add, op1=ALU.max,
                                         accum_out=mxs[:, r]).then_inc(d_tt, 1)
                dve.wait_ge(d_tt, count(NU, p, u + 1))
                dve.tensor_scalar(nmx[:, r], mxs[:, r], -1.0, None, ALU.mult).then_inc(d_mx, 1)

            def norm(p, u):
                n = UT[u] * P if UNITS[u][0] == "p" else SK
                r = slice(u % 3, u % 3 + 1)
                dve.wait_ge(d_ex, count(NU, p, u + 1))
                dve.reciprocal(rden[:, r], den[:, r]).then_inc(d_rc, 1)
                dve.wait_ge(d_rc, count(NU, p, u + 1))
                dve.tensor_scalar(tb[:, u % 3, 0:n], tb[:, u % 3, 0:n], rden[:, r], None, ALU.mult).then_inc(d_sc, 1)

            def outputs(p, og):
                vs = OGROUPS[og]
                kind, h, i = UNITS[VSTEPS[vs[0]][0]]
                dve.wait_ge(d_pv, count(NV, p, vs[-1] + 1))
                if kind == "p":
                    parts = [(slice(0, P), i * P, 512, bank(6 + og % 2))]
                else:
                    dve.wait_ge(d_ot, p * 2 + (h + 1))
                    o = bank(6, P, P).rearrange("p (b c) -> p b c", c=32)
                    parts = [(slice(DH * hh, DH * hh + DH), SEQ + 4 * TS * h, 4 * TS,
                              o[DH * hh:DH * hh + DH, :, TS * hh:TS * hh + TS]) for hh in range(2)]

                def part(t_, r, c0, w):
                    v = t_[r, ds(p, 1), c0:c0 + w].rearrange("p a c -> p (a c)")
                    return v if kind == "p" else v.rearrange("p (b c) -> p b c", c=TS)

                for r, c0, w, o in parts:
                    last = dve.tensor_copy(part(mh, r, c0, w), o)
                last.then_inc(d_oh, 1)
                dve.wait_ge(d_oh, p * NOG + (og + 1))
                for r, c0, w, o in parts:
                    last = dve.tensor_tensor(part(ml, r, c0, w), o, part(mh, r, c0, w).bitcast(F32), ALU.subtract)
                last.then_inc(d_ol, 1)

            def copy_samples(p, h):
                dve.wait_ge(d_pv, count(NV, p, V_OF[S_UNITS[h]] + 1))
                dve.tensor_copy(so[:], bank(6, P)).then_inc(d_oc, 1)

            def fill_qb(p, q0):
                dve.wait_ge(d_ev, quads(p, q0 + QK_Q))
                for h in range(2):
                    rows = slice(DH * h, DH * h + DH)
                    last = dve.tensor_copy(qb[rows, :, TS * h:TS * (h + 1)],
                                           qt[rows, SEQ:TOK].rearrange("p (b t) -> p b t", t=TS))
                last.then_inc(d_qb, 1)

            def convolve(p, u, first_pair):
                if first_pair:
                    conv(1 if u >= NU - PAIR0_TAPS else 0)
                elif u in TAP_UNITS:
                    j0 = TAPS_PRE - TAPS_STEP + TAP_UNITS.index(u)
                    n = p * TAPS_STEP + (TAPS * (CT - 1) + j0)
                    taps(CT - 1, p, n, n, p * TAPS_STEP + j0)

            def pair(p, first_pair, last_pair):
                for u in range(NU):
                    if u + 1 < NU:
                        norm(p, u + 1)
                    elif not last_pair:
                        norm(p + 1, 0)
                    if u == QK_AT:
                        convolve(p, u, first_pair)
                        if not last_pair:
                            fill_qb(p, UQ[QK_AT])
                    if u + 2 < NU:
                        mask_max(p, u + 2)
                    elif not last_pair:
                        mask_max(p + 1, u + 2 - NU)
                    if u == 0 and not first_pair:
                        outputs(p - 1, NOG - 1)
                    for h in range(2):
                        if u == S_UNITS[h] + 2:
                            copy_samples(p, h)
                    for og in range(NOG - 1):
                        if VSTEPS[OGROUPS[og][-1]][-1] + (4 if UNITS[VSTEPS[OGROUPS[og][0]][0]][0] == "s" else 2) == u:
                            outputs(p, og)
                    if u != QK_AT:
                        convolve(p, u, first_pair)
                if last_pair:
                    outputs(p, NOG - 1)

            fill_qb(0, -QK_Q)
            mask_max(0, 0)
            mask_max(0, 1)
            norm(0, 0)
            pair(0, True, False)
            with dve.Fori(1, NPAIR - 1) as p:
                pair(p, False, False)
            pair(NPAIR - 1, False, True)
            def variance(b):
                b0, w = LNB[b]
                if b == 0:
                    dve.wait_ge(st_out[CT - 1], 32)
                dve.wait_ge(n_vm, b + 1)
                dve.tensor_scalar(rstd_c[:, b0:b0 + w], ln_mean(b), LN_EPS, None, ALU.add).then_inc(n_rs, 1)

            def rstd(b):
                b0, w = LNB[b]
                dve.wait_ge(n_sd, b + 1)
                dve.reciprocal(rstd_c[:, b0:b0 + w], rstd_c[:, b0:b0 + w]).then_inc(n_rs, 1)
                dve.wait_ge(n_rs, 3 + b + 1)

            def by_block(b, a):
                return a.rearrange("p (b t) -> p b t", t=TS) if b == 2 else a

            def normed(s):
                b, c = divmod(s, CT)
                b0, w = LNB[b]
                v = ln_cols(b, c)
                dve.tensor_tensor(v, v, by_block(b, rstd_c[:, b0:b0 + w]), ALU.mult).then_inc(n_nm, 1)
                if s >= 1:
                    cut_swish(s - 1)

            def cut_swish(s):
                b, c = divmod(s, CT)
                b0, w = LNB[b]
                dve.wait_ge(n_hi, s + 1)
                dve.tensor_tensor(by_block(b, ml[:, CT + c, b0:b0 + w]), ln_cols(b, c),
                                  by_block(b, mh[:, CT + c, b0:b0 + w].bitcast(F32)), ALU.subtract).then_inc(n_lo, 1)

            def add_y(m, oc, g):
                b0, bn = BLOCKS[g]
                dve.wait_ge(e_mm, m + 1)
                dve.tensor_tensor(y[:, oc, b0:b0 + bn], bank(4 + m % 4, bn), y[:, oc, b0:b0 + bn],
                                  ALU.add).then_inc(e_y, 1)

            for b in range(3):
                dve.wait_ge(n_mm, b + 1)
                for c in range(CT):
                    dve.tensor_tensor(ln_cols(b, c), ln_cols(b, c), by_block(b, ln_mean(b)),
                                      ALU.subtract).then_inc(n_xc, 1)
            steps = [(variance, b) for b in range(3)]
            for b in range(3):
                steps += [(rstd, b)] + [(normed, CT * b + c) for c in range(CT)]
            dve.wait_ge(y_in[0], 16)
            for n, oc in enumerate(E1_ORDER):
                if oc == 0:
                    dve.wait_ge(y_in[1], 16)
                for g in range(3):
                    add_y(3 * n + g, oc, g)
                    if 3 * n + g >= VAR0 and steps:
                        f, a = steps.pop(0)
                        f(a)
            assert not steps
            cut_swish(3 * CT - 1)
            def mean_square(b):
                b0, bn = BLOCKS[b]
                dve.wait_ge(e_ss, b + 1)
                dve.tensor_scalar(rstd_c[:, b0:b0 + bn], y_meansq(b), DC / D, RMS_EPS, ALU.mult, ALU.add).then_inc(
                    e_ms, 1)

            def reciprocal(b):
                b0, bn = BLOCKS[b]
                dve.wait_ge(e_sd, b + 1)
                dve.reciprocal(rstd_c[:, b0:b0 + bn], rstd_c[:, b0:b0 + bn]).then_inc(e_rs, 1)
                dve.wait_ge(e_rs, b + 1)

            def lo_of(s):
                b, k = divmod(s, KT)
                b0, bn = BLOCKS[b]
                dve.wait_ge(e_hi, s + 1)
                dve.scalar_tensor_tensor(out=ml[:, k, b0:b0 + bn], in0=yn[:, s % 3, 0:bn], scalar=g2s[:, k:k + 1],
                                         in1=mh[:, k, b0:b0 + bn].bitcast(F32), op0=ALU.mult,
                                         op1=ALU.subtract).then_inc(e_lo, 1)

            def normalise(s):
                b, k = divmod(s, KT)
                b0, bn = BLOCKS[b]
                if s >= 3:
                    dve.wait_ge(e_lo, s - 2)
                dve.tensor_tensor(yn[:, s % 3, 0:bn], y[:, k, b0:b0 + bn], rstd_c[:, b0:b0 + bn],
                                  ALU.mult).then_inc(e_n, 1)
                if k >= 1:
                    lo_of(s - 1)
                if k == KT - 1:
                    lo_of(s)

            for g in range(3):
                for oc in range(KT):
                    add_y(NG + KT * g + oc, oc, g)
                    if g >= 1 and oc == SUM_AT:
                        mean_square(g - 1)
                    if g >= 1 and oc == SUM_AT + 1:
                        reciprocal(g - 1)
                    if g >= 1 and oc >= KT // 2:
                        normalise(KT * (g - 1) + 2 * (oc - KT // 2))
                        normalise(KT * (g - 1) + 2 * (oc - KT // 2) + 1)
            def glu(k6, cslot, f, b, i=None):
                base = 0 if i is None else i * 12
                b0, bn = BLOCKS[b]
                dve.wait_ge(gu_si, base + (k6 + 1))
                if k6 >= 2:
                    dve.wait_ge(gu_lo, base + (k6 - 1))
                dve.tensor_tensor(pr[:, k6 % 2, 0:bn], bank(2 * (k6 % 2) + 1, bn), sg[:, k6 % 2, 0:bn],
                                  ALU.mult).then_inc(gu_pr, 1)
                dve.wait_ge(gu_hi, base + (k6 + 1))
                dve.tensor_tensor(al[:, 2 * cslot + f, b0:b0 + bn], pr[:, k6 % 2, 0:bn],
                                  ah[:, 2 * cslot + f, b0:b0 + bn].bitcast(F32), ALU.subtract).then_inc(gu_lo, 1)

            def glus(c6, cslot, i):
                for n, (f, b) in enumerate(GLU_ORDER):
                    glu(c6 + n, cslot, f, b, i)

            def adds(half, i=None):
                base_m = START if i is None else i * (2 * NG) + START
                const_m = NG * half if i is not None else NG * (NCH - 1)
                dve.wait_ge(dn_y, base_m + const_m)
                for m in range(NG):
                    oc, (b0, bn) = m // 3, BLOCKS[m % 3]
                    dve.wait_ge(dn_mm, base_m + (const_m + m + 1))
                    dve.tensor_tensor(y[:, oc, b0:b0 + bn], bank(4 + m % 4, bn), y[:, oc, b0:b0 + bn],
                                      ALU.add).then_inc(dn_y, 1)

            mean_square(2)
            reciprocal(2)
            for n, (f, b) in enumerate(FIRST_ORDER):
                glu(n, 0, f, b)
                if n == 0:
                    for k in range(KT):
                        normalise(KT * 2 + k)
            with dve.Fori(0, (NCH - 1) // 2) as i:
                glus(6, 1, i)
                adds(0, i)
                glus(12, 0, i)
                adds(1, i)
            adds(0)


def laid_out(v):
    import numpy as np

    f = {k: np.asarray(a) for k, a in v.items()}
    w_in, w_out, w_gate, w_up, w_down = (f[k][0] for k in ("w_in", "w_out", "w_gate", "w_up", "w_down"))

    def cols(w, c0):
        return w[:, c0:c0 + P].reshape(KT, P, P).transpose(1, 0, 2).reshape(P, PC)

    def two(w, j, c0):
        return w[2 * j * P:(2 * j + 2) * P, c0:c0 + 512].reshape(2, P, 512).transpose(1, 0, 2).reshape(P, PC)

    def gate_up(c):
        return [cols(w, (2 * c + t) * P) for t in range(2) for w in (w_gate, w_up)]

    def down(c):
        return [w_down[(2 * c + t) * P:(2 * c + t + 1) * P] for t in range(2)]

    stream = [cols(w_in, 3 * DA + s * DC + c * P) for c in range(CT) for s in range(2)]
    stream += [two(w_in, j, b * DA) for b in range(3) for j in range(4)]
    stream += [w_out[k * P:(k + 1) * P] for k in range(KT)]
    stream += gate_up(0)
    for c in range(NCH - 1):
        stream += gate_up(c + 1) + down(c)
    stream += down(NCH - 1)

    x_all = np.concatenate([f["x_prompt"].reshape(SEQ, D), f["x_sample"].reshape(NS, D)])
    rows = np.concatenate([np.arange(512, LB), np.array([r for r in range(512) if r % 16 < TS])])
    assert rows.size == CK

    def cache(a):
        return a[0].reshape(NB_S, LB, NPAIR, P)[:, rows]

    def count(d):
        return sum(((d >= 0) & (d <= w) & (d % r == 0)).astype(np.int64) for w, r in ((128, 1), (512, 4), (2048, 16)))

    def log_count(d):
        c = count(d)
        return np.where(c > 0, np.log(np.maximum(c, 1)), -1.0e30).astype(np.float32)

    part = np.arange(P)[:, None]
    new_rows = np.concatenate([rows, np.arange(LB, LB + TS)])[None, :]
    state = f["state_conv"][0].transpose(2, 0, 1).reshape(CT, P, NB_S, PADC)

    def column(a):
        return a[0].reshape(-1, P).T

    return {
        "w_stream": np.stack(stream),
        "xT": x_all.T.reshape(KT, P, TOK),
        "kT_c": cache(f["cache_k"]).transpose(2, 0, 3, 1).reshape(NPAIR * NB_S, P, CK),
        "v_c": cache(f["cache_v"]).reshape(NB_S, CKT, P, NPAIR, P).transpose(3, 0, 2, 1, 4).reshape(
            NPAIR * NB_S, P, CKT, P),
        "cache_k": f["cache_k"].reshape(NB_S, LB, DA),
        "cache_v": f["cache_v"].reshape(NB_S, LB, DA),
        "stT": state,
        "g1": column(f["attn_norm_g"]),
        "g2": column(f["ffn_norm_g"]),
        "qkg": np.stack([np.tile(f[k], (P, 1)) for k in ("q_norm_g", "k_norm_g")], axis=1),
        "cw": f["conv_w"][0].T.reshape(CT, P, TAPS).transpose(1, 0, 2).reshape(P, CT * TAPS),
        "cb": column(f["conv_b"]),
        "lg": column(f["conv_ln_g"]),
        "lb": column(f["conv_ln_b"]),
        "ident_d": np.eye(P, dtype=np.float32),
        "mask_p": log_count(part + SEQ - P - np.arange(D)[None, :]),
        "mask_s": log_count(LB + part % TS - new_rows),
    }


OUTPUTS = [("yT", (KT, P, TOK)), ("nk_p", (SEQ, DA)), ("nv_p", (SEQ, DA)),
           ("nc_p", (CT, P, PADC)), ("nk_s", (NB_S, LB + TS, DA)), ("nv_s", (NB_S, LB + TS, DA)),
           ("nc_s", (CT, P, NB_S, PADC))]


def kernel(**inputs):
    import numpy as np
    import concourse.bacc as bacc
    from concourse.bass_utils import run_bass_kernel_spmd as run

    nc = bacc.Bacc("TRN2", target_bir_lowering=False, num_devices=1)
    arrays, args = {}, []
    for name, a in laid_out(inputs).items():
        a = np.ascontiguousarray(a)
        arrays[f"in_{name}"] = a
        args.append(nc.dram_tensor(f"in_{name}", a.shape, mybir.dt.from_np(a.dtype), kind="ExternalInput").ap())
    for name, shape in OUTPUTS:
        args.append(nc.dram_tensor(f"out_{name}", shape, F32, kind="ExternalOutput").ap())
    hymba_layer(nc, *args)
    r = run(nc, [arrays], core_ids=[0]).results[0]
    yT, nk_p, nv_p, nc_p, nk_s, nv_s, nc_s = (r[f"out_{name}"] for name, _ in OUTPUTS)
    y = yT.reshape(D, TOK).T
    return (y[:SEQ].reshape(1, SEQ, D), y[SEQ:].reshape(NB_S, TS, D),
            nk_p.reshape(1, 1, SEQ, H, DH), nv_p.reshape(1, 1, SEQ, H, DH),
            nc_p.reshape(DC, PADC).T.reshape(1, 1, PADC, DC),
            nk_s.reshape(1, NB_S, LB + TS, H, DH), nv_s.reshape(1, NB_S, LB + TS, H, DH),
            nc_s.reshape(DC, NB_S, PADC).transpose(1, 2, 0).reshape(1, NB_S, PADC, DC))
```
